# Optimizing a Trainium2 kernel written in Bass

```python
import jax
import jax.numpy as jnp
from jax import lax
import numpy as np
import math

D_MODEL = 1024
BATCH = 1
SEQ = 256
DEPTH = 2

HEAD_DIM = 64
MLA_HEADS = 6
MLA_NOPE = 64
MLA_ROPE = 32
MLA_V = 64
MLA_Q_RANK = 256
MLA_KV_RANK = 128
ROPE_THETA = 10000.0
MLA_Q_BLOCK = 128
MOBA_HEADS = 6
MOBA_BLOCK = 256
MOBA_TOPK = 3
MOBA_Q_CHUNK = 32
DIL_PATTERNS = ((128, 1), (512, 4), (2048, 16))
DIL_GROUP_HEADS = 4
DIL_HEADS = DIL_GROUP_HEADS * len(DIL_PATTERNS)
N_ALIBI = DIL_HEADS + MOBA_HEADS
N_BRANCHES = 3
D_FF = 2816
NORM_EPS = 1e-6
NEG_INF = -1e30
MLA_IN = MLA_Q_RANK + MLA_KV_RANK + MLA_ROPE
MOBA_IN = 3 * MOBA_HEADS * HEAD_DIM
DIL_IN = 3 * DIL_HEADS * HEAD_DIM
GATE_IN = N_BRANCHES * D_MODEL
IN_COLS = MLA_IN + MOBA_IN + DIL_IN + GATE_IN
MLA_OUT = MLA_HEADS * MLA_V
MOBA_OUT = MOBA_HEADS * HEAD_DIM
DIL_OUT = DIL_GROUP_HEADS * HEAD_DIM


def rms_norm(x, gain):
    xf = x.astype(jnp.float32)
    y = xf * lax.rsqrt(jnp.mean(xf * xf, axis=-1, keepdims=True) + NORM_EPS)
    return (y * gain.astype(jnp.float32)).astype(x.dtype)

def swiglu(h, w_gate, w_up, w_down):
    a = jnp.einsum('bsd,df->bsf', h, w_gate)
    u = jnp.einsum('bsd,df->bsf', h, w_up)
    return jnp.einsum('bsf,fd->bsd', jax.nn.silu(a) * u, w_down)

def alibi_slopes():
    return 2.0 ** (-8.0 * jnp.arange(1, N_ALIBI + 1, dtype=jnp.float32) / N_ALIBI)

def rope_tables(seq):
    pos = jnp.arange(seq, dtype=jnp.float32)
    inv = ROPE_THETA ** (-jnp.arange(0, MLA_ROPE, 2, dtype=jnp.float32) / MLA_ROPE)
    ang = pos[:, None] * inv[None, :]
    return jnp.cos(ang), jnp.sin(ang)

def apply_rope(t, cos, sin):
    cos = cos.astype(t.dtype)
    sin = sin.astype(t.dtype)
    t1, t2 = jnp.split(t, 2, axis=-1)
    return jnp.concatenate([t1 * cos - t2 * sin, t1 * sin + t2 * cos], axis=-1)

def mla_attention(h_cq, h_ckv, h_krope, q_norm, w_uq, kv_norm, w_ukv):
    B, S, _ = h_cq.shape
    cos, sin = rope_tables(S)
    c_q = rms_norm(h_cq, q_norm)
    q = jnp.einsum('bsr,rk->bsk', c_q, w_uq).reshape(B, S, MLA_HEADS, MLA_NOPE + MLA_ROPE)
    q = jnp.concatenate([q[..., :MLA_NOPE], apply_rope(q[..., MLA_NOPE:], cos[:, None], sin[:, None])], axis=-1)
    c_kv = rms_norm(h_ckv, kv_norm)
    kv = jnp.einsum('bsr,rk->bsk', c_kv, w_ukv).reshape(B, S, MLA_HEADS, MLA_NOPE + MLA_V)
    k_rope = apply_rope(h_krope, cos, sin)
    k = jnp.concatenate([kv[..., :MLA_NOPE], jnp.broadcast_to(k_rope[:, :, None, :], (B, S, MLA_HEADS, MLA_ROPE))], axis=-1)
    v = kv[..., MLA_NOPE:]
    q, k, v = (t.transpose(0, 2, 1, 3) for t in (q, k, v))
    scale = (MLA_NOPE + MLA_ROPE) ** -0.5
    nb = S // MLA_Q_BLOCK
    q_blocks = q.reshape(B, MLA_HEADS, nb, MLA_Q_BLOCK, MLA_NOPE + MLA_ROPE).transpose(2, 0, 1, 3, 4)
    kpos = jnp.arange(S)

    def block(args):
        qi, i = args
        s = jnp.einsum('bhqd,bhkd->bhqk', qi, k).astype(jnp.float32) * scale
        qpos = i * MLA_Q_BLOCK + jnp.arange(MLA_Q_BLOCK)
        s = jnp.where(kpos[None, :] <= qpos[:, None], s, NEG_INF)
        p = jax.nn.softmax(s, axis=-1).astype(v.dtype)
        return jnp.einsum('bhqk,bhkd->bhqd', p, v)

    o = lax.map(block, (q_blocks, jnp.arange(nb)))
    return o.transpose(1, 0, 3, 2, 4).reshape(B, S, MLA_OUT)

def moba_attention(q, k, v, slopes):
    B, H, S, D = q.shape
    nb = -(-S // MOBA_BLOCK)
    sp = nb * MOBA_BLOCK
    pad = ((0, 0), (0, 0), (0, sp - S), (0, 0))
    qp, kp, vp = (jnp.pad(t, pad) for t in (q, k, v))
    kb = kp.reshape(B, H, nb, MOBA_BLOCK, D)
    vb = vp.reshape(B, H, nb, MOBA_BLOCK, D)
    k_mean = jnp.mean(kb, axis=3)
    k_sel_n = min(MOBA_TOPK, nb)
    scale = D ** -0.5
    bi = jnp.arange(B)[:, None, None, None]
    hi = jnp.arange(H)[None, :, None, None]
    blk_ids = jnp.arange(nb)
    offs = jnp.arange(MOBA_BLOCK)
    slope5 = slopes[None, :, None, None, None]

    def chunk(c):
        start = c * MOBA_Q_CHUNK
        qc = lax.dynamic_slice_in_dim(qp, start, MOBA_Q_CHUNK, axis=2)
        b_own = start // MOBA_BLOCK
        tpos = start + jnp.arange(MOBA_Q_CHUNK)
        gate = jnp.einsum('bhqd,bhnd->bhqn', qc, k_mean).astype(jnp.float32)
        gate = jnp.where(blk_ids < b_own, gate, NEG_INF)
        _, idx = lax.top_k(gate, k_sel_n)
        sel_ok = idx < b_own
        k_sel = kb[bi, hi, idx]
        v_sel = vb[bi, hi, idx]
        s_sel = jnp.einsum('bhqd,bhqnpd->bhqnp', qc, k_sel).astype(jnp.float32) * scale
        kpos_sel = idx[..., None] * MOBA_BLOCK + offs
        dist_sel = (tpos[None, None, :, None, None] - kpos_sel).astype(jnp.float32)
        s_sel = jnp.where(sel_ok[..., None], s_sel - slope5 * dist_sel, NEG_INF)
        k_own = lax.dynamic_index_in_dim(kb, b_own, axis=2, keepdims=False)
        v_own = lax.dynamic_index_in_dim(vb, b_own, axis=2, keepdims=False)
        kpos_own = b_own * MOBA_BLOCK + offs
        dist_own = (tpos[:, None] - kpos_own[None, :]).astype(jnp.float32)
        s_own = jnp.einsum('bhqd,bhpd->bhqp', qc, k_own).astype(jnp.float32) * scale
        s_own = jnp.where(dist_own >= 0, s_own - slopes[None, :, None, None] * dist_own, NEG_INF)
        n_sel = k_sel_n * MOBA_BLOCK
        s = jnp.concatenate([s_sel.reshape(B, H, MOBA_Q_CHUNK, n_sel), s_own], axis=-1)
        p = jax.nn.softmax(s, axis=-1).astype(v.dtype)
        p_sel = p[..., :n_sel].reshape(B, H, MOBA_Q_CHUNK, k_sel_n, MOBA_BLOCK)
        p_own = p[..., n_sel:]
        return (jnp.einsum('bhqnp,bhqnpd->bhqd', p_sel, v_sel)
                + jnp.einsum('bhqp,bhpd->bhqd', p_own, v_own))

    o = lax.map(chunk, jnp.arange(sp // MOBA_Q_CHUNK))
    return o.transpose(1, 0, 3, 2, 4).reshape(B, sp, H * D)[:, :S]

def dilated_group_attention(q, k, v, window, dilation, slopes):
    B, H, S, D = q.shape
    L = window // dilation
    span = dilation * L
    P = -(-S // span) * span
    M = P // dilation
    nbk = M // L

    def to_blocks(t):
        t = jnp.pad(t, ((0, 0), (0, 0), (0, P - S), (0, 0)))
        return t.reshape(B, H, M, dilation, D).transpose(0, 1, 3, 2, 4).reshape(B, H, dilation, nbk, L, D)

    def window_keys(t):
        prev = jnp.pad(t[:, :, :, :-1], ((0, 0), (0, 0), (0, 0), (1, 0), (0, 0), (0, 0)))
        return jnp.concatenate([prev, t], axis=4)

    qb = to_blocks(q)
    kw = window_keys(to_blocks(k))
    vw = window_keys(to_blocks(v))
    s = jnp.einsum('bhrnqd,bhrnkd->bhrnqk', qb, kw).astype(jnp.float32) * (D ** -0.5)
    steps = L + jnp.arange(L)[:, None] - jnp.arange(2 * L)[None, :]
    band = (steps >= 0) & (steps <= L)
    before_start = (jnp.arange(nbk)[:, None, None] == 0) & (jnp.arange(2 * L) < L)[None, None, :]
    valid = band[None] & ~before_start
    dist = (steps * dilation).astype(jnp.float32)
    s = jnp.where(valid, s - slopes[None, :, None, None, None, None] * dist, NEG_INF)
    m = jnp.max(s, axis=-1, keepdims=True)
    e = jnp.exp(s - m)
    den = jnp.sum(e, axis=-1)
    o = jnp.einsum('bhrnqk,bhrnkd->bhrnqd', (e / den[..., None]).astype(v.dtype), vw)
    lse = m[..., 0] + jnp.log(den)
    o = o.reshape(B, H, dilation, M, D).transpose(0, 1, 3, 2, 4).reshape(B, H, P, D)[:, :, :S]
    lse = lse.reshape(B, H, dilation, M).transpose(0, 1, 3, 2).reshape(B, H, P)[:, :, :S]
    return o, lse

def hybrid_mixer(h, w_in, q_norm, w_uq, kv_norm, w_ukv, w_br_mla, w_br_moba, w_br_dil, w_out):
    B, S, _ = h.shape
    proj = jnp.einsum('bsd,dk->bsk', h, w_in)
    i0 = MLA_Q_RANK
    i1 = i0 + MLA_KV_RANK
    i2 = i1 + MLA_ROPE
    i3 = i2 + MOBA_IN
    i4 = i3 + DIL_IN
    h_cq, h_ckv, h_kr, h_moba, h_dil, h_gate = jnp.split(proj, [i0, i1, i2, i3, i4], axis=-1)
    slopes = alibi_slopes()
    a = mla_attention(h_cq, h_ckv, h_kr, q_norm, w_uq, kv_norm, w_ukv)
    mqkv = h_moba.reshape(B, S, 3, MOBA_HEADS, HEAD_DIM).transpose(2, 0, 3, 1, 4)
    b = moba_attention(mqkv[0], mqkv[1], mqkv[2], slopes[DIL_HEADS:])
    dqkv = h_dil.reshape(B, S, 3, DIL_HEADS, HEAD_DIM).transpose(2, 0, 3, 1, 4)
    outs, lses = [], []
    for g, (window, dilation) in enumerate(DIL_PATTERNS):
        hs = slice(g * DIL_GROUP_HEADS, (g + 1) * DIL_GROUP_HEADS)
        o_g, l_g = dilated_group_attention(dqkv[0][:, hs], dqkv[1][:, hs], dqkv[2][:, hs], window, dilation, slopes[hs])
        outs.append(o_g)
        lses.append(l_g)
    alpha = jax.nn.softmax(jnp.stack(lses), axis=0)
    c = jnp.einsum('gbhs,gbhsd->bhsd', alpha.astype(outs[0].dtype), jnp.stack(outs))
    c = c.transpose(0, 2, 1, 3).reshape(B, S, DIL_OUT)
    gates = jax.nn.sigmoid(h_gate).reshape(B, S, N_BRANCHES, D_MODEL)
    merged = (gates[:, :, 0] * jnp.einsum('bsk,kd->bsd', a, w_br_mla)
              + gates[:, :, 1] * jnp.einsum('bsk,kd->bsd', b, w_br_moba)
              + gates[:, :, 2] * jnp.einsum('bsk,kd->bsd', c, w_br_dil))
    return jnp.einsum('bsd,de->bse', merged, w_out)

def first_inputs(seed: int = 0) -> dict:
    key = jax.random.key(seed)
    ks = jax.random.split(key, 20)

    def nrm(k, shape, fan_in):
        return jax.random.normal(k, shape, jnp.float32) * (fan_in ** -0.5)

    def gain(k, shape):
        return 1.0 + 0.01 * jax.random.normal(k, shape, jnp.float32)

    return {
        'x': jax.random.normal(ks[0], (BATCH, SEQ, D_MODEL), jnp.float32),
        'ffn1_norm': gain(ks[1], (DEPTH, D_MODEL)),
        'ffn1_w_gate': nrm(ks[2], (DEPTH, D_MODEL, D_FF), D_MODEL),
        'ffn1_w_up': nrm(ks[3], (DEPTH, D_MODEL, D_FF), D_MODEL),
        'ffn1_w_down': nrm(ks[4], (DEPTH, D_FF, D_MODEL), D_FF),
        'mix_norm': gain(ks[5], (DEPTH, D_MODEL)),
        'w_in': nrm(ks[6], (DEPTH, D_MODEL, IN_COLS), D_MODEL),
        'q_norm': gain(ks[7], (DEPTH, MLA_Q_RANK)),
        'w_uq': nrm(ks[8], (DEPTH, MLA_Q_RANK, MLA_HEADS * (MLA_NOPE + MLA_ROPE)), MLA_Q_RANK),
        'kv_norm': gain(ks[9], (DEPTH, MLA_KV_RANK)),
        'w_ukv': nrm(ks[10], (DEPTH, MLA_KV_RANK, MLA_HEADS * (MLA_NOPE + MLA_V)), MLA_KV_RANK),
        'w_br_mla': nrm(ks[11], (DEPTH, MLA_OUT, D_MODEL), MLA_OUT),
        'w_br_moba': nrm(ks[12], (DEPTH, MOBA_OUT, D_MODEL), MOBA_OUT),
        'w_br_dil': nrm(ks[13], (DEPTH, DIL_OUT, D_MODEL), DIL_OUT),
        'w_out': nrm(ks[14], (DEPTH, D_MODEL, D_MODEL), D_MODEL),
        'ffn2_norm': gain(ks[15], (DEPTH, D_MODEL)),
        'ffn2_w_gate': nrm(ks[16], (DEPTH, D_MODEL, D_FF), D_MODEL),
        'ffn2_w_up': nrm(ks[17], (DEPTH, D_MODEL, D_FF), D_MODEL),
        'ffn2_w_down': nrm(ks[18], (DEPTH, D_FF, D_MODEL), D_FF),
        'final_norm': gain(ks[19], (D_MODEL,)),
    }

def first_block(x, ffn1_norm, ffn1_w_gate, ffn1_w_up, ffn1_w_down, mix_norm, w_in, q_norm, w_uq,
              kv_norm, w_ukv, w_br_mla, w_br_moba, w_br_dil, w_out, ffn2_norm, ffn2_w_gate,
              ffn2_w_up, ffn2_w_down, final_norm):
    for l in range(DEPTH):
        x = x + 0.5 * swiglu(rms_norm(x, ffn1_norm[l]), ffn1_w_gate[l], ffn1_w_up[l], ffn1_w_down[l])
        x = x + hybrid_mixer(rms_norm(x, mix_norm[l]), w_in[l], q_norm[l], w_uq[l], kv_norm[l], w_ukv[l],
                             w_br_mla[l], w_br_moba[l], w_br_dil[l], w_out[l])
        x = x + 0.5 * swiglu(rms_norm(x, ffn2_norm[l]), ffn2_w_gate[l], ffn2_w_up[l], ffn2_w_down[l])
    return rms_norm(x, final_norm)


CHUNK = 64
Q_BLOCK = 128
LN_EPS = 1e-5
DEEPNORM_ALPHA = (2 * DEPTH) ** 0.25
DEEPNORM_BETA = (8 * DEPTH) ** -0.25

FFN_RES = 0.5

H_A = 8
HD_A = 64
ROT_A = HD_A // 4
ROPE_THETA_2 = 500000.0
A_W = H_A * 2 * HD_A

H_B = 16
P_B = 64
D_INNER = H_B * P_B
G_B = 2
N_B = 128
CONV_B = 4
CONV_DIM = D_INNER + 2 * G_B * N_B

H_C = 16
HD_C = 64
C_W = H_C * HD_C

N_BRANCH = 3
BR_W = 1024

_SEGMENTS = (A_W, A_W, A_W, D_INNER, CONV_DIM, H_B, C_W, C_W, C_W, N_BRANCH * D_MODEL)
SPLIT_POINTS = tuple(int(v) for v in np.cumsum(_SEGMENTS)[:-1])
N_IN = int(sum(_SEGMENTS))


def _layernorm(x, g, b):
    xf = x.astype(jnp.float32)
    mu = jnp.mean(xf, -1, keepdims=True)
    xc = xf - mu
    var = jnp.mean(xc * xc, -1, keepdims=True)
    y = xc * lax.rsqrt(var + LN_EPS) * g.astype(jnp.float32) + b.astype(jnp.float32)
    return y.astype(x.dtype)

def _rmsnorm(x, g):
    xf = x.astype(jnp.float32)
    y = xf * lax.rsqrt(jnp.mean(xf * xf, -1, keepdims=True) + LN_EPS)
    return (y * g.astype(jnp.float32)).astype(x.dtype)

def _swiglu(x, w_in, w_out):
    gate, up = jnp.split(x @ w_in, 2, axis=-1)
    return (jax.nn.silu(gate) * up) @ w_out

def _rotary_tables(s):
    half = ROT_A // 2
    inv_freq = ROPE_THETA_2 ** (-jnp.arange(half, dtype=jnp.float32) * 2.0 / ROT_A)
    ang = jnp.arange(s, dtype=jnp.float32)[:, None] * inv_freq[None, :]
    return jnp.cos(ang), jnp.sin(ang)

def _apply_partial_rope(x, cos, sin):
    half = ROT_A // 2
    c = cos.reshape(cos.shape[0], 1, 1, half).astype(x.dtype)
    sn = sin.reshape(sin.shape[0], 1, 1, half).astype(x.dtype)
    x1 = x[..., :half]
    x2 = x[..., half:ROT_A]
    return jnp.concatenate([x1 * c - x2 * sn, x2 * c + x1 * sn, x[..., ROT_A:]], axis=-1)

def _diff_attention(qa, ka, va, lam, subln_g, layer):
    b, s, _ = qa.shape
    nb = s // Q_BLOCK
    cos, sin = _rotary_tables(s)
    q = _apply_partial_rope(qa.reshape(b, s, H_A, 2, HD_A), cos, sin)
    k = _apply_partial_rope(ka.reshape(b, s, H_A, 2, HD_A), cos, sin)
    v = va.reshape(b, s, H_A, 2 * HD_A)
    lam_init = 0.8 - 0.6 * math.exp(-0.3 * layer)
    lf = lam.astype(jnp.float32)
    lam_full = jnp.exp(jnp.sum(lf[0] * lf[1])) - jnp.exp(jnp.sum(lf[2] * lf[3])) + lam_init
    kpos = jnp.arange(s)
    kchunk = kpos // CHUNK
    qpos = kpos.reshape(nb, Q_BLOCK)
    qb = jnp.moveaxis(q.reshape(b, nb, Q_BLOCK, H_A, 2, HD_A), 1, 0)
    scale = HD_A ** -0.5

    def block(args):
        qblk, qp = args
        sc = jnp.einsum('bqhmd,bkhmd->bhmqk', qblk, k).astype(jnp.float32) * scale
        allowed = kchunk[None, :] <= (qp // CHUNK)[:, None]
        p = jax.nn.softmax(jnp.where(allowed, sc, -jnp.inf), axis=-1)
        w = p[:, :, 0] - lam_full * p[:, :, 1]
        return jnp.einsum('bhqk,bkhe->bqhe', w.astype(v.dtype), v)

    out = lax.map(block, (qb, qpos))
    out = jnp.moveaxis(out, 0, 1).reshape(b, s, H_A, 2 * HD_A)
    out = _rmsnorm(out, subln_g) * (1.0 - lam_init)
    return out.reshape(b, s, A_W)

def _stick_breaking(qc, kc, vc):
    b, s, _ = qc.shape
    nb = s // Q_BLOCK
    k = kc.reshape(b, s, H_C, HD_C)
    v = vc.reshape(b, s, H_C, HD_C)
    qb = jnp.moveaxis(qc.reshape(b, nb, Q_BLOCK, H_C, HD_C), 1, 0)
    kpos = jnp.arange(s)
    qpos = kpos.reshape(nb, Q_BLOCK)
    scale = HD_C ** -0.5

    def block(args):
        qblk, qp = args
        z = jnp.einsum('bqhd,bkhd->bhqk', qblk, k).astype(jnp.float32) * scale
        strict = kpos[None, :] < qp[:, None]
        log_stay = jnp.where(strict, jax.nn.log_sigmoid(-z), 0.0)
        after = lax.cumsum(log_stay, axis=3, reverse=True) - log_stay
        a = jnp.where(strict, jnp.exp(jax.nn.log_sigmoid(z) + after), 0.0)
        return jnp.einsum('bhqk,bkhd->bqhd', a.astype(v.dtype), v)

    out = lax.map(block, (qb, qpos))
    return jnp.moveaxis(out, 0, 1).reshape(b, s, C_W)

def _ssd(x, dt, a_neg, bm, cm):
    b, s = x.shape[:2]
    nc = s // CHUNK
    hg = H_B // G_B
    xr = x.reshape(b, nc, CHUNK, G_B, hg, P_B)
    dtr = dt.reshape(b, nc, CHUNK, G_B, hg)
    br = bm.reshape(b, nc, CHUNK, G_B, N_B)
    cr = cm.reshape(b, nc, CHUNK, G_B, N_B)
    acum = jnp.cumsum(dtr * a_neg.reshape(G_B, hg), axis=2)
    xdt = xr * dtr[..., None]
    causal = jnp.tril(jnp.ones((CHUNK, CHUNK), dtype=bool))[None, None, :, :, None, None]
    seg = acum[:, :, :, None] - acum[:, :, None, :]
    decay = jnp.exp(jnp.where(causal, seg, -jnp.inf))
    cb = jnp.einsum('bctgn,bcsgn->bctsg', cr, br)
    y_diag = jnp.einsum('bctsgh,bcsghp->bctghp', cb[..., None] * decay, xdt)
    decay_to_end = jnp.exp(acum[:, :, -1:] - acum)
    states = jnp.einsum('bclgn,bclghp->bcghpn', br, xdt * decay_to_end[..., None])
    chunk_decay = jnp.exp(acum[:, :, -1])

    def step(h_prev, inp):
        st, dc = inp
        return h_prev * dc[..., None, None] + st, h_prev

    h0 = jnp.zeros((b, G_B, hg, P_B, N_B), jnp.float32)
    _, h_in = lax.scan(step, h0, (jnp.moveaxis(states, 1, 0), jnp.moveaxis(chunk_decay, 1, 0)))
    h_in = jnp.moveaxis(h_in, 0, 1)
    y_off = jnp.einsum('bclgn,bcghpn->bclghp', cr, h_in) * jnp.exp(acum)[..., None]
    return (y_diag + y_off).reshape(b, s, H_B, P_B)

def _mamba2(zb, xbc, dtb, conv_w, conv_b, dt_bias, a_log, d_skip, norm_g):
    b, s, _ = zb.shape
    xbc = lax.conv_general_dilated(
        xbc, conv_w[:, None, :], window_strides=(1,), padding=[(CONV_B - 1, 0)],
        dimension_numbers=('NWC', 'WIO', 'NWC'), feature_group_count=CONV_DIM) + conv_b
    xbc = jax.nn.silu(xbc).astype(jnp.float32)
    xs, bm, cm = jnp.split(xbc, [D_INNER, D_INNER + G_B * N_B], axis=-1)
    dt = jax.nn.softplus(dtb.astype(jnp.float32) + dt_bias.astype(jnp.float32))
    a_neg = -jnp.exp(a_log.astype(jnp.float32))
    xh = xs.reshape(b, s, H_B, P_B)
    y = _ssd(xh, dt, a_neg, bm.reshape(b, s, G_B, N_B), cm.reshape(b, s, G_B, N_B))
    y = y + d_skip.astype(jnp.float32)[:, None] * xh
    y = y.reshape(b, s, D_INNER) * jax.nn.silu(zb.astype(jnp.float32))
    y = _rmsnorm(y.reshape(b, s, G_B, D_INNER // G_B), norm_g.reshape(G_B, D_INNER // G_B))
    return y.reshape(b, s, D_INNER).astype(zb.dtype)

def _hybrid_mixer(h, layer, w_in, gate_bias, diff_lambda, diff_subln_g, conv_w, conv_b,
                  dt_bias, a_log, d_skip, norm_g, w_branch, w_out):
    b, s, _ = h.shape
    qa, ka, va, zb, xbc, dtb, qc, kc, vc, gpre = jnp.split(h @ w_in, SPLIT_POINTS, axis=-1)
    o_a = _diff_attention(qa, ka, va, diff_lambda, diff_subln_g, layer)
    o_b = _mamba2(zb, xbc, dtb, conv_w, conv_b, dt_bias, a_log, d_skip, norm_g)
    o_c = _stick_breaking(qc, kc, vc)
    branches = jnp.stack([o_a, o_b.astype(h.dtype), o_c], axis=2)
    proj = jnp.einsum('bsrc,rcd->bsrd', branches, w_branch)
    gates = jax.nn.sigmoid(gpre.reshape(b, s, N_BRANCH, D_MODEL) + gate_bias)
    merged = jnp.einsum('bsrd,bsrd->bsd', gates, proj)
    return merged @ w_out

def second_inputs(seed: int = 0) -> dict:
    key = jax.random.key(seed)
    ks = jax.random.split(key, 24)
    f32 = jnp.float32
    L = DEPTH

    def nrm(k, shape, scale):
        return jax.random.normal(k, shape, f32) * scale

    dt0 = jnp.exp(jax.random.uniform(ks[11], (L, H_B), f32, math.log(1e-3), math.log(1e-1)))
    return {
        'x': nrm(ks[0], (BATCH, SEQ, D_MODEL), 1.0),
        'ffn1_w_in': nrm(ks[1], (L, D_MODEL, 2 * D_FF), DEEPNORM_BETA * D_MODEL ** -0.5),
        'ffn1_w_out': nrm(ks[2], (L, D_FF, D_MODEL), DEEPNORM_BETA * D_FF ** -0.5),
        'ln1_g': 1.0 + nrm(ks[3], (L, D_MODEL), 0.02),
        'ln1_b': nrm(ks[4], (L, D_MODEL), 0.02),
        'w_mix_in': nrm(ks[5], (L, D_MODEL, N_IN), D_MODEL ** -0.5),
        'gate_bias': nrm(ks[6], (L, N_BRANCH, D_MODEL), 0.02),
        'diff_lambda': nrm(ks[7], (L, 4, HD_A), 0.1),
        'diff_subln_g': 1.0 + nrm(ks[8], (L, 2 * HD_A), 0.02),
        'ssm_conv_w': nrm(ks[9], (L, CONV_B, CONV_DIM), CONV_B ** -0.5),
        'ssm_conv_b': nrm(ks[10], (L, CONV_DIM), 0.02),
        'ssm_dt_bias': dt0 + jnp.log(-jnp.expm1(-dt0)),
        'ssm_A_log': jnp.log(jax.random.uniform(ks[12], (L, H_B), f32, 1.0, 16.0)),
        'ssm_D': 1.0 + nrm(ks[13], (L, H_B), 0.02),
        'ssm_norm_g': 1.0 + nrm(ks[14], (L, D_INNER), 0.02),
        'w_branch': nrm(ks[15], (L, N_BRANCH, BR_W, D_MODEL), DEEPNORM_BETA * BR_W ** -0.5),
        'w_mix_out': nrm(ks[16], (L, D_MODEL, D_MODEL), DEEPNORM_BETA * D_MODEL ** -0.5),
        'ln2_g': 1.0 + nrm(ks[17], (L, D_MODEL), 0.02),
        'ln2_b': nrm(ks[18], (L, D_MODEL), 0.02),
        'ffn2_w_in': nrm(ks[19], (L, D_MODEL, 2 * D_FF), DEEPNORM_BETA * D_MODEL ** -0.5),
        'ffn2_w_out': nrm(ks[20], (L, D_FF, D_MODEL), DEEPNORM_BETA * D_FF ** -0.5),
        'ln3_g': 1.0 + nrm(ks[21], (L, D_MODEL), 0.02),
        'ln3_b': nrm(ks[22], (L, D_MODEL), 0.02),
    }

def second_block(x, ffn1_w_in, ffn1_w_out, ln1_g, ln1_b, w_mix_in, gate_bias, diff_lambda,
              diff_subln_g, ssm_conv_w, ssm_conv_b, ssm_dt_bias, ssm_A_log, ssm_D, ssm_norm_g,
              w_branch, w_mix_out, ln2_g, ln2_b, ffn2_w_in, ffn2_w_out, ln3_g, ln3_b):
    for l in range(DEPTH):
        x = _layernorm(DEEPNORM_ALPHA * x + FFN_RES * _swiglu(x, ffn1_w_in[l], ffn1_w_out[l]),
                       ln1_g[l], ln1_b[l])
        mix = _hybrid_mixer(x, l, w_mix_in[l], gate_bias[l], diff_lambda[l], diff_subln_g[l],
                            ssm_conv_w[l], ssm_conv_b[l], ssm_dt_bias[l], ssm_A_log[l], ssm_D[l],
                            ssm_norm_g[l], w_branch[l], w_mix_out[l])
        x = _layernorm(DEEPNORM_ALPHA * x + mix, ln2_g[l], ln2_b[l])
        x = _layernorm(DEEPNORM_ALPHA * x + FFN_RES * _swiglu(x, ffn2_w_in[l], ffn2_w_out[l]),
                       ln3_g[l], ln3_b[l])
    return x


def setup_inputs(seed=0):
    out = dict(first_inputs(seed))
    for name, value in second_inputs(seed + 1).items():
        if name != "x":
            out[name + "_2"] = value
    return out


def reference(
    x, ffn1_norm, ffn1_w_gate, ffn1_w_up, ffn1_w_down, mix_norm, w_in, q_norm, w_uq, kv_norm,
    w_ukv, w_br_mla, w_br_moba, w_br_dil, w_out, ffn2_norm, ffn2_w_gate, ffn2_w_up, ffn2_w_down,
    final_norm, ffn1_w_in_2, ffn1_w_out_2, ln1_g_2, ln1_b_2, w_mix_in_2, gate_bias_2,
    diff_lambda_2, diff_subln_g_2, ssm_conv_w_2, ssm_conv_b_2, ssm_dt_bias_2, ssm_A_log_2,
    ssm_D_2, ssm_norm_g_2, w_branch_2, w_mix_out_2, ln2_g_2, ln2_b_2, ffn2_w_in_2, ffn2_w_out_2,
    ln3_g_2, ln3_b_2,
):
    x = first_block(
        x, ffn1_norm, ffn1_w_gate, ffn1_w_up, ffn1_w_down, mix_norm, w_in, q_norm, w_uq,
        kv_norm, w_ukv, w_br_mla, w_br_moba, w_br_dil, w_out, ffn2_norm, ffn2_w_gate, ffn2_w_up,
        ffn2_w_down, final_norm,
    )
    return second_block(
        x, ffn1_w_in_2, ffn1_w_out_2, ln1_g_2, ln1_b_2, w_mix_in_2, gate_bias_2, diff_lambda_2,
        diff_subln_g_2, ssm_conv_w_2, ssm_conv_b_2, ssm_dt_bias_2, ssm_A_log_2, ssm_D_2,
        ssm_norm_g_2, w_branch_2, w_mix_out_2, ln2_g_2, ln2_b_2, ffn2_w_in_2, ffn2_w_out_2,
        ln3_g_2, ln3_b_2,
    )


_drawn_inputs = setup_inputs


def setup_inputs(seed=0):
    import zlib

    import numpy as np

    out = dict(_drawn_inputs(seed))
    spreads = {}
    factors = {'ffn1_norm': 8.0,
     'mix_norm': 8.0,
     'q_norm': 8.0,
     'kv_norm': 8.0,
     'ffn2_norm': 8.0,
     'final_norm': 19.848,
     'gate_bias_2': 8.0,
     'diff_lambda_2': 6.29,
     'diff_subln_g_2': 33.563,
     'ssm_conv_b_2': 8.0,
     'ssm_A_log_2': 28.864,
     'ssm_D_2': 29.92,
     'ssm_norm_g_2': 26.24}
    for name, (base, spread) in spreads.items():
        noise = np.random.default_rng([zlib.crc32(name.encode()), seed]).standard_normal(out[name].shape)
        drawn = base * np.exp(spread * noise) if base else spread * noise
        out[name] = jnp.asarray(drawn.astype(out[name].dtype))
    for name, factor in factors.items():
        out[name] = (out[name] * factor).astype(out[name].dtype)
    return out
```

```python
import math
from collections import deque
from contextlib import ExitStack

import numpy as np

import concourse.bass as bass
from concourse import mybir

F32 = mybir.dt.float32
F32R = mybir.dt.float32r
ACT = mybir.ActivationFunctionType
ALU = mybir.AluOpType
AX_X = mybir.AxisListType.X

D = 1024
DFF = 2816
NCH = DFF // 256
NEG = -1e30
PIECE = 1024
BLOCK = 2048
NRAW = 3
NHL = 5
N_IN1 = 6944
MIX2 = 11792
QA, KA, VA, ZB, XBC, DTB, QC, KC, VC, GP = (0, 1024, 2048, 3072, 4096, 5632, 5648, 6672, 7696, 8720)
ALPHA = 4.0 ** 0.25


def plan():
    pieces = []

    def gemm(key, idx, nk, ranges):
        width = sum(c1 - c0 for _, c0, c1 in ranges)
        per = PIECE // width
        for k in range(0, nk, per):
            pieces.append((key, width, [(idx, kt, ranges) for kt in range(k, min(nk, k + per))]))

    def ffn(key, l, gate, up, shift, down):
        for c in range(NCH):
            gemm((key, "up", l, c), (l,), 8,
                 [(gate, 256 * c, 256 * c + 256), (up, shift + 256 * c, shift + 256 * c + 256)])
        gemm((key, "down", l), (l,), 22, [(down, 0, 1024)])

    for l in (0, 1):
        ffn("f1", l, "ffn1_w_gate", "ffn1_w_up", 0, "ffn1_w_down")
        gemm(("mla", l), (l,), 8, [("w_in", 0, 416)])
        mo, di = 416, 416 + 1152
        for c in range(4):
            gemm(("qk1", l, c), (l,), 8, QK1[c])
            if c == 0:
                for j in (0, 1):
                    gemm(("uq", l, j), (l,), 2, [("w_uq", 288 * j, 288 * j + 288)])
                for j in (0, 1):
                    gemm(("ukv", l, j), (l,), 1, [("w_ukv", 384 * j, 384 * j + 384)])
        gemm(("qk1", l, 4), (l,), 8, QK1[4])
        gemm(("v1", l, 0), (l,), 8, [("w_in", mo + 768, mo + 1152)])
        for j in (0, 1):
            gemm(("v1", l, 1 + j), (l,), 8, [("w_in", di + 1536 + 384 * j, di + 1920 + 384 * j)])
        for c in range(6):
            gemm(("g1", l, c), (l,), 8, [("w_in", 3872 + 512 * c, 4384 + 512 * c)])
        for r, (name, nk) in enumerate(BR1):
            for n in (0, 1):
                gemm(("br1", l, r, n), (l,), nk, [(name, 512 * n, 512 * n + 512)])
        for n in (0, 1):
            gemm(("o1", l, n), (l,), 8, [("w_out", 512 * n, 512 * n + 512)])
        ffn("f2", l, "ffn2_w_gate", "ffn2_w_up", 0, "ffn2_w_down")
    for l in (0, 1):
        ffn("F1", l, "ffn1_w_in_2", "ffn1_w_in_2", DFF, "ffn1_w_out_2")
        w = "w_mix_in_2"
        gemm(("dt", l), (l,), 8, [(w, DTB, DTB + 16)])
        for c in (2, 0, 1):
            gemm(("xbc", l, c), (l,), 8, [(w, XBC + 512 * c, XBC + 512 * c + 512)])
        for key, at in (("z", ZB), ("qa", QA), ("ka", KA), ("va", VA), ("qc", QC), ("kc", KC), ("vc", VC)):
            for n in (0, 1):
                gemm((key, l, n), (l,), 8, [(w, at + 512 * n, at + 512 * n + 512)])
        for c in range(6):
            gemm(("g2", l, c), (l,), 8, [(w, GP + 512 * c, GP + 512 * c + 512)])
        for r in (1, 0, 2):
            for n in (0, 1):
                gemm(("br2", l, r, n), (l, r), 8, [("w_branch_2", 512 * n, 512 * n + 512)])
        for n in (0, 1):
            gemm(("o2", l, n), (l,), 8, [("w_mix_out_2", 512 * n, 512 * n + 512)])
        ffn("F2", l, "ffn2_w_in_2", "ffn2_w_in_2", DFF, "ffn2_w_out_2")
    return pieces


BR1 = [("w_br_mla", 3), ("w_br_moba", 3), ("w_br_dil", 2)]
_Q = [("w_in", 416 + 128 * i) for i in range(6)] + [("w_in", 1568 + 128 * i) for i in range(12)]
QK1 = [[(n, c, c + 128) for n, c in _Q[4 * i:4 * i + 4]] for i in range(5)]

COLS = {}
ROWS = {"lam": (0, 256), "dtb": (256, 272), "alog": (272, 288), "dsk": (288, 304)}


def cols_plan():
    out, at = [], 0
    for l in (0, 1):
        for name, n in (("ffn1_norm", 8), ("mix_norm", 8), ("q_norm", 2), ("kv_norm", 1), ("ffn2_norm", 8),
                        ("diff_subln_g_2", 1), ("ssm_norm_g_2", 8), ("ssm_conv_w_2", 48), ("ssm_conv_b_2", 12)):
            out.append((name, l, at, n))
            COLS[(name, l)] = at
            at += n
    return out, at


_COLS, NCOLS = cols_plan()
VROWS = ["final"] + [(l, n) for l in (0, 1) for n in
                     ("ln1_g", "ln1_b", "gb0", "gb1", "gb2", "ln2_g", "ln2_b", "ln3_g", "ln3_b")]


def place_pieces():
    blocks, cur, used = [], [], 0
    for i, (key, width, kts) in enumerate(plan()):
        n = width * len(kts)
        if used + n > BLOCK:
            blocks.append((cur, used))
            cur, used = [], 0
        cur.append((i, used, n))
        used += n
    blocks.append((cur, used))
    return blocks


class Engine:
    def __init__(self, sem):
        self.sem, self.queue, self.n, self.met = sem, [], 0, {}

    def need(self, *tokens):
        for t in tokens:
            if t is None:
                continue
            if isinstance(t, (list, deque)):
                self.need(*t)
                continue
            sem, v = t
            if self.met.get(id(sem), 0) < v:
                self.met[id(sem)] = v
                self.queue.append(lambda e, sem=sem, v=v: e.wait_ge(sem, v))

    def go(self, fn):
        self.n += 1
        self.queue.append(lambda e, fn=fn: fn(e).then_inc(self.sem, 1))
        return (self.sem, self.n)

    def put(self, fn):
        self.queue.append(fn)

    def run(self, e):
        for fn in self.queue:
            fn(e)


class Pool:

    def __init__(self, bufs):
        self.free = deque((b, []) for b in bufs)

    def get(self):
        return self.free.popleft()

    def put(self, buf, tokens):
        self.free.append((buf, list(tokens)))


class Line:

    def __init__(self, sem, buf):
        self.sem, self.buf, self.n, self.free = sem, buf, 0, []


def bass_two_blocks(nc: bass.Bass, x, wpack, cols, rows, vrows, ident_d, bias_d, msk_d, rope_d, scratch, out):
    ctx = ExitStack()
    with ctx:
        counter = [0]

        def sbuf(shape, dt=F32, scope=ctx):
            counter[0] += 1
            return scope.enter_context(nc.sbuf_tensor(f"t{counter[0]}", shape, dt))

        def sem(name):
            return ctx.enter_context(nc.semaphore(name))

        pe, act, dve, pool = (Engine(sem(n)) for n in ("s_pe", "s_act", "s_dve", "s_pool"))
        sp = Engine(sem("s_sp"))
        psum = [ctx.enter_context(nc.psum_tensor(f"ps{i}", [128, 512], F32)) for i in range(8)]
        mmb, aux = Pool(psum[0:4]), Pool(psum[4:8])

        RAW = [sbuf([128, BLOCK]) for _ in range(NRAW)]
        HI = [sbuf([128, PIECE], F32R) for _ in range(NHL)]
        LO = [sbuf([128, PIECE], F32R) for _ in range(NHL)]
        X = [sbuf([128, D]) for _ in range(2)]
        XNB = sbuf([128, 2, D])
        XN = [XNB[:, t, :] for t in (0, 1)]
        ident = sbuf([128, 128])
        colt = sbuf([128, NCOLS])
        STAT = sbuf([128, 512])
        stat_at = [0]

        def stat(n):
            if stat_at[0] + n > 512:
                stat_at[0] = 0
            a = STAT[:, stat_at[0]:stat_at[0] + n]
            stat_at[0] += n
            return a

        class XT:
            def __init__(self, nk, scope=ctx):
                self.H = sbuf([128, nk, 256], F32R, scope)
                self.L = sbuf([128, nk, 256], F32R, scope)
                self.tok = [None] * nk
                self.free = []

        xT = XT(8)
        phalf = sbuf([128, 2])
        t_half = pool.go(lambda e: e.memset(phalf[:, :], -0.5))

        def A(out, in_, func, need=(), scale=1.0, bias=None, accum=None):
            act.need(*need)
            kw = {}
            if bias is not None:
                kw["bias"] = bias
            if accum is not None:
                kw["accum_out"] = accum
            return act.go(lambda e: e.activation(out, in_, func, scale=scale, **kw))

        def TT(out, a, b, op, need=(), eng=None):
            g = eng or dve
            g.need(*need)
            return g.go(lambda e: e.tensor_tensor(out, a, b, op))

        def TS(out, a, s1, s2, op0, op1=None, need=()):
            dve.need(*need)
            if op1 is None:
                return dve.go(lambda e: e.tensor_scalar(out, a, s1, None, op0))
            return dve.go(lambda e: e.tensor_scalar(out, a, s1, s2, op0, op1))

        def STT(out, a, s, b, op0, op1, need=()):
            dve.need(*need)
            return dve.go(lambda e: e.scalar_tensor_tensor(out=out, in0=a, scalar=s, in1=b, op0=op0, op1=op1))

        def RED(out, a, op, need=(), negate=None):
            dve.need(*need)
            return dve.go(lambda e: e.tensor_reduce(out, a, AX_X, op, negate=negate))

        def RCP(out, a, need=()):
            dve.need(*need)
            return dve.go(lambda e: e.reciprocal(out, a))

        def CP(out, a, need=()):
            dve.need(*need)
            return dve.go(lambda e: e.tensor_copy(out, a))

        def mm(out, l, r, start, stop, last=False, skip=False):
            fn = lambda e: e.matmul(out, l, r, start=start, stop=stop, skip_group_check=skip)
            return pe.go(fn) if last else pe.put(fn)

        def tr(out, in_, last=False):
            k = in_.shape[0]
            fn = lambda e: e.transpose(out, in_, ident[0:k, 0:k])
            return pe.go(fn) if last else pe.put(fn)

        def rsqrt(var, need):
            n = var.shape[-1]
            r = stat(n)
            pool.need(t_half, *need)
            return r, pool.go(lambda e: e.tensor_tensor(r, var, phalf[:, 0:n], ALU.pow))

        def bc(ap, n):
            return ap.unsqueeze(2).broadcast_to([ap.shape[0], ap.shape[1], n])

        def bc1(ap, n):
            return ap.unsqueeze(1).broadcast_to([ap.shape[0], n, ap.shape[1]])

        def once(out, in_, name):
            s = sem(name)
            sp.put(lambda e: e.dma_start(out, in_).then_inc(s, 16))
            return (s, 16)

        def load(line, out, in_, need=()):
            sp.need(*line.free, *need)
            line.free = []
            line.n += 1
            sp.put(lambda e: e.dma_start(out, in_).then_inc(line.sem, 16))
            return (line.sem, 16 * line.n)

        pieces = plan()
        blocks = place_pieces()
        dsem = [sem(f"s_w{i}") for i in range(NRAW)]
        where = {}
        offs, at = [], 0
        for b, (ps, used) in enumerate(blocks):
            offs.append(at)
            at += 128 * used
            for i, off, n in ps:
                where[i] = (b, off, n)

        class Stream:
            u = 0
            loaded = 0
            split = 0
            t_raw = {}
            t_hi = {}
            t_lo = {}
            t_pe = {}

            def load(self):
                b = self.loaded
                if b >= len(blocks):
                    return
                if b >= NRAW:
                    last = blocks[b - NRAW][0][-1][0]
                    if last not in self.t_lo:
                        return
                    sp.need(self.t_hi[last], self.t_lo[last])
                used = blocks[b][1]
                src = wpack[offs[b]:offs[b] + 128 * used].rearrange("(p c) -> p c", p=128)
                dst = RAW[b % NRAW][:, 0:used]
                sp.put(lambda e: e.dma_start(dst, src).then_inc(dsem[b % NRAW], 16))
                self.t_raw[b] = (dsem[b % NRAW], 16 * (b // NRAW + 1))
                self.loaded += 1

            def halve(self, i):
                b, off, n = where[i]
                raw = RAW[b % NRAW][:, off:off + n]
                hi, lo = HI[i % NHL][:, 0:n], LO[i % NHL][:, 0:n]
                self.t_hi[i] = A(hi, raw, ACT.Copy, [self.t_raw[b], self.t_pe.get(i - NHL)])
                self.t_lo[i] = TT(lo, raw, hi.bitcast(F32), ALU.subtract,
                                  [self.t_raw[b], self.t_hi[i], self.t_pe.get(i - NHL)])

            def ahead(self):
                while self.loaded < len(blocks) and (self.loaded < NRAW or
                                                     blocks[self.loaded - NRAW][0][-1][0] in self.t_lo):
                    self.load()

            def take(self, key):
                assert pieces[self.u][0] == key, (pieces[self.u][0], key)
                self.ahead()
                while self.split < min(len(pieces), self.u + NHL - 1):
                    self.halve(self.split)
                    self.split += 1
                    self.ahead()
                i = self.u
                _, width, kts = pieces[i]
                return HI[i % NHL], LO[i % NHL], width, [kt for _, kt, _ in kts], [self.t_hi[i], self.t_lo[i]]

            def done(self, tok):
                self.t_pe[self.u] = tok
                self.u += 1
                bg_step()

        S = Stream()
        fibers = deque()

        def bg_step():
            for f in list(fibers):
                try:
                    next(f)
                except StopIteration:
                    fibers.remove(f)

        def bg_drain():
            while fibers:
                bg_step()

        def gemm(key, xt, nk, outs, need=()):
            pe.need(*need)
            seen = 0
            while seen < nk:
                hi, lo, w, kts, ready = S.take(key)
                pe.need(*ready)
                tok = None
                for i, kt in enumerate(kts):
                    pe.need(xt.tok[kt])
                    o = i * w
                    for t in (0, 1):
                        sl = slice(128 * t, 128 * t + 128)
                        for n, (xs, ws) in enumerate(((xt.H, hi), (xt.H, lo), (xt.L, hi))):
                            for ap, c0, c1 in outs[t]:
                                last = n == 2 and t == 1 and i == len(kts) - 1 and c1 == w
                                tok = mm(ap, xs[:, kt, sl], ws[:, o + c0:o + c1], kt == 0 and n == 0,
                                         kt == nk - 1 and n == 2, last)
                seen += len(kts)
                S.done(tok)
            return tok

        def gemm_w(key, xt, nk, outs, need=()):
            pe.need(*need)
            seen = 0
            while seen < nk:
                hi, lo, w, kts, ready = S.take(key)
                pe.need(*ready)
                for i, kt in enumerate(kts):
                    pe.need(xt.tok[kt])
                    for m, ap in enumerate(outs):
                        o = i * w + 128 * m
                        for n, (ws, xs) in enumerate(((hi, xt.H), (hi, xt.L), (lo, xt.H))):
                            last = n == 2 and m == len(outs) - 1 and i == len(kts) - 1
                            tok = mm(ap, ws[:, o:o + 128], xs[:, kt, :], kt == 0 and n == 0 and m % 2 == 0,
                                     kt == nk - 1 and n == 2, last, skip=True)
                seen += len(kts)
                S.done(tok)
            return tok

        def to_T(src, toks, nk, xt, gain=None, at=0):
            last = None
            for k in range(0, nk, 2):
                m = min(2, nk - k)
                ps, free = aux.get()
                pe.need(*free, *toks)
                for j in range(m):
                    for t in (0, 1):
                        last = tr(ps[:, 256 * j + 128 * t:256 * j + 128 * t + 128],
                                  src[t][:, 128 * (k + j):128 * (k + j) + 128], last=(j == m - 1 and t == 1))
                if gain is None:
                    hi = xt.H[:, at + k:at + k + m, :].rearrange("p a b -> p (a b)")
                    lo = xt.L[:, at + k:at + k + m, :].rearrange("p a b -> p (a b)")
                    t1 = A(hi, ps[:, 0:256 * m], ACT.Copy, [last, xt.free])
                    t2 = TT(lo, ps[:, 0:256 * m], hi.bitcast(F32), ALU.subtract, [last, t1, xt.free])
                else:
                    for j in range(m):
                        t1 = A(xt.H[:, at + k + j, :], ps[:, 256 * j:256 * j + 256], ACT.Copy, [last, xt.free],
                               scale=gain[:, k + j:k + j + 1])
                    for j in range(m):
                        hi, lo = xt.H[:, at + k + j, :], xt.L[:, at + k + j, :]
                        g = gain[:, k + j:k + j + 1]
                        p = ps[:, 256 * j:256 * j + 256]
                        t2 = STT(lo, p, g, hi.bitcast(F32), ALU.mult, ALU.subtract, [last, t1, xt.free])
                for j in range(m):
                    xt.tok[at + k + j] = [t1, t2]
                aux.put(ps, [t1, t2])
            return last

        def col(name, l, n):
            return colt[:, COLS[(name, l)]:COLS[(name, l)] + n]

        state = {"x": [[], []], "xn": []}

        for t in (0, 1):
            state["x"][t] = [once(X[t][:, :], x[0, 128 * t:128 * t + 128, :], f"s_x{t}")]
        t_id = once(ident[:, :], ident_d, "s_id")
        t_col = once(colt[:, :], cols, "s_col")
        S.ahead()

        def rms_to(gain, eps=1e-6):
            toks = []
            for t in (0, 1):
                ss, ms = stat(1), stat(1)
                a = A(XN[t][:, :], X[t][:, :], ACT.Square, [*state["x"][t], state["xn"]], accum=ss)
                b = TS(ms, ss, 1.0 / D, eps, ALU.mult, ALU.add, [a])
                r, c = rsqrt(ms, [b])
                toks.append(TS(XN[t][:, :], X[t][:, :], r, None, ALU.mult, need=[c]))
            state["xn"] = [to_T(XN, [*toks, t_id, t_col], 8, xT, gain)]

        def swiglu(key, l, hT, sring):
            pend = []

            def turn(c, hb, th):
                ps, free = aux.get()
                pe.need(*free, *th)
                for j in (0, 1):
                    for t in (0, 1):
                        last = tr(ps[:, 256 * j + 128 * t:256 * j + 128 * t + 128],
                                  hb[:, t, 128 * j:128 * j + 128], last=(j == 1 and t == 1))
                hi = hT.H[:, 2 * c:2 * c + 2, :].rearrange("p a b -> p (a b)")
                lo = hT.L[:, 2 * c:2 * c + 2, :].rearrange("p a b -> p (a b)")
                t1 = A(hi, ps[:, :], ACT.Copy, [last])
                t2 = TT(lo, ps[:, :], hi.bitcast(F32), ALU.subtract, [last, t1])
                hT.tok[2 * c] = hT.tok[2 * c + 1] = [t1, t2]
                aux.put(ps, [t1, t2])
                sring.put(hb, [last])

            def act_step(c, banks, tok):
                hb, free = sring.get()
                th = []
                for t in (0, 1):
                    a = A(hb[:, t, :], banks[t][:, 0:256], ACT.Silu, [tok, *free])
                    th.append(TT(hb[:, t, :], hb[:, t, :], banks[t][:, 256:512], ALU.mult, [a, tok]))
                    mmb.put(banks[t], [th[-1]])
                yield
                turn(c, hb, th)

            for c in range(NCH):
                banks, need = [], []
                for t in (0, 1):
                    b, f = mmb.get()
                    banks.append(b)
                    need += f
                tok = gemm((key, "up", l, c), xT, 8, [[(b[:, :], 0, 512)] for b in banks], need)
                f = act_step(c, banks, tok)
                next(f)
                fibers.append(f)
            xT.free = [tok]
            banks, need = [], []
            for _ in range(4):
                b, f = mmb.get()
                banks.append(b)
                need += f
            if fibers:
                pass
            outs = [[(banks[2 * t + n][:, :], 512 * n, 512 * n + 512) for n in (0, 1)] for t in (0, 1)]
            tok = gemm((key, "down", l), hT, 22, outs, need)
            return banks, tok

        def first(l, blk):
            def ffn(key, name):
                rms_to(col(name, l, 8))
                with ExitStack() as ph:
                    hT = XT(22, ph)
                    sring = Pool([sbuf([128, 2, 256], F32, ph) for _ in range(2)])
                    banks, tok = swiglu(key, l, hT, sring)
                    for t in (0, 1):
                        ts = []
                        for n in (0, 1):
                            xs = X[t][:, 512 * n:512 * n + 512]
                            ts.append(STT(xs, banks[2 * t + n][:, :], 0.5, xs, ALU.mult, ALU.add, [tok]))
                            mmb.put(banks[2 * t + n], [ts[-1]])
                        state["x"][t] = ts

            ffn("f1", "ffn1_norm")
            mixer1(l, blk)
            ffn("f2", "ffn2_norm")

        def softmax_probs(S_mm, scale, bias, bias_tok, need, tmp, nm, den, pr):
            ps, free = aux.get()
            pe.need(*free, *need)
            qT, kT = S_mm
            mm(ps[:, 0:128], qT[:, 0:128], kT[:, 0:128], True, True)
            t0 = mm(ps[:, 128:384], qT[:, 128:256], kT[:, 0:256], True, True, True)
            sm, f2 = tmp.get()
            t1 = STT(sm[:, :], ps[:, 0:384], scale, bias, ALU.mult, ALU.add, [t0, bias_tok, *f2])
            aux.put(ps, [t1])
            RED(nm[:, 0:1], sm[:, 0:128], ALU.max, [t1], negate=True)
            t2 = RED(nm[:, 1:2], sm[:, 128:384], ALU.max, negate=True)
            p, f3 = pr.get()
            A(p[:, 0:128], sm[:, 0:128], ACT.Exp, [t2, *f3], bias=nm[:, 0:1], accum=den[:, 0:1])
            t3 = A(p[:, 128:384], sm[:, 128:384], ACT.Exp, bias=nm[:, 1:2], accum=den[:, 1:2])
            tmp.put(sm, [t3])
            return p, t3, t1

        def turn_probs(p, need, pr, pt):
            ps, free = aux.get()
            pe.need(*free, *need)
            for j in range(3):
                t0 = tr(ps[:, 128 * j:128 * j + 128], p[:, 128 * j:128 * j + 128], last=(j == 2))
            pr.put(p, [t0])
            q, f = pt.get()
            t1 = A(q[:, :], ps[:, 0:384], ACT.Copy, [t0, *f])
            aux.put(ps, [t1])
            return q, t1

        def values(q, t_q, v, dv, pt, need=()):
            ps, free = aux.get()
            pe.need(*free, t_q, *need)
            mm(ps[:, 0:dv], q[:, 0:128], v[0], True, True)
            mm(ps[:, dv:2 * dv], q[:, 128:256], v[0], True, False)
            t0 = mm(ps[:, dv:2 * dv], q[:, 256:384], v[1], False, True, True)
            pt.put(q, [t0])
            return ps, t0

        def mixer1(l, blk):
            rms_to(col("mix_norm", l, 8))
            with ExitStack() as ph:
                QK = sbuf([128, 18, 256], F32, ph)
                V = sbuf([128, 2, 1152], F32, ph)
                Omla = sbuf([128, 2, 384], F32, ph)
                Omo = sbuf([128, 2, 384], F32, ph)
                Odn = sbuf([128, 2, 768], F32, ph)
                Odl = sbuf([128, 2, 256], F32, ph)
                oT = [XT(3, ph) for _ in range(2)]
                tmp = Pool([sbuf([128, 384], F32, ph) for _ in range(2)])
                pr = Pool([sbuf([128, 384], F32, ph) for _ in range(3)])
                pt = Pool([sbuf([128, 384], F32, ph) for _ in range(2)])
                t_qk = {}
                t_v = {}
                res = {}
                fence = [*state["xn"]]

                def finish(o_view, den2, n):
                    def f(ps, t0, need):
                        r = stat(2)
                        a = RCP(r, den2, need)
                        b = TT(o_view, ps[:, 0:2 * n].rearrange("p (t d) -> p t d", t=2), bc(r, n), ALU.mult,
                               [a, t0])
                        aux.put(ps, [b])
                        return b
                    return f

                with ExitStack() as pm:
                    lat = sbuf([128, 2, 416], F32, pm)
                    qs = sbuf([128, 2, 576], F32, pm)
                    ks = sbuf([128, 2, 576], F32, pm)
                    vm = sbuf([128, 2, 384], F32, pm)
                    cq = XT(2, pm)
                    ckv = XT(1, pm)
                    ra = sbuf([128, 2, 96], F32, pm)
                    rb = sbuf([128, 2, 96], F32, pm)
                    qkh = Pool([sbuf([96, 512], F32, pm) for _ in range(2)])
                    tm = {}

                    def rope(dst, src, t, h, need):
                        cc, ss = blk["rope"][:, t, 0:32], blk["rope"][:, t, 32:64]
                        a3 = ra[:, t, 0:32 * h].rearrange("p (h d) -> p h d", h=h)
                        b3 = rb[:, t, 0:32 * h].rearrange("p (h d) -> p h d", h=h)
                        TT(a3, src, bc1(cc, h), ALU.mult, [*need, blk["t_rope"]])
                        t1 = TT(b3, src, bc1(ss, h), ALU.mult)
                        TT(dst[:, :, 0:16], a3[:, :, 0:16], b3[:, :, 16:32], ALU.subtract, [t1])
                        return TT(dst[:, :, 16:32], a3[:, :, 16:32], b3[:, :, 0:16], ALU.add), t1

                    def latents(banks, tok):
                        a, b = [], []
                        ss = stat(4)
                        for t in (0, 1):
                            A(lat[:, t, 0:256], banks[t][:, 0:256], ACT.Square, [tok, *fence],
                              accum=ss[:, 2 * t:2 * t + 1])
                            a.append(A(lat[:, t, 256:384], banks[t][:, 256:384], ACT.Square,
                                       accum=ss[:, 2 * t + 1:2 * t + 2]))
                        ms = stat(4)
                        toks = []
                        for t in (0, 1):
                            TS(ms[:, 2 * t:2 * t + 1], ss[:, 2 * t:2 * t + 1], 1.0 / 256, 1e-6, ALU.mult, ALU.add, [a[t]])
                            b.append(TS(ms[:, 2 * t + 1:2 * t + 2], ss[:, 2 * t + 1:2 * t + 2], 1.0 / 128, 1e-6,
                                        ALU.mult, ALU.add))
                            kr = lat[:, t, 384:416].unsqueeze(1)
                            tk, _ = rope(kr, banks[t][:, 384:416].unsqueeze(1), t, 1, [tok, a[t]])
                            tm["kr", t] = CP(ks[:, t, :].rearrange("p (h d) -> p h d", h=6)[:, :, 64:96],
                                             bc1(lat[:, t, 384:416], 6), [tk])
                        for t in (0, 1):
                            r, c = rsqrt(ms[:, 2 * t:2 * t + 2], [b[t]])
                            toks.append(TS(lat[:, t, 0:256], banks[t][:, 0:256], r[:, 0:1], None, ALU.mult, need=[c]))
                            toks.append(TS(lat[:, t, 256:384], banks[t][:, 256:384], r[:, 1:2], None, ALU.mult))
                            mmb.put(banks[t], [toks[-1], tm["kr", t]])
                        yield
                        to_T([lat[:, t, 0:256] for t in (0, 1)], toks, 2, cq, col("q_norm", l, 2))
                        to_T([lat[:, t, 256:384] for t in (0, 1)], toks, 1, ckv, col("kv_norm", l, 1))

                    banks, need = two()
                    tok = gemm(("mla", l), xT, 8, [[(b[:, 0:416], 0, 416)] for b in banks], need)
                    f = latents(banks, tok)
                    next(f)
                    fibers.append(f)

                    def qk_chunk(c):
                        n = 4 if c < 4 else 2
                        banks, need = two() if n == 4 else one()
                        outs = [banks[m // 2][:, 256 * (m % 2):256 * (m % 2) + 256] for m in range(n)]
                        tok = gemm_w(("qk1", l, c), xT, 8, outs, need)
                        for j, b in enumerate(banks):
                            dst = QK[:, 4 * c + 2 * j:4 * c + 2 * j + 2, :].rearrange("p a b -> p (a b)")
                            if j == 0:
                                t1 = A(dst, b[:, :], ACT.Copy, [tok])
                            else:
                                t1 = CP(dst, b[:, :], [tok])
                            mmb.put(b, [t1])
                            t_qk[4 * c + 2 * j] = t_qk[4 * c + 2 * j + 1] = t1

                    qk_chunk(0)
                    for j in (0, 1):
                        banks, need = two()
                        tok = gemm(("uq", l, j), cq, 2, [[(b[:, 0:288], 0, 288)] for b in banks], need)
                        for t in (0, 1):
                            dst = qs[:, t, 288 * j:288 * j + 288]
                            a = A(dst, banks[t][:, 0:288], ACT.Copy, [tok])
                            v3 = dst.rearrange("p (h d) -> p h d", h=3)[:, :, 64:96]
                            p3 = banks[t][:, 0:288].rearrange("p (h d) -> p h d", h=3)[:, :, 64:96]
                            b, t1 = rope(v3, p3, t, 3, [a])
                            tm["q", j, t] = b
                            mmb.put(banks[t], [a, t1])
                    for j in (0, 1):
                        banks, need = two()
                        tok = gemm(("ukv", l, j), ckv, 1, [[(b[:, 0:384], 0, 384)] for b in banks], need)
                        for t in (0, 1):
                            p3 = banks[t][:, 0:384].rearrange("p (h d) -> p h d", h=3)
                            k3 = ks[:, t, 288 * j:288 * j + 288].rearrange("p (h d) -> p h d", h=3)
                            v3 = vm[:, t, 192 * j:192 * j + 192].rearrange("p (h d) -> p h d", h=3)
                            a = A(k3[:, :, 0:64], p3[:, :, 0:64], ACT.Copy, [tok])
                            b = CP(v3, p3[:, :, 64:128], [tok, a])
                            tm["k", j, t] = [a, tm["kr", t]]
                            tm["v", j, t] = b
                            mmb.put(banks[t], [a, b])

                    def mla_heads():
                        turned, probs, pts = {}, {}, {}
                        for s in range(6 + 5):
                            if s < 6:
                                ps, free = aux.get()
                                pe.need(*free)
                                for n, src in enumerate((qs, ks)):
                                    for t in (0, 1):
                                        pe.need(tm["qk"[n], s // 3, t])
                                        t0 = tr(ps[0:96, 256 * n + 128 * t:256 * n + 128 * t + 128],
                                                src[:, t, 96 * s:96 * s + 96], last=(n == 1 and t == 1))
                                b, f = qkh.get()
                                t1 = A(b[:, :], ps[0:96, :], ACT.Copy, [t0, *f])
                                aux.put(ps, [t1])
                                turned[s] = (b, t1)
                            if 0 <= s - 1 < 6:
                                h = s - 1
                                b, t1 = turned[h]
                                nm, den = stat(2), stat(2)
                                p, t3, t2 = softmax_probs((b[:, 0:256], b[:, 256:512]), 96.0 ** -0.5,
                                                          blk["causal"][:, :], blk["t_causal"], [t1], tmp, nm, den, pr)
                                qkh.put(b, [t2])
                                probs[h] = (p, t3, den)
                            if 0 <= s - 3 < 6:
                                h = s - 3
                                p, t3, den = probs[h]
                                pts[h] = turn_probs(p, [t3], pr, pt)
                            if 0 <= s - 4 < 6:
                                h = s - 4
                                q, tq = pts[h]
                                v = [vm[:, t, 64 * h:64 * h + 64] for t in (0, 1)]
                                ps, t0 = values(q, tq, v, 64, pt, [tm["v", h // 3, 0], tm["v", h // 3, 1]])
                                res["mla"] = finish(Omla[:, :, 64 * h:64 * h + 64], probs[h][2], 64)(ps, t0, [probs[h][1]])
                            yield

                    fibers.append(mla_heads())
                    for c in (1, 2, 3, 4):
                        qk_chunk(c)
                    for j, (c0, w) in enumerate(((0, 384), (384, 384), (768, 384))):
                        banks, need = two()
                        tok = gemm(("v1", l, j), xT, 8, [[(b[:, 0:384], 0, 384)] for b in banks], need)
                        for t in (0, 1):
                            dst = V[:, t, c0:c0 + w]
                            t1 = (A(dst, banks[t][:, 0:w], ACT.Copy, [tok]) if t == 0
                                  else CP(dst, banks[t][:, 0:w], [tok]))
                            t_v[j, t] = t1
                            mmb.put(banks[t], [t1])
                    bg_drain()

                G = sbuf([128, 2, 3072], F32, ph)
                nmd, dnd = stat(24), stat(24)

                def heads():
                    items = [("mo", h) for h in range(6)] + [("di", h) for h in range(12)]
                    probs, pts, tl = {}, {}, {}
                    last = []
                    nb = len(blk["bias"])
                    for s in range(-1, len(items) + 4):
                        if s + 1 < len(items):
                            kind, h = items[s + 1]
                            line = blk["bias"][(s + 1) % nb]
                            row = h + 12 if kind == "mo" else h
                            tl[s + 1] = load(line, line.buf[:, :], bias_d[row])
                        if 0 <= s < len(items):
                            kind, h = items[s]
                            qb, kb = (h // 2, 3 + h // 2) if kind == "mo" else (6 + h // 2, 12 + h // 2)
                            rows_ = slice(64 * (h % 2), 64 * (h % 2) + 64)
                            if kind == "mo":
                                nm, den = stat(2), stat(2)
                            else:
                                nm = nmd.rearrange("p (t h) -> p h t", t=2)[:, h, :]
                                den = dnd.rearrange("p (t h) -> p h t", t=2)[:, h, :]
                            line = blk["bias"][s % nb]
                            p, t3, t2 = softmax_probs((QK[rows_, qb, :], QK[rows_, kb, :]), 0.125, line.buf[:, :],
                                                      tl[s], [t_qk[qb], t_qk[kb]], tmp, nm, den, pr)
                            line.free = [t2]
                            probs[s] = (p, t3, den)
                        if 0 <= s - 2 < len(items):
                            p, t3, den = probs[s - 2]
                            pts[s - 2] = turn_probs(p, [t3], pr, pt)
                        if 0 <= s - 3 < len(items):
                            kind, h = items[s - 3]
                            q, tq = pts[s - 3]
                            if kind == "mo":
                                v = [V[:, t, 64 * h:64 * h + 64] for t in (0, 1)]
                                nv = [t_v[0, 0], t_v[0, 1]]
                            else:
                                v = [V[:, t, 384 + 64 * h:448 + 64 * h] for t in (0, 1)]
                                nv = [t_v[1 + h // 6, 0], t_v[1 + h // 6, 1]]
                            ps, t0 = values(q, tq, v, 64, pt, nv)
                            if kind == "mo":
                                res["mo"] = finish(Omo[:, :, 64 * h:64 * h + 64], probs[s - 3][2], 64)(
                                    ps, t0, [probs[s - 3][1]])
                            else:
                                t1 = CP(Odn[:, :, 64 * h:64 * h + 64],
                                        ps[:, 0:128].rearrange("p (t d) -> p t d", t=2), [t0])
                                aux.put(ps, [t1])
                                res["dn"] = [t1, probs[s - 3][1]]
                        yield
                    lg, ls = stat(24), stat(24)
                    a = A(lg, dnd, ACT.Ln, res["dn"])
                    b = TT(ls, lg, nmd, ALU.subtract, [a])
                    v4 = lambda ap: ap.rearrange("p (t g h) -> p t g h", t=2, g=3)
                    v4h = lambda ap: ap.rearrange("p (t g h) -> p t h g", t=2, g=3)
                    mx, sm_, e = stat(8), stat(8), stat(24)
                    c = RED(mx.rearrange("p (t h) -> p t h", t=2), v4h(ls), ALU.max, [b])
                    m3 = mx.rearrange("p (t h) -> p t h", t=2)
                    for g in range(3):
                        d = TT(v4(ls)[:, :, g, :], v4(ls)[:, :, g, :], m3, ALU.subtract, [c])
                    a = A(e, ls, ACT.Exp, [d])
                    b = RED(sm_.rearrange("p (t h) -> p t h", t=2), v4h(e), ALU.add, [a])
                    s3 = sm_.rearrange("p (t h) -> p t h", t=2)
                    for g in range(3):
                        c = TT(v4(ls)[:, :, g, :], v4(dnd)[:, :, g, :], s3, ALU.mult, [b])
                    d = RCP(lg, ls, [c])
                    w_ = stat(24)
                    d = TT(w_, e, lg, ALU.mult, [d])
                    yield
                    o4 = Odl[:, :, :].rearrange("p t (h d) -> p t h d", h=4)
                    for g in range(3):
                        n4 = Odn[:, :, 256 * g:256 * g + 256].rearrange("p t (h d) -> p t h d", h=4)
                        for t in (0, 1):
                            c = TT(n4[:, t], n4[:, t], bc(v4(w_)[:, t, g, :], 64), ALU.mult, [d, *res["dn"]])
                    s1 = TT(o4, Odn[:, :, 0:256].rearrange("p t (h d) -> p t h d", h=4),
                            Odn[:, :, 256:512].rearrange("p t (h d) -> p t h d", h=4), ALU.add, [c])
                    res["di"] = TT(o4, o4, Odn[:, :, 512:768].rearrange("p t (h d) -> p t h d", h=4), ALU.add, [s1])
                    yield

                fibers.append(heads())
                t_g = {}
                for c in range(6):
                    banks, need = two()
                    tok = gemm(("g1", l, c), xT, 8, [[(b[:, :], 0, 512)] for b in banks], need)
                    for t in (0, 1):
                        t_g[c, t] = A(G[:, t, 512 * c:512 * c + 512], banks[t][:, :], ACT.Copy, [tok])
                        mmb.put(banks[t], [t_g[c, t]])
                bg_drain()
                for t in (0, 1):
                    a = A(G[:, t, :], G[:, t, :], ACT.Sigmoid, [t_g[5, t]])
                    for c in range(6):
                        t_g[c, t] = a
                xT.free = [tok]
                srcs = [(Omla, "mla", 3), (Omo, "mo", 3), (Odl, "di", 2)]
                used = {}
                for r in (0, 1):
                    o, name, nk = srcs[r]
                    to_T([o[:, t, :] for t in (0, 1)], [res[name]], nk, oT[r])
                merged = [[], []]
                for r in range(3):
                    o, name, nk = srcs[r]
                    ot = oT[r % 2]
                    for n in (0, 1):
                        banks, need = two()
                        tok = gemm(("br1", l, r, n), ot, nk, [[(b[:, :], 0, 512)] for b in banks], need)
                        merge(XN, state["xn"], banks, tok, n, r == 0,
                              [G[:, t, 1024 * r + 512 * n:1024 * r + 512 * n + 512] for t in (0, 1)],
                              [t_g[2 * r + n, t] for t in (0, 1)], merged)
                    if r == 0:
                        ot.free = [tok]
                        to_T([Odl[:, t, :] for t in (0, 1)], [res["di"]], 2, oT[0])
                state["xn"] = [to_T(XN, merged[0] + merged[1], 8, xT)]
                for n in (0, 1):
                    banks, need = two()
                    tok = gemm(("o1", l, n), xT, 8, [[(b[:, :], 0, 512)] for b in banks], need)
                    for t in (0, 1):
                        xs = X[t][:, 512 * n:512 * n + 512]
                        a = TT(xs, xs, banks[t][:, :], ALU.add, [tok])
                        mmb.put(banks[t], [a])
                        state["x"][t] = [a]
                xT.free = [tok]

        def merge(dst, dfree, banks, tok, n, is_first, gates, t_gate, merged):
            for t in (0, 1):
                m = dst[t][:, 512 * n:512 * n + 512]
                if is_first:
                    a = TT(m, banks[t][:, :], gates[t], ALU.mult, [tok, t_gate[t], dfree])
                    mmb.put(banks[t], [a])
                else:
                    b = TT(gates[t], banks[t][:, :], gates[t], ALU.mult, [tok, t_gate[t]])
                    mmb.put(banks[t], [b])
                    a = TT(m, m, gates[t], ALU.add, [b, *merged[t]])
                merged[t] = merged[t] + [a]

        def two():
            (a, f), (b, g) = mmb.get(), mmb.get()
            return [a, b], f + g

        def one():
            a, f = mmb.get()
            return [a], f

        with ExitStack() as b1:
            blk = {}
            blk["rope"] = sbuf([128, 2, 64], F32, b1)
            blk["t_rope"] = once(blk["rope"][:, :, :], rope_d[:, :, 0:64], "s_rope1")
            blk["causal"] = sbuf([128, 384], F32, b1)
            blk["t_causal"] = once(blk["causal"][:, :], bias_d[18], "s_causal1")
            blk["bias"] = [Line(sem(f"s_bias{i}"), sbuf([128, 384], F32, b1)) for i in range(3)]
            for l in (0, 1):
                first(l, blk)

        b2 = ctx
        VR = [Line(sem(f"s_vr{i}"), sbuf([128, D], F32, b2)) for i in range(2)]
        vr_at = [0]

        def vrow(name):
            line = VR[vr_at[0] % 2]
            vr_at[0] += 1
            i = VROWS.index(name)
            fence = state["x"][0] + state["x"][1] if vr_at[0] <= 2 else []
            return line, load(line, line.buf[:, :], vrows[i:i + 1, :].broadcast_to([128, D]), fence)

        def final_norm():
            line, tl = vrow("final")
            for t in (0, 1):
                ss, ms = stat(1), stat(1)
                a = A(XN[t][:, :], X[t][:, :], ACT.Square, [*state["x"][t], state["xn"]], accum=ss)
                b = TS(ms, ss, 1.0 / D, 1e-6, ALU.mult, ALU.add, [a])
                r, c = rsqrt(ms, [b])
                e = STT(X[t][:, :], X[t][:, :], r, line.buf[:, :], ALU.mult, ALU.mult, [c, tl])
                line.free.append(e)
                state["x"][t] = [e]

        def plain_to():
            state["xp"] = [to_T(X, [state["x"][0], state["x"][1], t_id], 8, xT)]

        def layer_norm(g, b, need):
            lg, tg = vrow(g)
            lb, tb = vrow(b)
            for t in (0, 1):
                st_, mv = stat(12), stat(2)
                for n in (0, 1):
                    dve.need(*need[t])
                    a = dve.go(lambda e, n=n, t=t, st_=st_: e.bn_stats(st_[:, 6 * n:6 * n + 6],
                                                                     X[t][:, 512 * n:512 * n + 512]))
                dve.need(a)
                a = dve.go(lambda e, mv=mv, st_=st_: e.bn_aggr(mv, st_))
                ve = stat(1)
                c = TS(ve, mv[:, 1:2], 1e-5, None, ALU.add, need=[a])
                r, c = rsqrt(ve, [c])
                xs = X[t][:, :]
                a = TS(xs, xs, mv[:, 0:1], r, ALU.subtract, ALU.mult, [c])
                a = TT(xs, xs, lg.buf[:, :], ALU.mult, [a, tg])
                lg.free.append(a)
                a = TT(xs, xs, lb.buf[:, :], ALU.add, [a, tb])
                lb.free.append(a)
                state["x"][t] = [a]

        def ffn2(key, l, g, b):
            plain_to()
            with ExitStack() as ph:
                hT = XT(22, ph)
                sring = Pool([sbuf([128, 2, 256], F32, ph) for _ in range(2)])
                al = []
                for t in (0, 1):
                    al.append(TS(X[t][:, :], X[t][:, :], ALPHA, None, ALU.mult, need=[*state["x"][t], state["xp"]]))
                banks, tok = swiglu(key, l, hT, sring)
                need = [[], []]
                for t in (0, 1):
                    for n in (0, 1):
                        xs = X[t][:, 512 * n:512 * n + 512]
                        need[t].append(STT(xs, banks[2 * t + n][:, :], 0.5, xs, ALU.mult, ALU.add, [tok, al[t]]))
                        mmb.put(banks[2 * t + n], [need[t][-1]])
                layer_norm(g, b, need)

        def mixer2(l):
            lam_init = 0.8 - 0.6 * math.exp(-0.3 * l)
            plain_to()
            fence = state["x"][0] + state["x"][1]
            al = []
            for t in (0, 1):
                al.append(TS(X[t][:, :], X[t][:, :], ALPHA, None, ALU.mult, need=[*state["x"][t], state["xp"]]))
            with ExitStack() as ph:
                OA = sbuf([128, 2, 1024], F32, ph)
                OB = sbuf([128, 2, 1024], F32, ph)
                OC = XNB
                tmp = Pool([sbuf([128, 384], F32, ph) for _ in range(2)])
                pr = Pool([sbuf([128, 384], F32, ph) for _ in range(3)])
                pt = Pool([sbuf([128, 384], F32, ph) for _ in range(2)])
                rw = sbuf([128, 304], F32, ph)
                rw_line.buf = rw
                t_rw = load(rw_line, rw[:, :], rows[l:l + 1, :].broadcast_to([128, 304]), fence)
                rc = ph
                R1 = sbuf([128, 6144], F32, ph)
                QKA = R1[:, 0:4096].rearrange("p (a b) -> p a b", a=16)
                VAt = R1[:, 4096:6144].rearrange("p (a b) -> p a b", a=2)
                reg2 = ExitStack()
                Z = XN
                BC = sbuf([128, 4, 256], F32, reg2)
                XD = sbuf([128, 2, 1024], F32, reg2)
                AR = sbuf([128, 4, 256], F32, reg2)
                M = sbuf([128, 4, 384], F32, reg2)
                CB = sbuf([128, 2, 384], F32, reg2)
                cacc = Pool([sbuf([128, 256], F32, reg2) for _ in range(3)])
                ROT = Pool([sbuf([128, 512], F32, reg2) for _ in range(2)])
                rt = [sbuf([128, 128], F32, reg2) for _ in range(2)]
                dtt, dA = sbuf([128, 2, 16], F32, reg2), sbuf([128, 2, 16], F32, reg2)
                s16 = [sbuf([128, 32], F32, reg2) for _ in range(2)]
                arow = sbuf([16, 256], F32, reg2)
                acol = sbuf([128, 2, 16], F32, reg2)
                cadd = sbuf([128, 6, 16], F32, reg2)
                tk = {}

                def scalars():
                    d3 = s_lam[:, :].rearrange("p (a b) -> p a b", a=2)
                    l4 = rw[:, 0:256].rearrange("p (a c b) -> p a c b", a=2, c=2)
                    a = TT(d3, l4[:, :, 0, :], l4[:, :, 1, :], ALU.mult, [t_rw, fence])
                    sd = stat(2)
                    b = RED(sd, d3, ALU.add, [a])
                    es = stat(2)
                    c = A(es, sd, ACT.Exp, [b])
                    nl = stat(1)
                    TS(nl, es[:, 1:2], es[:, 0:1], -lam_init, ALU.subtract, ALU.add, [c])
                    tk["nlam"] = (dve.sem, dve.n)
                    gs = stat(1)
                    tk["gs"] = TS(gs, col("diff_subln_g_2", l, 1), 1.0 - lam_init, None, ALU.mult)
                    an = stat(16)
                    a = A(an, rw[:, 272:288], ACT.Exp, [t_rw])
                    tk["an"] = TS(an, an, -1.0, None, ALU.mult, need=[a])
                    return nl, gs, an

                nlam, gsub, aneg = scalars()

                b_, f = one()
                dtb = b_[0]
                tok = dt_gemm(l, dtb, f)

                def dts():
                    z, w = s16
                    for t in (0, 1):
                        a = TT(z[:, 16 * t:16 * t + 16], dtb[:, 16 * t:16 * t + 16], rw[:, 256:272], ALU.add,
                               [tok, t_rw])
                    mmb.put(dtb, [a])
                    yield
                    b = A(w[:, :], z[:, :], ACT.Abs, [a])
                    b = A(w[:, :], w[:, :], ACT.Exp, [b], scale=-1.0)
                    b = A(w[:, :], w[:, :], ACT.Ln, [b], bias=1.0)
                    d2 = dtt[:, :, :].rearrange("p t h -> p (t h)")
                    tk["dt"] = STT(d2, z[:, :], 0.0, w[:, :], ALU.max, ALU.add, [b])
                    c = TT(dA[:, :, :], dtt[:, :, :], bc1(aneg, 2), ALU.mult, [tk["dt"], tk["an"]])
                    yield
                    ps, free = aux.get()
                    pe.need(*free, c, t_u64)
                    for t in (0, 1):
                        a = mm(ps[0:16, 128 * t:128 * t + 128], dA[:, t, :], U64[:, :], True, True, t == 1)
                    a = A(arow[:, :], ps[0:16, 0:256], ACT.Copy, [a])
                    aux.put(ps, [a])
                    tk["arow"] = a
                    sp.need(a, scr_line.free)
                    scr_line.n += 1
                    sp.put(lambda e: e.dma_start(scratch[l], arow[:, :]).then_inc(scr_line.sem, 16))
                    tk["scr"] = (scr_line.sem, 16 * scr_line.n)
                    yield
                    ps, free = aux.get()
                    pe.need(*free, a)
                    for t in (0, 1):
                        b = tr(ps[:, 16 * t:16 * t + 16], arow[:, 128 * t:128 * t + 128], last=(t == 1))
                    c = CP(acol[:, :, :].rearrange("p t h -> p (t h)"), ps[:, 0:32], [b])
                    aux.put(ps, [c])
                    tk["acol"] = c

                f = dts()
                next(f)
                fibers.append(f)

                t_bc, t_xd, t_ob = [None] * 4, [None] * 4, [None] * 4

                def conv_tile(ct, src, prev):
                    acc, free = cacc.get()
                    w = colt[:, COLS[("ssm_conv_w_2", l)] + 4 * ct:COLS[("ssm_conv_w_2", l)] + 4 * ct + 4]
                    b = colt[:, COLS[("ssm_conv_b_2", l)] + ct:COLS[("ssm_conv_b_2", l)] + ct + 1]
                    a = A(acc[:, :], src, ACT.Identity, [tk["xbc"], *free, fence, prev], scale=w[:, 3:4], bias=b)
                    for s in (1, 2, 3):
                        a = STT(acc[:, s:256], src[:, 0:256 - s], w[:, 3 - s:4 - s], acc[:, s:256], ALU.mult, ALU.add,
                                [a])
                    return acc, a

                def xbc_chunk(c):
                    banks, need = two()
                    outs = [banks[m // 2][:, 256 * (m % 2):256 * (m % 2) + 256] for m in range(4)]
                    tk["xbc"] = gemm_w(("xbc", l, c), xT, 8, outs, need)

                    def post():
                        a = None
                        for m in range(4):
                            if c == 2:
                                acc, a = conv_tile(8 + m, outs[m], a)
                                t_bc[m] = A(BC[:, m, :], acc[:, :], ACT.Silu, [a])
                                cacc.put(acc, [t_bc[m]])
                                if m % 2:
                                    mmb.put(banks[m // 2], [a])
                                if m % 2:
                                    yield
                                continue
                            acc, a = conv_tile(4 * c + m, outs[m], a)
                            if m % 2:
                                mmb.put(banks[m // 2], [a])
                            b = A(acc[:, :], acc[:, :], ACT.Silu, [a])
                            ct = 4 * c + m
                            ps, free = aux.get()
                            pe.need(*free, b)
                            for t in (0, 1):
                                e = tr(ps[:, 128 * t:128 * t + 128], acc[:, 128 * t:128 * t + 128], last=(t == 1))
                            cacc.put(acc, [e])
                            for t in (0, 1):
                                p3 = ps[:, 128 * t:128 * t + 128].rearrange("p (h d) -> p h d", h=2)
                                o3 = OB[:, t, 128 * ct:128 * ct + 128].rearrange("p (h d) -> p h d", h=2)
                                x3 = XD[:, t, 128 * ct:128 * ct + 128].rearrange("p (h d) -> p h d", h=2)
                                TT(o3, p3, bc(rw[:, 288 + 2 * ct:290 + 2 * ct], 64), ALU.mult, [e, t_rw])
                                tk["xd"] = TT(x3, p3, bc(dtt[:, t, 2 * ct:2 * ct + 2], 64), ALU.mult, [tk["dt"]])
                            aux.put(ps, [tk["xd"]])
                            yield
                    f = post()
                    next(f)
                    fibers.append(f)

                for c in (2, 0, 1):
                    xbc_chunk(c)

                def z_post(banks, tok, n):
                    for t in (0, 1):
                        a = A(Z[t][:, 512 * n:512 * n + 512], banks[t][:, :], ACT.Silu, [tok, state["xn"]])
                        mmb.put(banks[t], [a])
                        tk["z", n, t] = a
                    yield

                def ssd():
                    for g in (0, 1):
                        ps, free = aux.get()
                        pe.need(*free, *t_bc)
                        mm(ps[:, 0:256], BC[:, g, 0:128], BC[:, 2 + g, 0:256], True, True)
                        a = mm(ps[:, 256:384], BC[:, g, 128:256], BC[:, 2 + g, 128:256], True, True, True)
                        tk["cb", g] = TT(CB[:, g, :], ps[:, 0:384], tri[:, :], ALU.mult, [a, t_tri])
                        aux.put(ps, [tk["cb", g]])
                        yield
                    halves = [range(4 * q, 4 * q + 4) for q in range(4)]
                    t_m = None
                    ypsum = {}
                    for q in range(4):
                        hs = slice(4 * q, 4 * q + 4)
                        g = q // 2
                        src = scratch[l, 4 * q:4 * q + 4, :].unsqueeze(0).broadcast_to([128, 4, 256])
                        ta = load(ar_line, AR[:, :, :], src, [tk["scr"]])
                        base = TS(cadd[:, 0, hs], acol[:, 0, hs], -1.0, None, ALU.mult, need=[tk["acol"]])
                        b4 = TS(cadd[:, 4, hs], acol[:, 1, hs], -1.0, None, ALU.mult)
                        CP(cadd[:, 1, hs], cadd[:, 0, hs], [base])
                        c5 = CP(cadd[:, 5, hs], cadd[:, 4, hs], [b4])
                        tot = lambda c: AR[:, :, 64 * c + 63]
                        lowp = slice(0, 64)
                        a = TT(cadd[lowp, 1, hs], cadd[lowp, 1, hs], AR[lowp, :, 63], ALU.add, [ta, c5])
                        a = TT(cadd[:, 2, hs], cadd[:, 1, hs], tot(1), ALU.add, [a])
                        a = TT(cadd[:, 3, hs], cadd[:, 2, hs], tot(2), ALU.add, [a])
                        a = TT(cadd[lowp, 5, hs], cadd[lowp, 5, hs], AR[lowp, :, 64 * 2 + 63], ALU.add, [a])
                        for k, tc in enumerate((0, 1, 2, 3, 2, 3)):
                            b = TT(M[:, :, 64 * k:64 * k + 64], AR[:, :, 64 * tc:64 * tc + 64],
                                   bc(cadd[:, k, hs], 64), ALU.add, [a, tk.get("mfree")])
                        ar_line.free = [b]
                        yield
                        mf = M[:, :, :].rearrange("p h c -> p (h c)")
                        a = TS(mf, mf, 0.0, None, ALU.min, need=[b])
                        a = A(mf, mf, ACT.Exp, [a])
                        yield
                        b = TT(M[:, :, :], M[:, :, :], bc1(CB[:, g, :], 4), ALU.mult, [a, tk["cb", g]])
                        yield
                        ps, free = aux.get()
                        pe.need(*free, b, tk["xd"])
                        for j in range(4):
                            h = 4 * q + j
                            c = slice(64 * h, 64 * h + 64)
                            mm(ps[:, 64 * j:64 * j + 64], M[:, j, 0:128], XD[:, 0, c], True, True)
                            mm(ps[:, 256 + 64 * j:320 + 64 * j], M[:, j, 128:256], XD[:, 0, c], True, False)
                            e = mm(ps[:, 256 + 64 * j:320 + 64 * j], M[:, j, 256:384], XD[:, 1, c], False, True, j == 3)
                        tk["mfree"] = e
                        for t in (0, 1):
                            o = OB[:, t, 256 * q:256 * q + 256]
                            a = TT(o, o, ps[:, 256 * t:256 * t + 256], ALU.add, [e, tk["xd"]])
                            tk["y", q, t] = TT(o, o, Z[t][:, 256 * q:256 * q + 256], ALU.mult, [a, tk["z", q // 2, t]])
                        aux.put(ps, [a])
                        yield
                    scr_line.free = [ta]
                    tk["ob"] = []
                    for t in (0, 1):
                        ss, ms = stat(2), stat(2)
                        for g in (0, 1):
                            o = OB[:, t, 512 * g:512 * g + 512]
                            a = A(Z[t][:, 512 * g:512 * g + 512], o, ACT.Square, [tk["y", 2 * g, t], tk["y", 2 * g + 1, t]],
                                  accum=ss[:, g:g + 1])
                        b = TS(ms, ss, 1.0 / 512, 1e-5, ALU.mult, ALU.add, [a])
                        r, c = rsqrt(ms, [b])
                        for g in (0, 1):
                            o = OB[:, t, 512 * g:512 * g + 512]
                            tk["ob"].append(TS(o, o, r[:, g:g + 1], None, ALU.mult, need=[c]))
                    tk["zfree"] = tk["ob"]
                    yield

                for n in (0, 1):
                    banks, need = two()
                    tok = gemm(("z", l, n), xT, 8, [[(b[:, :], 0, 512)] for b in banks], need)
                    for _ in z_post(banks, tok, n):
                        pass
                bg_drain()
                fibers.append(ssd())

                def rope_chunk(name, n, base):
                    banks, need = two()
                    tok = gemm((name, l, n), xT, 8, [[(b[:, :], 0, 512)] for b in banks], need)

                    def post():
                        done, bufs = [], []
                        for t in (0, 1):
                            buf, free = ROT.get()
                            a = A(buf[:, :], banks[t][:, :], ACT.Copy, [tok, *free])
                            p3 = banks[t][:, :].rearrange("p (h d) -> p h d", h=8)[:, :, 0:16]
                            d3 = buf[:, :].rearrange("p (h d) -> p h d", h=8)
                            a3 = rt[0][:, :].rearrange("p (h d) -> p h d", h=8)
                            b3 = rt[1][:, :].rearrange("p (h d) -> p h d", h=8)
                            TT(a3, p3, bc1(rope2[:, t, 0:16], 8), ALU.mult, [tok, t_rope2, a, tk.get("rt")])
                            b = TT(b3, p3, bc1(rope2[:, t, 16:32], 8), ALU.mult)
                            mmb.put(banks[t], [b])
                            TT(d3[:, :, 0:8], a3[:, :, 0:8], b3[:, :, 8:16], ALU.subtract, [b])
                            tk["rt"] = TT(d3[:, :, 8:16], a3[:, :, 8:16], b3[:, :, 0:8], ALU.add)
                            done.append(tk["rt"])
                            bufs.append(buf)
                        yield
                        for k in (0, 2):
                            ps, free = aux.get()
                            pe.need(*free, *done)
                            for j in (0, 1):
                                for t in (0, 1):
                                    a = tr(ps[:, 256 * j + 128 * t:256 * j + 128 * t + 128],
                                           bufs[t][:, 128 * (k + j):128 * (k + j) + 128], last=(j == 1 and t == 1))
                            hh = base + 4 * n + k
                            b = A(QKA[:, hh:hh + 2, :].rearrange("p a b -> p (a b)"), ps[:, :], ACT.Copy, [a])
                            aux.put(ps, [b])
                            tk["qka", hh] = tk["qka", hh + 1] = b
                        for t in (0, 1):
                            ROT.put(bufs[t], [a])
                    f = post()
                    next(f)
                    fibers.append(f)

                for n in (0, 1):
                    rope_chunk("qa", n, 0)
                for n in (0, 1):
                    rope_chunk("ka", n, 8)

                def v_chunk(name, n, dst):
                    banks, need = two()
                    tok = gemm((name, l, n), xT, 8, [[(b[:, :], 0, 512)] for b in banks], need)
                    for t in (0, 1):
                        o = dst[:, t, 512 * n:512 * n + 512]
                        a = A(o, banks[t][:, :], ACT.Copy, [tok]) if t else CP(o, banks[t][:, :], [tok])
                        mmb.put(banks[t], [a])
                        tk[name, n, t] = a

                for n in (0, 1):
                    v_chunk("va", n, VAt)
                bg_drain()
                fence2 = [*tk["ob"], tk["mfree"]]
                reg2.close()
                reg3 = ExitStack()
                QKC = sbuf([128, 16, 256], F32, reg3)
                VCt = sbuf([128, 2, 1024], F32, reg3)

                def heads_a():
                    st, w_, pts = {}, {}, {}
                    for s in range(16 + 5):
                        if s >= 5 and s % 2 == 1 and (s - 5) // 2 < 8:
                            h = (s - 5) // 2
                            q, tq = pts[h]
                            v = [VAt[:, t, 128 * h:128 * h + 128] for t in (0, 1)]
                            ps, t0 = values(q, tq, v, 128, pt, [tk["va", h // 4, 0], tk["va", h // 4, 1]])
                            ss, ms = stat(2), stat(2)
                            jb, jf = tmp.get()
                            for t in (0, 1):
                                a = A(jb[:, 128 * t:128 * t + 128], ps[:, 128 * t:128 * t + 128], ACT.Square,
                                      [t0, *jf], accum=ss[:, t:t + 1])
                            tmp.put(jb, [a])
                            b = TS(ms, ss, 1.0 / 128, 1e-5, ALU.mult, ALU.add, [a])
                            r, c = rsqrt(ms, [b])
                            o3 = OA[:, :, 128 * h:128 * h + 128]
                            tk["oa"] = TT(o3, ps[:, 0:256].rearrange("p (t d) -> p t d", t=2), bc(r, 128), ALU.mult,
                                          [c])
                            aux.put(ps, [tk["oa"]])
                        if s >= 4 and s % 2 == 0 and s // 2 - 2 < 8:
                            h = s // 2 - 2
                            pts[h] = turn_probs(w_[h][0], [w_[h][1]], pr, pt)
                        if s >= 2 and s % 2 == 0 and s // 2 - 1 < 8:
                            h = s // 2 - 1
                            p0, ta, d0 = st[2 * h]
                            p1, tb, d1 = st[2 * h + 1]
                            r = stat(4)
                            RCP(r[:, 0:2], d0, [ta])
                            a = RCP(r[:, 2:4], d1, [tb])
                            b = TS(r[:, 2:4], r[:, 2:4], nlam, None, ALU.mult, need=[a, tk["nlam"]])
                            sl = [slice(0, 128), slice(128, 384)]
                            for t in (0, 1):
                                a = TS(p0[:, sl[t]], p0[:, sl[t]], r[:, t:t + 1], None, ALU.mult, need=[b])
                            for t in (0, 1):
                                a = STT(p0[:, sl[t]], p1[:, sl[t]], r[:, 2 + t:3 + t], p0[:, sl[t]], ALU.mult, ALU.add,
                                        [(dve.sem, dve.n - 1)])
                            pr.put(p1, [a])
                            w_[h] = (p0, a)
                        if s < 16:
                            h, m = s // 2, s % 2
                            rr = slice(64 * m, 64 * m + 64)
                            nm, den = stat(2), stat(2)
                            p, t3, _ = softmax_probs((QKA[rr, h, :], QKA[rr, 8 + h, :]), 0.125, chunk[:, :], t_chunk,
                                                     [tk["qka", h], tk["qka", 8 + h]], tmp, nm, den, pr)
                            st[s] = (p, t3, den)
                        yield

                fibers.append(heads_a())

                def qkc_chunk(name, n, base):
                    banks, need = two()
                    outs = [banks[m // 2][:, 256 * (m % 2):256 * (m % 2) + 256] for m in range(4)]
                    tok = gemm_w((name, l, n), xT, 8, outs, need)
                    for j in (0, 1):
                        hh = base + 4 * n + 2 * j
                        o = QKC[:, hh:hh + 2, :].rearrange("p a b -> p (a b)")
                        a = (A(o, banks[j][:, :], ACT.Copy, [tok, *fence2]) if j
                             else CP(o, banks[j][:, :], [tok, *fence2]))
                        mmb.put(banks[j], [a])
                        tk["qkc", hh] = tk["qkc", hh + 1] = a

                for n in (0, 1):
                    qkc_chunk("qc", n, 0)
                for n in (0, 1):
                    qkc_chunk("kc", n, 8)
                for n in (0, 1):
                    v_chunk("vc", n, VCt)
                bg_drain()
                fence3 = [tk["oa"]]
                G = R1[:, :].rearrange("p (a b) -> p a b", a=2)

                def heads_c():
                    arg, pts = {}, {}
                    st1 = {}
                    for s in range(16 + 5):
                        if 0 <= s - 4 < 16:
                            h = s - 4
                            q, tq = pts[h]
                            v = [VCt[:, t, 64 * h:64 * h + 64] for t in (0, 1)]
                            ps, t0 = values(q, tq, v, 64, pt, [tk["vc", h // 8, 0], tk["vc", h // 8, 1]])
                            tk["oc"] = CP(OC[:, :, 64 * h:64 * h + 64],
                                          ps[:, 0:128].rearrange("p (t d) -> p t d", t=2), [t0, *fence2])
                            aux.put(ps, [tk["oc"]])
                        if 0 <= s - 3 < 16:
                            w, c = arg[s - 3]
                            pts[s - 3] = turn_probs(w, [c], pr, pt)
                        if 0 <= s - 1 < 16:
                            z, w, a = st1[s - 1]
                            a = STT(w[:, :], z[:, :], 0.0, w[:, :], ALU.max, ALU.add, [a])
                            dve.need(a)
                            for t, (lo_, n_) in enumerate(((0, 128), (128, 256))):
                                wv = w[:, lo_:lo_ + n_][:, ::-1]
                                cv = wv
                                dve.need(t_zero)
                                b = dve.go(lambda e, wv=wv, cv=cv, n_=n_: e.tensor_tensor_scan(
                                    cv, wv, zero[:, 0:n_], 0.0, ALU.add, ALU.add))
                            b = TT(z[:, :], z[:, :], w[:, :], ALU.subtract, [b])
                            c = A(w[:, :], z[:, :], ACT.Exp, [b])
                            tmp.put(z, [c])
                            arg[s - 1] = (w, c)
                        if s < 16:
                            rr = slice(64 * (s % 2), 64 * (s % 2) + 64)
                            b = s // 2
                            ps, free = aux.get()
                            pe.need(*free, tk["qkc", b], tk["qkc", 8 + b])
                            qT, kT = QKC[rr, b, :], QKC[rr, 8 + b, :]
                            mm(ps[:, 0:128], qT[:, 0:128], kT[:, 0:128], True, True)
                            t0 = mm(ps[:, 128:384], qT[:, 128:256], kT[:, 0:256], True, True, True)
                            z, f2 = tmp.get()
                            t1 = STT(z[:, :], ps[:, 0:384], 0.125, strict[:, :], ALU.mult, ALU.add, [t0, t_strict, *f2])
                            aux.put(ps, [t1])
                            w, f3 = pr.get()
                            a = A(w[:, :], z[:, :], ACT.Abs, [t1, *f3])
                            a = A(w[:, :], w[:, :], ACT.Exp, [a], scale=-1.0)
                            a = A(w[:, :], w[:, :], ACT.Ln, [a], bias=1.0)
                            st1[s] = (z, w, a)
                        yield

                oT = XT(8, reg3)
                oT.free = fence2
                fibers.append(heads_c())
                t_g = {}
                for c in range(6):
                    if c % 2 == 0:
                        line, tl = vrow((l, f"gb{c // 2}"))
                    banks, need = two()
                    tok = gemm(("g2", l, c), xT, 8, [[(b[:, :], 0, 512)] for b in banks], need)
                    for t in (0, 1):
                        g = G[:, t, 512 * c:512 * c + 512]
                        t_g[c, t] = TT(g, banks[t][:, :], line.buf[:, 512 * (c % 2):512 * (c % 2) + 512], ALU.add,
                                       [tok, tl, *fence3])
                        mmb.put(banks[t], [t_g[c, t]])
                    if c % 2:
                        line.free = [t_g[c, 0], t_g[c, 1]]
                    if c == 3:
                        t_ob2 = to_T([OB[:, t, :] for t in (0, 1)], tk["ob"], 8, oT, col("ssm_norm_g_2", l, 8))
                bg_drain()
                xT.free = [tok]
                for t in (0, 1):
                    a = A(G[:, t, :], G[:, t, :], ACT.Sigmoid, [t_g[5, t]])
                    for c in range(6):
                        t_g[c, t] = a
                merged = [[], []]
                dm = [OB[:, t, :] for t in (0, 1)]
                order = (1, 0, 2)
                ga = gsub.broadcast_to([128, 8])
                to_T([OA[:, t, :] for t in (0, 1)], [tk["oa"], tk["gs"]], 8, xT, ga)
                for i, r in enumerate(order):
                    ot = (oT, xT, oT)[i]
                    for n in (0, 1):
                        banks, need = two()
                        tok = gemm(("br2", l, r, n), ot, 8, [[(b[:, :], 0, 512)] for b in banks], need)
                        merge(dm, t_ob2, banks, tok, n, i == 0,
                              [G[:, t, 1024 * r + 512 * n:1024 * r + 512 * n + 512] for t in (0, 1)],
                              [t_g[2 * r + n, t] for t in (0, 1)], merged)
                    ot.free = [tok]
                    if i == 0:
                        state["xn"] = [to_T([OC[:, t, :] for t in (0, 1)], [tk["oc"]], 8, oT)]
                to_T(dm, merged[0] + merged[1], 8, xT)
                need2 = [[], []]
                for n in (0, 1):
                    banks, need = two()
                    tok = gemm(("o2", l, n), xT, 8, [[(b[:, :], 0, 512)] for b in banks], need)
                    for t in (0, 1):
                        xs = X[t][:, 512 * n:512 * n + 512]
                        a = TT(xs, xs, banks[t][:, :], ALU.add, [tok, al[t]])
                        mmb.put(banks[t], [a])
                        need2[t].append(a)
                xT.free = [tok]
                layer_norm((l, "ln2_g"), (l, "ln2_b"), need2)
                reg3.close()
                rw_line.free = [tok]

        def dt_gemm(l, ps, need):
            pe.need(*need)
            key = ("dt", l)
            hi, lo, w, kts, ready = S.take(key)
            assert len(kts) == 8
            pe.need(*ready)
            for t in (0, 1):
                for kt in kts:
                    pe.need(xT.tok[kt])
                    o = kt * w
                    for n, (xs, ws) in enumerate(((xT.H, hi), (xT.H, lo), (xT.L, hi))):
                        tok = mm(ps[:, 16 * t:16 * t + 16], xs[:, kt, 128 * t:128 * t + 128], ws[:, o:o + w],
                                 kt == 0 and n == 0, kt == 7 and n == 2, kt == 7 and n == 2)
            S.done(tok)
            return tok

        fence_b2 = state["x"][0] + state["x"][1]

        def once2(out, in_, name):
            sp.need(*fence_b2)
            return once(out, in_, name)

        U64 = sbuf([128, 128], F32, b2)
        t_u64 = once2(U64[:, :], msk_d[:, 384:512], "s_u64")
        tri = sbuf([128, 384], F32, b2)
        t_tri = once2(tri[:, :], msk_d[:, 0:384], "s_tri")
        strict = sbuf([128, 384], F32, b2)
        t_strict = once2(strict[:, :], bias_d[19], "s_strict")
        chunk = sbuf([128, 384], F32, b2)
        t_chunk = once2(chunk[:, :], bias_d[20], "s_chunk")
        rope2 = sbuf([128, 2, 32], F32, b2)
        t_rope2 = once2(rope2[:, :, :], rope_d[:, :, 64:96], "s_rope2")
        zero = sbuf([128, 256], F32, b2)
        dve.need(fence_b2)
        t_zero = dve.go(lambda e: e.memset(zero[:, :], 0.0))
        s_lam = sbuf([128, 128], F32, b2)
        rw_line, ar_line, scr_line = Line(sem("s_rw"), None), Line(sem("s_ar"), None), Line(sem("s_scr"), None)

        final_norm()
        for l in (0, 1):
            ffn2("F1", l, (l, "ln1_g"), (l, "ln1_b"))
            mixer2(l)
            ffn2("F2", l, (l, "ln3_g"), (l, "ln3_b"))

        s_out = sem("s_out")
        for t in (0, 1):
            sp.need(*state["x"][t])
            sp.put(lambda e, t=t: e.dma_start(out[0, 128 * t:128 * t + 128, :], X[t][:, :]).then_inc(s_out, 16))
        sp.need((s_out, 32), (scr_line.sem, 16 * scr_line.n))
        assert S.u == len(pieces)

        block = ctx.enter_context(nc.Block())
        block.sync(sp.run)
        block.scalar(act.run)
        block.vector(dve.run)
        block.gpsimd(pool.run)
        block.tensor(pe.run)


def constants():
    f = np.float32
    q = np.arange(128)[:, None]
    k = np.arange(128)[None, :]

    def three(fn):
        return np.concatenate([fn(q, k), fn(q + 128, k), fn(q + 128, k + 128)], axis=1)

    slopes = (f(2.0) ** (f(-8.0) * np.arange(1, 19, dtype=f) / f(18))).astype(f)
    bias = np.zeros((21, 128, 384), f)
    for h in range(18):
        if h < 4:
            ok = lambda a, b: (a >= b) & (a - b <= 128)
        elif h < 12:
            dil = 4 if h < 8 else 16
            ok = lambda a, b, dil=dil: (a >= b) & ((a - b) % dil == 0)
        else:
            ok = lambda a, b: a >= b
        bias[h] = three(lambda a, b: np.where(ok(a, b), -slopes[h] * (a - b).astype(f), f(NEG)).astype(f))
    bias[18] = three(lambda a, b: np.where(a >= b, f(0), f(NEG)))
    bias[19] = three(lambda a, b: np.where(a > b, f(0), f(NEG)))
    bias[20] = three(lambda a, b: np.where(b // 64 <= a // 64, f(0), f(NEG)))
    msk = np.zeros((128, 512), f)
    msk[:, 0:128] = (k >= q)
    msk[:, 128:256] = 1.0
    msk[:, 256:384] = (k >= q)
    msk[:, 384:512] = (k >= q) & (k // 64 == q // 64)
    pos = np.arange(256, dtype=f)
    inv1 = f(10000.0) ** (-np.arange(0, 32, 2, dtype=f) / f(32))
    a1 = (pos[:, None] * inv1[None, :]).astype(f)
    inv2 = f(500000.0) ** (-np.arange(8, dtype=f) * f(2.0) / f(16))
    a2 = (pos[:, None] * inv2[None, :]).astype(f)
    c1, s1, c2, s2 = np.cos(a1), np.sin(a1), np.cos(a2), np.sin(a2)
    rope = np.concatenate([c1, c1, s1, s1, c2, c2, s2, s2], axis=1).astype(f)
    rope = np.ascontiguousarray(rope.reshape(2, 128, 96).transpose(1, 0, 2))
    return np.eye(128, dtype=f), bias, msk, rope


def kernel(**inputs):
    import numpy as _np
    import concourse.bacc as _bacc
    from concourse import mybir as _mybir
    from concourse.bass_utils import run_bass_kernel_spmd as _run

    a = {k: _np.ascontiguousarray(v) for k, v in inputs.items()}
    blocks = place_pieces()
    pieces = plan()
    total = sum(128 * used for _, used in blocks)
    wpack = _np.empty(total, _np.float32)
    at = 0
    for ps, used in blocks:
        dst = wpack[at:at + 128 * used].reshape(128, used)
        at += 128 * used
        for i, off, n in ps:
            _, width, kts = pieces[i]
            for idx, kt, ranges in kts:
                for name, c0, c1 in ranges:
                    dst[:, off:off + c1 - c0] = a[name][idx][128 * kt:128 * kt + 128, c0:c1]
                    off += c1 - c0
    cols = _np.empty((128, NCOLS), _np.float32)
    for name, l, c, n in _COLS:
        v = a[name][l]
        if name == "ssm_conv_w_2":
            cols[:, c:c + n] = v.reshape(4, 12, 128).transpose(2, 1, 0).reshape(128, 48)
        else:
            cols[:, c:c + n] = v.reshape(n, 128).T
    rows = _np.concatenate([a["diff_lambda_2"].reshape(2, 256), a["ssm_dt_bias_2"], a["ssm_A_log_2"], a["ssm_D_2"]],
                           axis=1)
    vr = [a["final_norm"]]
    for l in (0, 1):
        vr += [a["ln1_g_2"][l], a["ln1_b_2"][l], a["gate_bias_2"][l, 0], a["gate_bias_2"][l, 1],
               a["gate_bias_2"][l, 2], a["ln2_g_2"][l], a["ln2_b_2"][l], a["ln3_g_2"][l], a["ln3_b_2"][l]]
    ident, bias, msk, rope = constants()
    arrays = {"in_x": a["x"], "in_w": wpack, "in_cols": cols, "in_rows": _np.ascontiguousarray(rows),
              "in_vrows": _np.stack(vr), "in_ident": ident, "in_bias": bias, "in_msk": msk, "in_rope": rope}
    nc = _bacc.Bacc("TRN2", target_bir_lowering=False, num_devices=1)
    args = [nc.dram_tensor(k, v.shape, _mybir.dt.from_np(v.dtype), kind="ExternalInput").ap()
            for k, v in arrays.items()]
    scratch = nc.dram_tensor("scratch", (2, 16, 256), _mybir.dt.float32, kind="Internal").ap()
    out = nc.dram_tensor("out_0", (1, 256, 1024), _mybir.dt.float32, kind="ExternalOutput").ap()
    bass_two_blocks(nc, *args, scratch, out)
    r = _run(nc, [arrays], core_ids=[0])
    return r.results[0]["out_0"]
```

```python
import math
from collections import deque
from contextlib import ExitStack

import numpy as np

import concourse.bass as bass
from concourse import mybir

F32 = mybir.dt.float32
F32R = mybir.dt.float32r
ACT = mybir.ActivationFunctionType
ALU = mybir.AluOpType
AX_X = mybir.AxisListType.X

D = 1024
DFF = 2816
NCH = DFF // 256
NEG = -1e30
PIECE = 1024
BLOCK = 2048
NRAW = 3
NHL = 5
SKEW = 4
N_IN1 = 6944
MIX2 = 11792
QA, KA, VA, ZB, XBC, DTB, QC, KC, VC, GP = (0, 1024, 2048, 3072, 4096, 5632, 5648, 6672, 7696, 8720)
ALPHA = 4.0 ** 0.25
SLOPES = [2.0 ** (-8.0 * i / 18) for i in range(1, 19)]


def plan():
    pieces = []

    def gemm(key, idx, nk, ranges):
        width = sum(c1 - c0 for _, c0, c1 in ranges)
        per = PIECE // width
        for k in range(0, nk, per):
            pieces.append((key, width, [(idx, kt, ranges) for kt in range(k, min(nk, k + per))]))

    def ffn(key, l, gate, up, shift, down):
        for c in range(NCH):
            gemm((key, "up", l, c), (l,), 8,
                 [(gate, 256 * c, 256 * c + 256), (up, shift + 256 * c, shift + 256 * c + 256)])
        gemm((key, "down", l), (l,), 22, [(down, 0, 1024)])

    for l in (0, 1):
        ffn("f1", l, "ffn1_w_gate", "ffn1_w_up", 0, "ffn1_w_down")
        gemm(("mla", l), (l,), 8, [("w_in", 0, 416)])
        mo, di = 416, 416 + 1152
        for c in range(4):
            gemm(("qk1", l, c), (l,), 8, QK1[c])
            if c == 0:
                for j in (0, 1):
                    gemm(("uq", l, j), (l,), 2, [("w_uq", 288 * j, 288 * j + 288)])
                for j in (0, 1):
                    gemm(("ukv", l, j), (l,), 1, [("w_ukv", 384 * j, 384 * j + 384)])
        gemm(("v1", l, 0), (l,), 8, [("w_in", mo + 768, mo + 1152)])
        gemm(("qk1", l, 4), (l,), 8, QK1[4])
        for j in (0, 1):
            gemm(("v1", l, 1 + j), (l,), 8, [("w_in", di + 1536 + 384 * j, di + 1920 + 384 * j)])
        for c in range(6):
            gemm(("g1", l, c), (l,), 8, [("w_in", 3872 + 512 * c, 4384 + 512 * c)])
        for r, name, nk in BR1:
            for n in (0, 1):
                gemm(("br1", l, r, n), (l,), nk, [(name, 512 * n, 512 * n + 512)])
        for n in (0, 1):
            gemm(("o1", l, n), (l,), 8, [("w_out", 512 * n, 512 * n + 512)])
        ffn("f2", l, "ffn2_w_gate", "ffn2_w_up", 0, "ffn2_w_down")
    for l in (0, 1):
        ffn("F1", l, "ffn1_w_in_2", "ffn1_w_in_2", DFF, "ffn1_w_out_2")
        w = "w_mix_in_2"
        for n in (0, 1):
            gemm(("z", l, n), (l,), 8, [(w, ZB + 512 * n, ZB + 512 * n + 512)])
        gemm(("dt", l), (l,), 8, [(w, DTB, DTB + 16)])
        for c in (2, 0, 1):
            gemm(("xbc", l, c), (l,), 8, [(w, XBC + 512 * c, XBC + 512 * c + 512)])
        for key, at in (("qa", QA), ("ka", KA), ("va", VA), ("qc", QC), ("kc", KC), ("vc", VC)):
            for n in (0, 1):
                gemm((key, l, n), (l,), 8, [(w, at + 512 * n, at + 512 * n + 512)])
        for c in range(6):
            gemm(("g2", l, c), (l,), 8, [(w, GP + 512 * c, GP + 512 * c + 512)])
        for r in (1, 0, 2):
            for n in (0, 1):
                gemm(("br2", l, r, n), (l, r), 8, [("w_branch_2", 512 * n, 512 * n + 512)])
        for n in (0, 1):
            gemm(("o2", l, n), (l,), 8, [("w_mix_out_2", 512 * n, 512 * n + 512)])
        ffn("F2", l, "ffn2_w_in_2", "ffn2_w_in_2", DFF, "ffn2_w_out_2")
    return pieces


BR1 = [(0, "w_br_mla", 3), (2, "w_br_dil", 2), (1, "w_br_moba", 3)]
_Q = [("w_in", 416 + 128 * i) for i in range(6)] + [("w_in", 1568 + 128 * i) for i in range(12)]
QK1 = [[(n, c, c + 128) for n, c in _Q[4 * i:4 * i + 4]] for i in range(5)]

COLS = {}
ROWS = {"lam": (0, 256), "dtb": (256, 272), "alog": (272, 288), "dsk": (288, 304)}


def cols_plan():
    out, at = [], 0
    for l in (0, 1):
        for name, n in (("ffn1_norm", 8), ("mix_norm", 8), ("q_norm", 2), ("kv_norm", 1), ("ffn2_norm", 8),
                        ("diff_subln_g_2", 1), ("ssm_norm_g_2", 8), ("ssm_conv_w_2", 48), ("ssm_conv_b_2", 12)):
            out.append((name, l, at, n))
            COLS[(name, l)] = at
            at += n
    return out, at


_COLS, NCOLS = cols_plan()
VROWS = ["final"] + [(l, n) for l in (0, 1) for n in
                     ("ln1_g", "ln1_b", "gb0", "gb1", "gb2", "ln2_g", "ln2_b", "ln3_g", "ln3_b")]


def place_pieces():
    blocks, cur, used = [], [], 0
    for i, (key, width, kts) in enumerate(plan()):
        n = width * len(kts)
        if used + n > BLOCK:
            blocks.append((cur, used))
            cur, used = [], 0
        cur.append((i, used, n))
        used += n
    blocks.append((cur, used))
    return blocks


class Engine:
    def __init__(self, sem):
        self.sem, self.queue, self.n, self.met = sem, [], 0, {}

    def need(self, *tokens):
        for t in tokens:
            if t is None:
                continue
            if isinstance(t, (list, deque)):
                self.need(*t)
                continue
            sem, v = t
            if self.met.get(id(sem), 0) < v:
                self.met[id(sem)] = v
                self.queue.append(lambda e, sem=sem, v=v: e.wait_ge(sem, v))

    def go(self, fn):
        self.n += 1
        self.queue.append(lambda e, fn=fn: fn(e).then_inc(self.sem, 1))
        return (self.sem, self.n)

    def put(self, fn):
        self.queue.append(fn)

    def run(self, e):
        for fn in self.queue:
            fn(e)


class Pool:

    def __init__(self, bufs):
        self.free = deque((b, []) for b in bufs)

    def get(self):
        return self.free.popleft()

    def put(self, buf, tokens):
        self.free.append((buf, list(tokens)))


class Line:

    def __init__(self, sem, buf):
        self.sem, self.buf, self.n, self.free = sem, buf, 0, []


def bass_two_blocks(nc: bass.Bass, x, wpack, cols, rows, vrows, ident_d, bias_d, msk_d, rope_d, scratch, out):
    ctx = ExitStack()
    with ctx:
        counter = [0]

        def sbuf(shape, dt=F32, scope=ctx):
            counter[0] += 1
            return scope.enter_context(nc.sbuf_tensor(f"t{counter[0]}", shape, dt))

        def sem(name):
            return ctx.enter_context(nc.semaphore(name))

        pe, act, dve, pool = (Engine(sem(n)) for n in ("s_pe", "s_act", "s_dve", "s_pool"))
        sp = Engine(sem("s_sp"))
        psum = [ctx.enter_context(nc.psum_tensor(f"ps{i}", [128, 512], F32)) for i in range(8)]
        mmb, aux = Pool(psum[0:4]), Pool(psum[4:8])

        RAW = [sbuf([128, BLOCK]) for _ in range(NRAW)]
        HI = [sbuf([128, PIECE], F32R) for _ in range(NHL)]
        LO = [sbuf([128, PIECE], F32R) for _ in range(NHL)]
        X = [sbuf([128, D])[:, :] for _ in range(2)]
        XNB = sbuf([128, 2, D])
        XN = [XNB[:, t, :] for t in (0, 1)]
        ident = sbuf([128, 128])
        colt = sbuf([128, NCOLS])
        STAT = sbuf([128, 512])
        stat_at = [0]

        def stat(n):
            if stat_at[0] + n > 512:
                stat_at[0] = 0
            a = STAT[:, stat_at[0]:stat_at[0] + n]
            stat_at[0] += n
            return a

        class XT:
            def __init__(self, nk, scope=ctx):
                self.H = sbuf([128, nk, 256], F32R, scope)
                self.L = sbuf([128, nk, 256], F32R, scope)
                self.tok = [[None, None] for _ in range(nk)]
                self.free = []

        xT = XT(8)
        phalf = sbuf([128, 2])
        t_half = pool.go(lambda e: e.memset(phalf[:, :], -0.5))

        def A(out, in_, func, need=(), scale=1.0, bias=None, accum=None):
            act.need(*need)
            kw = {}
            if bias is not None:
                kw["bias"] = bias
            if accum is not None:
                kw["accum_out"] = accum
            return act.go(lambda e: e.activation(out, in_, func, scale=scale, **kw))

        def TT(out, a, b, op, need=(), eng=None):
            g = eng or dve
            g.need(*need)
            return g.go(lambda e: e.tensor_tensor(out, a, b, op))

        def TS(out, a, s1, s2, op0, op1=None, need=()):
            dve.need(*need)
            if op1 is None:
                return dve.go(lambda e: e.tensor_scalar(out, a, s1, None, op0))
            return dve.go(lambda e: e.tensor_scalar(out, a, s1, s2, op0, op1))

        def STT(out, a, s, b, op0, op1, need=()):
            dve.need(*need)
            return dve.go(lambda e: e.scalar_tensor_tensor(out=out, in0=a, scalar=s, in1=b, op0=op0, op1=op1))

        def RED(out, a, op, need=(), negate=None):
            dve.need(*need)
            return dve.go(lambda e: e.tensor_reduce(out, a, AX_X, op, negate=negate))

        def RCP(out, a, need=()):
            dve.need(*need)
            return dve.go(lambda e: e.reciprocal(out, a))

        def CP(out, a, need=()):
            dve.need(*need)
            return dve.go(lambda e: e.tensor_copy(out, a))

        def mm(out, l, r, start, stop, last=False, skip=False):
            fn = lambda e: e.matmul(out, l, r, start=start, stop=stop, skip_group_check=skip)
            return pe.go(fn) if last else pe.put(fn)

        def tr(out, in_, last=False):
            k = in_.shape[0]
            fn = lambda e: e.transpose(out, in_, ident[0:k, 0:k])
            return pe.go(fn) if last else pe.put(fn)

        def rsqrt(var, need):
            n = var.shape[-1]
            r = stat(n)
            pool.need(t_half, *need)
            return r, pool.go(lambda e: e.tensor_tensor(r, var, phalf[:, 0:n], ALU.pow))

        def bc(ap, n):
            return ap.unsqueeze(2).broadcast_to([ap.shape[0], ap.shape[1], n])

        def bc1(ap, n):
            return ap.unsqueeze(1).broadcast_to([ap.shape[0], n, ap.shape[1]])

        def once(out, in_, name):
            s = sem(name)
            sp.put(lambda e: e.dma_start(out, in_).then_inc(s, 16))
            return (s, 16)

        def load(line, out, in_, need=()):
            sp.need(*line.free, *need)
            line.free = []
            line.n += 1
            sp.put(lambda e: e.dma_start(out, in_).then_inc(line.sem, 16))
            return (line.sem, 16 * line.n)

        pieces = plan()
        blocks = place_pieces()
        dsem = [sem(f"s_w{i}") for i in range(NRAW)]
        where = {}
        offs, at = [], 0
        for b, (ps, used) in enumerate(blocks):
            offs.append(at)
            at += 128 * used
            for i, off, n in ps:
                where[i] = (b, off, n)

        class Stream:
            u = 0
            loaded = 0
            split = [0, 0]
            t_raw = {}
            t_hi = {}
            t_lo = {}
            t_pe = {}

            def load(self):
                b = self.loaded
                if b >= len(blocks):
                    return
                if b >= NRAW:
                    last = blocks[b - NRAW][0][-1][0]
                    if last not in self.t_lo:
                        return
                    sp.need(self.t_hi[last], self.t_lo[last])
                used = blocks[b][1]
                src = wpack[offs[b]:offs[b] + 128 * used].rearrange("(p c) -> p c", p=128)
                dst = RAW[b % NRAW][:, 0:used]
                sp.put(lambda e: e.dma_start(dst, src).then_inc(dsem[b % NRAW], 16))
                self.t_raw[b] = (dsem[b % NRAW], 16 * (b // NRAW + 1))
                self.loaded += 1

            def halve(self, i, part):
                b, off, n = where[i]
                raw = RAW[b % NRAW][:, off:off + n]
                hi, lo = HI[i % NHL][:, 0:n], LO[i % NHL][:, 0:n]
                if part == 0:
                    self.t_hi[i] = A(hi, raw, ACT.Copy, [self.t_raw[b], self.t_pe.get(i - NHL)])
                else:
                    self.t_lo[i] = TT(lo, raw, hi.bitcast(F32), ALU.subtract,
                                      [self.t_raw[b], self.t_hi[i], self.t_pe.get(i - NHL)])

            def ahead(self):
                while self.loaded < len(blocks) and (self.loaded < NRAW or
                                                     blocks[self.loaded - NRAW][0][-1][0] in self.t_lo):
                    self.load()

            def take(self, key, j=0):
                i = self.u + j
                assert pieces[i][0] == key, (pieces[i][0], key)
                self.ahead()
                for part, upto in ((0, self.u + NHL), (1, self.u + NHL - 1)):
                    while self.split[part] < min(len(pieces), upto):
                        self.halve(self.split[part], part)
                        self.split[part] += 1
                        self.ahead()
                assert self.split[1] > i
                _, width, kts = pieces[i]
                return HI[i % NHL], LO[i % NHL], width, [kt for _, kt, _ in kts], [self.t_hi[i], self.t_lo[i]]

            def done(self, tok):
                self.t_pe[self.u] = tok
                self.u += 1
                bg_step()

        S = Stream()
        fibers = deque()

        def bg_step():
            for f in list(fibers):
                try:
                    next(f)
                except StopIteration:
                    fibers.remove(f)

        def bg_drain():
            while fibers:
                bg_step()

        def gemm(key, xt, nk, outs, need=(), mid=None):
            pe.need(*need)

            def rows(piece, t):
                hi, lo, w, kts, ready = piece
                pe.need(*ready)
                sl = slice(128 * t, 128 * t + 128)
                for i, kt in enumerate(kts):
                    pe.need(xt.tok[kt][t])
                    o = i * w
                    for n, (xs, ws) in enumerate(((xt.H, hi), (xt.H, lo), (xt.L, hi))):
                        for ap, c0, c1 in outs[t]:
                            last = n == 2 and i == len(kts) - 1 and c1 == w
                            tok = mm(ap, xs[:, kt, sl], ws[:, o + c0:o + c1], kt == 0 and n == 0,
                                     kt == nk - 1 and n == 2, last)
                return tok

            total = sum(1 for p in pieces[S.u:S.u + 32] if p[0] == key)
            late = min(SKEW, total) if mid else 0
            toks = [None, None]
            for _ in range(total - late):
                piece = S.take(key)
                toks = [rows(piece, t) for t in (0, 1)]
                S.done(toks[1])
            if late:
                for j in range(late):
                    toks[0] = rows(S.take(key, j), 0)
                mid(toks[0])
                for _ in range(late):
                    toks[1] = rows(S.take(key), 1)
                    S.done(toks[1])
            return toks

        def gemm_w(key, xt, nk, outs, need=()):
            pe.need(*need)
            seen = 0
            while seen < nk:
                hi, lo, w, kts, ready = S.take(key)
                pe.need(*ready)
                for i, kt in enumerate(kts):
                    pe.need(*xt.tok[kt])
                    for m, ap in enumerate(outs):
                        o = i * w + 128 * m
                        for n, (ws, xs) in enumerate(((hi, xt.H), (hi, xt.L), (lo, xt.H))):
                            last = n == 2 and m == len(outs) - 1 and i == len(kts) - 1
                            tok = mm(ap, ws[:, o:o + 128], xs[:, kt, :], kt == 0 and n == 0 and m % 2 == 0,
                                     kt == nk - 1 and n == 2, last, skip=True)
                seen += len(kts)
                S.done(tok)
            return [tok, tok]

        def to_T(src, toks, nk, xt, gain=None, at=0):
            last = None
            for k in range(0, nk, 2):
                m = min(2, nk - k)
                ps, free = aux.get()
                pe.need(*free, *toks)
                for j in range(m):
                    for t in (0, 1):
                        last = tr(ps[:, 256 * j + 128 * t:256 * j + 128 * t + 128],
                                  src[t][:, 128 * (k + j):128 * (k + j) + 128], last=(j == m - 1 and t == 1))
                if gain is None:
                    hi = xt.H[:, at + k:at + k + m, :].rearrange("p a b -> p (a b)")
                    lo = xt.L[:, at + k:at + k + m, :].rearrange("p a b -> p (a b)")
                    t1 = A(hi, ps[:, 0:256 * m], ACT.Copy, [last, xt.free])
                    t2 = TT(lo, ps[:, 0:256 * m], hi.bitcast(F32), ALU.subtract, [last, t1, xt.free])
                else:
                    for j in range(m):
                        t1 = A(xt.H[:, at + k + j, :], ps[:, 256 * j:256 * j + 256], ACT.Copy, [last, xt.free],
                               scale=gain[:, k + j:k + j + 1])
                    for j in range(m):
                        hi, lo = xt.H[:, at + k + j, :], xt.L[:, at + k + j, :]
                        g = gain[:, k + j:k + j + 1]
                        p = ps[:, 256 * j:256 * j + 256]
                        t2 = STT(lo, p, g, hi.bitcast(F32), ALU.mult, ALU.subtract, [last, t1, xt.free])
                for j in range(m):
                    xt.tok[at + k + j] = [[t1, t2], [t1, t2]]
                aux.put(ps, [t1, t2])
            return last

        def turn(src, toks, t, ks, xt, gain=None):
            k0, m = ks[0], len(ks)
            ps, free = aux.get()
            pe.need(*free, *toks)
            for j in range(m):
                last = tr(ps[:, 128 * j:128 * j + 128], src[:, 128 * (k0 + j):128 * (k0 + j) + 128], last=(j == m - 1))
            sl = slice(128 * t, 128 * t + 128)
            if gain is None:
                p3 = ps[:, 0:128 * m].rearrange("p (a b) -> p a b", a=m)
                hi, lo = xt.H[:, k0:k0 + m, sl], xt.L[:, k0:k0 + m, sl]
                t1 = A(hi, p3, ACT.Copy, [last, xt.free])
                t2 = TT(lo, p3, hi.bitcast(F32), ALU.subtract, [last, t1, xt.free])
            else:
                for j in range(m):
                    t1 = A(xt.H[:, k0 + j, sl], ps[:, 128 * j:128 * j + 128], ACT.Copy, [last, xt.free],
                           scale=gain[:, k0 + j:k0 + j + 1])
                for j in range(m):
                    t2 = STT(xt.L[:, k0 + j, sl], ps[:, 128 * j:128 * j + 128], gain[:, k0 + j:k0 + j + 1],
                             xt.H[:, k0 + j, sl].bitcast(F32), ALU.mult, ALU.subtract, [last, t1, xt.free])
            for k in ks:
                xt.tok[k][t] = [t1, t2]
            aux.put(ps, [t1, t2])
            return last

        def col(name, l, n):
            return colt[:, COLS[(name, l)]:COLS[(name, l)] + n]

        state = {"x": [[], []], "xn": [], "rstd": [None, None], "later": [], "second": None}

        for t in (0, 1):
            state["x"][t] = [once(X[t][:, :], x[0, 128 * t:128 * t + 128, :], f"s_x{t}")]
        t_id = once(ident[:, :], ident_d, "s_id")
        t_col = once(colt[:, :], cols, "s_col")
        S.ahead()

        def mean_square(t, halves, eps=1e-6):
            ss, ms = stat(2), stat(1)
            for n in (0, 1):
                a = A(XN[t][:, 512 * n:512 * n + 512], X[t][:, 512 * n:512 * n + 512], ACT.Square,
                      [halves[n], state["xn"]], accum=ss[:, n:n + 1])
            b = TS(ms, ss[:, 0:1], ss[:, 1:2], 1.0 / D, ALU.add, ALU.mult, [a])
            b = TS(ms, ms, eps, None, ALU.add, need=[b])
            return rsqrt(ms, [b])

        VR = [Line(sem(f"s_vr{i}"), None) for i in range(2)]
        vr_at = [0]

        def vrow(name):
            line = VR[vr_at[0] % 2]
            vr_at[0] += 1
            i = VROWS.index(name)
            return line, load(line, line.buf[:, :], vrows[i:i + 1, :].broadcast_to([128, D]))

        def enter_scaled(gain):
            def f(t, halves):
                state["rstd"][t] = mean_square(t, halves)

                def turned():
                    for n in (0, 1):
                        a = turn(X[t], [halves[n], t_id, t_col], t, range(4 * n, 4 * n + 4), xT, gain)
                    state["x"][t] = [*halves, a]
                return turned
            return f

        def enter_rms(gain):
            def f(t, halves):
                r, c = mean_square(t, halves)
                cols_ = [slice(512 * n, 512 * n + 512) for n in (0, 1)]
                a = [TS(XN[t][:, cs], X[t][:, cs], r, None, ALU.mult, need=[c]) for cs in cols_]
                state["rstd"][t] = None
                state["x"][t] = [*halves, *a]

                def turned():
                    for n in (0, 1):
                        b = turn(XN[t], [a[n], t_id, t_col], t, range(4 * n, 4 * n + 4), xT, gain)
                    state["xn"] = [b]
                return turned
            return f

        def turn_x(t, a):
            def turned():
                for n in (0, 1):
                    b = turn(X[t], [a[n], t_id], t, range(4 * n, 4 * n + 4), xT)

                def scale_x():
                    state["x"][t] = [TS(X[t], X[t], ALPHA, None, ALU.mult, need=[*a, b])]
                state["later"].append(scale_x)
            return turned

        def enter_final():
            line, tl = vrow("final")

            def f(t, halves):
                r, c = mean_square(t, halves)
                state["rstd"][t] = None
                a = []
                for n in (0, 1):
                    cs = slice(512 * n, 512 * n + 512)
                    a.append(STT(X[t][:, cs], X[t][:, cs], r, line.buf[:, cs], ALU.mult, ALU.mult, [c, tl]))
                line.free.append(a[1])
                return turn_x(t, a)
            return f

        def enter_ln(g, b):
            (lg, tg), (lb, tb) = vrow(g), vrow(b)

            def f(t, halves):
                st_, mv, ve = stat(12), stat(2), stat(1)
                for n in (0, 1):
                    dve.need(halves[n])
                    a = dve.go(lambda e, n=n: e.bn_stats(st_[:, 6 * n:6 * n + 6], X[t][:, 512 * n:512 * n + 512]))
                dve.need(a)
                a = dve.go(lambda e: e.bn_aggr(mv, st_))
                c = TS(ve, mv[:, 1:2], 1e-5, None, ALU.add, need=[a])
                r, c = rsqrt(ve, [c])
                done = []
                for n in (0, 1):
                    cs = slice(512 * n, 512 * n + 512)
                    xs = X[t][:, cs]
                    a = TS(xs, xs, mv[:, 0:1], r, ALU.subtract, ALU.mult, [c])
                    a = TT(xs, xs, lg.buf[:, cs], ALU.mult, [a, tg])
                    done.append(TT(xs, xs, lb.buf[:, cs], ALU.add, [a, tb]))
                lg.free.append(done[1])
                lb.free.append(done[1])
                state["x"][t] = done
                state["rstd"][t] = None
                return turn_x(t, done)
            return f

        def between(tok=None):
            state["second"]()
            state["second"] = None

        def run_later():
            for f in state["later"]:
                f()
            state["later"] = []

        def swiglu(key, l, hT, sring, update):
            def act_half(hb, free, t, bank, tok):
                rs = state["rstd"][t]
                if rs is None:
                    a = A(hb[:, t, :], bank[:, 0:256], ACT.Silu, [tok, *free])
                    th = TT(hb[:, t, :], hb[:, t, :], bank[:, 256:512], ALU.mult, [a, tok])
                else:
                    r, tr_ = rs
                    a = A(hb[:, t, :], bank[:, 0:256], ACT.Silu, [tok, tr_, *free], scale=r)
                    th = STT(hb[:, t, :], bank[:, 256:512], r, hb[:, t, :], ALU.mult, ALU.mult, [a, tok, tr_])
                mmb.put(bank, [th])
                return th

            def turn_later(c, hb, th):
                yield
                ps, free = aux.get()
                pe.need(*free, *th)
                for j in (0, 1):
                    for t in (0, 1):
                        last = tr(ps[:, 256 * j + 128 * t:256 * j + 128 * t + 128],
                                  hb[:, t, 128 * j:128 * j + 128], last=(j == 1 and t == 1))
                hi = hT.H[:, 2 * c:2 * c + 2, :].rearrange("p a b -> p (a b)")
                lo = hT.L[:, 2 * c:2 * c + 2, :].rearrange("p a b -> p (a b)")
                t1 = A(hi, ps[:, :], ACT.Copy, [last])
                t2 = TT(lo, ps[:, :], hi.bitcast(F32), ALU.subtract, [last, t1])
                hT.tok[2 * c] = hT.tok[2 * c + 1] = [[t1, t2], [t1, t2]]
                aux.put(ps, [t1, t2])
                sring.put(hb, [last])

            for c in range(NCH):
                banks, need = two()
                hb, free = sring.get()
                th = []

                def mid(tok):
                    th.append(act_half(hb, free, 0, banks[0], tok))
                    between()

                toks = gemm((key, "up", l, c), xT, 8, [[(b[:, :], 0, 512)] for b in banks], need,
                            mid if c == 0 else None)
                for t in range(len(th), 2):
                    th.append(act_half(hb, free, t, banks[t], toks[t]))
                f = turn_later(c, hb, th)
                next(f)
                fibers.append(f)
                if c == 1:
                    run_later()
            xT.free = [toks[1]]
            (b01, n01), (b23, n23) = two(), two()
            banks = [b01, b23]
            outs = [[(banks[t][n][:, :], 512 * n, 512 * n + 512) for n in (0, 1)] for t in (0, 1)]
            turned = []
            toks = gemm((key, "down", l), hT, 22, outs, n01 + n23,
                        lambda tok: turned.append(update(0, banks[0], tok)))
            state["fence"] = [toks[1]]
            turned[0]()
            state["second"] = update(1, banks[1], toks[1])

        def two():
            (a, f), (b, g) = mmb.get(), mmb.get()
            return [a, b], f + g

        def one():
            a, f = mmb.get()
            return [a], f

        def ffn(key, l, then):
            with ExitStack() as ph:
                hT = XT(22, ph)
                sring = Pool([sbuf([128, 2, 256], F32, ph) for _ in range(2)])

                def update(t, banks, tok):
                    halves = []
                    for n in (0, 1):
                        xs = X[t][:, 512 * n:512 * n + 512]
                        halves.append(STT(xs, banks[n][:, :], 0.5, xs, ALU.mult, ALU.add, [tok, *state["x"][t]]))
                        mmb.put(banks[n], [halves[n]])
                    return then(t, halves)

                swiglu(key, l, hT, sring, update)

        def product_out(key, l, then):
            halves = [[], []]
            for n in (0, 1):
                banks, need = two()

                def update(t, tok):
                    xs = X[t][:, 512 * n:512 * n + 512]
                    halves[t].append(TT(xs, xs, banks[t][:, :], ALU.add, [tok, *state["x"][t]]))
                    mmb.put(banks[t], [halves[t][-1]])

                turned = []

                def mid(tok):
                    update(0, tok)
                    turned.append(then(0, halves[0]))

                toks = gemm((key, l, n), xT, 8, [[(b[:, :], 0, 512)] for b in banks], need, mid if n else None)
                state["fence"] = [toks[1]]
                if n == 0:
                    update(0, toks[0])
                else:
                    turned[0]()
                update(1, toks[1])
            state["second"] = then(1, halves[1])

        def softmax_scores(S_mm, scale, bias, bias_tok, need, tmp, nm, den, slope=1.0):
            ps, free = aux.get()
            pe.need(*free, *need)
            qT, kT = S_mm
            mm(ps[:, 0:128], qT[:, 0:128], kT[:, 0:128], True, True)
            t0 = mm(ps[:, 128:384], qT[:, 128:256], kT[:, 0:256], True, True, True)
            sm, f2 = tmp.get()
            t1 = STT(sm[:, :], ps[:, 0:384], scale / slope, bias, ALU.mult, ALU.add, [t0, bias_tok, *f2])
            aux.put(ps, [t1])
            RED(nm[:, 0:1], sm[:, 0:128], ALU.max, [t1], negate=True)
            t2 = RED(nm[:, 1:2], sm[:, 128:384], ALU.max, negate=True)
            if slope != 1.0:
                t2 = TS(nm, nm, slope, None, ALU.mult, need=[t2])

            def exps(pr):
                p, f3 = pr.get()
                A(p[:, 0:128], sm[:, 0:128], ACT.Exp, [t2, *f3], scale=slope, bias=nm[:, 0:1], accum=den[:, 0:1])
                t3 = A(p[:, 128:384], sm[:, 128:384], ACT.Exp, scale=slope, bias=nm[:, 1:2], accum=den[:, 1:2])
                tmp.put(sm, [t3])
                return p, t3, den
            return exps, t1

        def turn_probs(p, need, pr, pt):
            ps, free = aux.get()
            pe.need(*free, *need)
            for j in range(3):
                t0 = tr(ps[:, 128 * j:128 * j + 128], p[:, 128 * j:128 * j + 128], last=(j == 2))
            pr.put(p, [t0])
            q, f = pt.get()
            t1 = A(q[:, :], ps[:, 0:384], ACT.Copy, [t0, *f])
            aux.put(ps, [t1])
            return q, t1

        def values(q, t_q, v, dv, pt, need=()):
            ps, free = aux.get()
            pe.need(*free, t_q, *need)
            mm(ps[:, 0:dv], q[:, 0:128], v[0], True, True)
            mm(ps[:, dv:2 * dv], q[:, 128:256], v[0], True, False)
            t0 = mm(ps[:, dv:2 * dv], q[:, 256:384], v[1], False, True, True)
            pt.put(q, [t0])
            return ps, t0

        def mixer1(l, blk, then):
            with ExitStack() as ph:
                QK = sbuf([128, 18, 256], F32, ph)
                V = sbuf([128, 2, 1152], F32, ph)
                Omla = sbuf([128, 2, 384], F32, ph)
                Omo = sbuf([128, 2, 384], F32, ph)
                Odn = sbuf([128, 2, 768], F32, ph)
                Odl = sbuf([128, 2, 256], F32, ph)
                oT = [XT(3, ph) for _ in range(2)]
                tmp = Pool([sbuf([128, 384], F32, ph) for _ in range(2)])
                pr = Pool([sbuf([128, 384], F32, ph) for _ in range(3)])
                pt = Pool([sbuf([128, 384], F32, ph) for _ in range(2)])
                t_qk = {}
                t_v = {}
                res = {}
                fence = state["fence"]

                def finish(o_view, den2, n):
                    def f(ps, t0, need):
                        r = stat(2)
                        a = RCP(r, den2, need)
                        b = TT(o_view, ps[:, 0:2 * n].rearrange("p (t d) -> p t d", t=2), bc(r, n), ALU.mult,
                               [a, t0])
                        aux.put(ps, [b])
                        return b
                    return f

                nmd, dnd = stat(24), stat(24)

                def heads():
                    act.put(lambda e: e.preload_act_table_set("natural_log_exp_and_others"))
                    items = [("mo", h) for h in range(6)] + [("di", h) for h in range(12)]
                    probs, pts = {}, {}
                    for s in range(len(items) + 4):
                        if 0 <= s - 1 < len(items):
                            probs[s - 1] = probs[s - 1](pr)
                        if 0 <= s < len(items):
                            kind, h = items[s]
                            qb, kb = (h // 2, 3 + h // 2) if kind == "mo" else (6 + h // 2, 12 + h // 2)
                            rows_ = slice(64 * (h % 2), 64 * (h % 2) + 64)
                            if kind == "mo":
                                nm, den = stat(2), stat(2)
                            else:
                                nm = nmd.rearrange("p (t h) -> p h t", t=2)[:, h, :]
                                den = dnd.rearrange("p (t h) -> p h t", t=2)[:, h, :]
                            table, slope = (3, SLOPES[12 + h]) if kind == "mo" else (h // 4, SLOPES[h])
                            probs[s], _ = softmax_scores((QK[rows_, qb, :], QK[rows_, kb, :]), 0.125,
                                                         blk["dist"][:, table, :], blk["t_dist"],
                                                         [t_qk[qb], t_qk[kb]], tmp, nm, den, slope)
                        if 0 <= s - 2 < len(items):
                            p, t3, den = probs[s - 2]
                            pts[s - 2] = turn_probs(p, [t3], pr, pt)
                        if 0 <= s - 3 < len(items):
                            kind, h = items[s - 3]
                            q, tq = pts[s - 3]
                            if kind == "mo":
                                v = [V[:, t, 64 * h:64 * h + 64] for t in (0, 1)]
                                nv = [t_v[0, 0], t_v[0, 1]]
                            else:
                                v = [V[:, t, 384 + 64 * h:448 + 64 * h] for t in (0, 1)]
                                nv = [t_v[1 + h // 6, 0], t_v[1 + h // 6, 1]]
                            ps, t0 = values(q, tq, v, 64, pt, nv)
                            if kind == "mo":
                                res["mo"] = finish(Omo[:, :, 64 * h:64 * h + 64], probs[s - 3][2], 64)(
                                    ps, t0, [probs[s - 3][1]])
                            else:
                                t1 = CP(Odn[:, :, 64 * h:64 * h + 64],
                                        ps[:, 0:128].rearrange("p (t d) -> p t d", t=2), [t0])
                                aux.put(ps, [t1])
                                res["dn"] = [t1, probs[s - 3][1]]
                        yield
                        if s % 3 == 2:
                            yield
                    lg, ls = stat(24), stat(24)
                    a = A(lg, dnd, ACT.Ln, res["dn"])
                    b = TT(ls, lg, nmd, ALU.subtract, [a])
                    v4 = lambda ap: ap.rearrange("p (t g h) -> p t g h", t=2, g=3)
                    v4h = lambda ap: ap.rearrange("p (t g h) -> p t h g", t=2, g=3)
                    mx, sm_, e = stat(8), stat(8), stat(24)
                    c = RED(mx.rearrange("p (t h) -> p t h", t=2), v4h(ls), ALU.max, [b])
                    m3 = mx.rearrange("p (t h) -> p t h", t=2)
                    for g in range(3):
                        d = TT(v4(ls)[:, :, g, :], v4(ls)[:, :, g, :], m3, ALU.subtract, [c])
                    a = A(e, ls, ACT.Exp, [d])
                    b = RED(sm_.rearrange("p (t h) -> p t h", t=2), v4h(e), ALU.add, [a])
                    s3 = sm_.rearrange("p (t h) -> p t h", t=2)
                    for g in range(3):
                        c = TT(v4(ls)[:, :, g, :], v4(dnd)[:, :, g, :], s3, ALU.mult, [b])
                    d = RCP(lg, ls, [c])
                    w_ = stat(24)
                    d = TT(w_, e, lg, ALU.mult, [d])
                    yield
                    o4 = Odl[:, :, :].rearrange("p t (h d) -> p t h d", h=4)
                    for g in range(3):
                        n4 = Odn[:, :, 256 * g:256 * g + 256].rearrange("p t (h d) -> p t h d", h=4)
                        for t in (0, 1):
                            c = TT(n4[:, t], n4[:, t], bc(v4(w_)[:, t, g, :], 64), ALU.mult, [d, *res["dn"]])
                    s1 = TT(o4, Odn[:, :, 0:256].rearrange("p t (h d) -> p t h d", h=4),
                            Odn[:, :, 256:512].rearrange("p t (h d) -> p t h d", h=4), ALU.add, [c])
                    res["di"] = TT(o4, o4, Odn[:, :, 512:768].rearrange("p t (h d) -> p t h d", h=4), ALU.add, [s1])
                    yield

                with ExitStack() as pm:
                    lat = sbuf([128, 2, 416], F32, pm)
                    qs = sbuf([128, 2, 576], F32, pm)
                    ks = sbuf([128, 2, 576], F32, pm)
                    vm = sbuf([128, 2, 384], F32, pm)
                    cq = XT(2, pm)
                    ckv = XT(1, pm)
                    ra = sbuf([128, 2, 96], F32, pm)
                    rb = sbuf([128, 2, 96], F32, pm)
                    qkh = Pool([sbuf([96, 512], F32, pm) for _ in range(2)])
                    tm = {}

                    def rope(dst, src, t, h, need):
                        cc, ss = blk["rope"][:, t, 0:32], blk["rope"][:, t, 32:64]
                        a3 = ra[:, t, 0:32 * h].rearrange("p (h d) -> p h d", h=h)
                        b3 = rb[:, t, 0:32 * h].rearrange("p (h d) -> p h d", h=h)
                        TT(a3, src, bc1(cc, h), ALU.mult, [*need, blk["t_rope"]])
                        t1 = TT(b3, src, bc1(ss, h), ALU.mult)
                        TT(dst[:, :, 0:16], a3[:, :, 0:16], b3[:, :, 16:32], ALU.subtract, [t1])
                        return TT(dst[:, :, 16:32], a3[:, :, 16:32], b3[:, :, 0:16], ALU.add), t1

                    def latents(banks, tok):
                        a, b = [], []
                        ss = stat(4)
                        for t in (0, 1):
                            A(lat[:, t, 0:256], banks[t][:, 0:256], ACT.Square, [tok, *fence],
                              accum=ss[:, 2 * t:2 * t + 1])
                            a.append(A(lat[:, t, 256:384], banks[t][:, 256:384], ACT.Square,
                                       accum=ss[:, 2 * t + 1:2 * t + 2]))
                        ms = stat(4)
                        toks = []
                        for t in (0, 1):
                            TS(ms[:, 2 * t:2 * t + 1], ss[:, 2 * t:2 * t + 1], 1.0 / 256, 1e-6, ALU.mult, ALU.add, [a[t]])
                            b.append(TS(ms[:, 2 * t + 1:2 * t + 2], ss[:, 2 * t + 1:2 * t + 2], 1.0 / 128, 1e-6,
                                        ALU.mult, ALU.add))
                            kr = lat[:, t, 384:416].unsqueeze(1)
                            tk, _ = rope(kr, banks[t][:, 384:416].unsqueeze(1), t, 1, [tok, a[t]])
                            tm["kr", t] = CP(ks[:, t, :].rearrange("p (h d) -> p h d", h=6)[:, :, 64:96],
                                             bc1(lat[:, t, 384:416], 6), [tk])
                        for t in (0, 1):
                            r, c = rsqrt(ms[:, 2 * t:2 * t + 2], [b[t]])
                            toks.append(TS(lat[:, t, 0:256], banks[t][:, 0:256], r[:, 0:1], None, ALU.mult, need=[c]))
                            toks.append(TS(lat[:, t, 256:384], banks[t][:, 256:384], r[:, 1:2], None, ALU.mult))
                            mmb.put(banks[t], [toks[-1], tm["kr", t]])

                        yield
                        to_T([lat[:, t, 0:256] for t in (0, 1)], toks, 2, cq, col("q_norm", l, 2))
                        to_T([lat[:, t, 256:384] for t in (0, 1)], toks, 1, ckv, col("kv_norm", l, 1))

                    banks, need = two()
                    tok = gemm(("mla", l), xT, 8, [[(b[:, 0:416], 0, 416)] for b in banks], need, between)
                    f = latents(banks, tok)
                    next(f)
                    fibers.append(f)

                    def qk_chunk(c):
                        n = 4 if c < 4 else 2
                        banks, need = two() if n == 4 else one()
                        outs = [banks[m // 2][:, 256 * (m % 2):256 * (m % 2) + 256] for m in range(n)]
                        tok = gemm_w(("qk1", l, c), xT, 8, outs, need)
                        for j, b in enumerate(banks):
                            dst = QK[:, 4 * c + 2 * j:4 * c + 2 * j + 2, :].rearrange("p a b -> p (a b)")
                            if j == 0:
                                t1 = A(dst, b[:, :], ACT.Copy, [tok])
                            else:
                                t1 = CP(dst, b[:, :], [tok])
                            mmb.put(b, [t1])
                            t_qk[4 * c + 2 * j] = t_qk[4 * c + 2 * j + 1] = t1

                    qk_chunk(0)
                    for j in (0, 1):
                        banks, need = two()
                        tok = gemm(("uq", l, j), cq, 2, [[(b[:, 0:288], 0, 288)] for b in banks], need)
                        for t in (0, 1):
                            dst = qs[:, t, 288 * j:288 * j + 288]
                            a = A(dst, banks[t][:, 0:288], ACT.Copy, [tok])
                            v3 = dst.rearrange("p (h d) -> p h d", h=3)[:, :, 64:96]
                            p3 = banks[t][:, 0:288].rearrange("p (h d) -> p h d", h=3)[:, :, 64:96]
                            b, t1 = rope(v3, p3, t, 3, [a])
                            tm["q", j, t] = b
                            mmb.put(banks[t], [a, t1])
                    for j in (0, 1):
                        banks, need = two()
                        tok = gemm(("ukv", l, j), ckv, 1, [[(b[:, 0:384], 0, 384)] for b in banks], need)
                        for t in (0, 1):
                            p3 = banks[t][:, 0:384].rearrange("p (h d) -> p h d", h=3)
                            k3 = ks[:, t, 288 * j:288 * j + 288].rearrange("p (h d) -> p h d", h=3)
                            v3 = vm[:, t, 192 * j:192 * j + 192].rearrange("p (h d) -> p h d", h=3)
                            a = A(k3[:, :, 0:64], p3[:, :, 0:64], ACT.Copy, [tok])
                            b = CP(v3, p3[:, :, 64:128], [tok, a])
                            tm["k", j, t] = [a, tm["kr", t]]
                            tm["v", j, t] = b
                            mmb.put(banks[t], [a, b])

                    def mla_heads():
                        turned, probs, pts = {}, {}, {}
                        for s in range(6 + 5):
                            if 0 <= s - 2 < 6:
                                probs[s - 2] = probs[s - 2](pr)
                            if s < 6:
                                ps, free = aux.get()
                                pe.need(*free)
                                for n, src in enumerate((qs, ks)):
                                    for t in (0, 1):
                                        pe.need(tm["qk"[n], s // 3, t])
                                        t0 = tr(ps[0:96, 256 * n + 128 * t:256 * n + 128 * t + 128],
                                                src[:, t, 96 * s:96 * s + 96], last=(n == 1 and t == 1))
                                b, f = qkh.get()
                                t1 = A(b[:, :], ps[0:96, :], ACT.Copy, [t0, *f])
                                aux.put(ps, [t1])
                                turned[s] = (b, t1)
                            if 0 <= s - 1 < 6:
                                h = s - 1
                                b, t1 = turned[h]
                                nm, den = stat(2), stat(2)
                                probs[h], t2 = softmax_scores((b[:, 0:256], b[:, 256:512]), 96.0 ** -0.5,
                                                              blk["causal"][:, :], blk["t_causal"], [t1], tmp, nm, den)
                                qkh.put(b, [t2])
                            if 0 <= s - 3 < 6:
                                h = s - 3
                                p, t3, den = probs[h]
                                pts[h] = turn_probs(p, [t3], pr, pt)
                            if 0 <= s - 4 < 6:
                                h = s - 4
                                q, tq = pts[h]
                                v = [vm[:, t, 64 * h:64 * h + 64] for t in (0, 1)]
                                ps, t0 = values(q, tq, v, 64, pt, [tm["v", h // 3, 0], tm["v", h // 3, 1]])
                                res["mla"] = finish(Omla[:, :, 64 * h:64 * h + 64], probs[h][2], 64)(ps, t0, [probs[h][1]])
                            yield
                            if s % 2:
                                yield

                    def v_chunk(j):
                        c0 = 384 * j
                        banks, need = two()
                        tok = gemm(("v1", l, j), xT, 8, [[(b[:, 0:384], 0, 384)] for b in banks], need)
                        for t in (0, 1):
                            dst = V[:, t, c0:c0 + 384]
                            t1 = (A(dst, banks[t][:, 0:384], ACT.Copy, [tok]) if t == 0
                                  else CP(dst, banks[t][:, 0:384], [tok]))
                            t_v[j, t] = t1
                            mmb.put(banks[t], [t1])

                    def all_heads():
                        yield from mla_heads()
                        res["mla_done"] = True
                        to_T([Omla[:, t, :] for t in (0, 1)], [res["mla"]], 3, oT[0])
                        yield from heads()
                        to_T([Odl[:, t, :] for t in (0, 1)], [res["di"]], 2, oT[1])

                    fibers.append(all_heads())
                    for c in (1, 2, 3):
                        qk_chunk(c)
                    v_chunk(0)
                    qk_chunk(4)
                    v_chunk(1)
                    v_chunk(2)
                    assert res["mla_done"]

                G = sbuf([128, 2, 3072], F32, ph)
                gated = set()
                t_g = {}
                for c in range(6):
                    banks, need = two()
                    tok = gemm(("g1", l, c), xT, 8, [[(b[:, :], 0, 512)] for b in banks], need)
                    if not fibers:
                        gated.add(c)
                    for t in (0, 1):
                        t_g[c, t] = A(G[:, t, 512 * c:512 * c + 512], banks[t][:, :],
                                      ACT.Copy if fibers else ACT.Sigmoid, [tok])
                        mmb.put(banks[t], [t_g[c, t]])
                bg_drain()
                order = [(r, nk) for r, _, nk in BR1]
                for r, _ in order:
                    for c in (2 * r, 2 * r + 1):
                        for t in (0, 1):
                            if c not in gated:
                                g = G[:, t, 512 * c:512 * c + 512]
                                t_g[c, t] = A(g, g, ACT.Sigmoid, [t_g[c, t]])
                third = lambda: to_T([Omo[:, t, :] for t in (0, 1)], [res["mo"]], 3, oT[0])
                branches("br1", l, order, [oT[0], oT[1], oT[0]], G, t_g, XN, state["xn"], third)
                product_out("o1", l, then)

        def branches(key, l, order, ots, G, t_g, dst, dfree, third):
            merged = {}
            for i, (r, nk, *_) in enumerate(order):
                for n in (0, 1):
                    banks, need = two()

                    def merge(t, tok):
                        m = dst[t][:, 512 * n:512 * n + 512]
                        g = G[:, t, 1024 * r + 512 * n:1024 * r + 512 * n + 512]
                        if i == 0:
                            a = TT(m, banks[t][:, :], g, ALU.mult, [tok, t_g[2 * r + n, t], dfree])
                            mmb.put(banks[t], [a])
                        else:
                            b = TT(g, banks[t][:, :], g, ALU.mult, [tok, t_g[2 * r + n, t]])
                            mmb.put(banks[t], [b])
                            a = TT(m, m, g, ALU.add, [b, merged[t, n]])
                        merged[t, n] = a

                    late = i == len(order) - 1 and n == 1

                    def mid(tok):
                        merge(0, tok)
                        for t in (0, 1):
                            state["xn"] = [turn(dst[t], [merged[t, 0]], t, range(0, 4), xT)]

                    toks = gemm((key, l, r, n), ots[i], nk, [[(b[:, :], 0, 512)] for b in banks], need,
                                mid if late else None)
                    if not late:
                        merge(0, toks[0])
                    merge(1, toks[1])
                ots[i].free = [toks[1]]
                if i == 0:
                    third()
            for t in (0, 1):
                state["xn"] = [turn(dst[t], [merged[t, 1]], t, range(4, 8), xT)]

        with ExitStack() as b1:
            blk = {}
            blk["rope"] = sbuf([128, 2, 64], F32, b1)
            blk["t_rope"] = once(blk["rope"][:, :, :], rope_d[:, :, 0:64], "s_rope1")
            blk["causal"] = sbuf([128, 384], F32, b1)
            blk["t_causal"] = once(blk["causal"][:, :], bias_d[4], "s_causal1")
            blk["dist"] = sbuf([128, 4, 384], F32, b1)
            blk["t_dist"] = once(blk["dist"][:, :, :], bias_d[0:4].rearrange("n p c -> p n c"), "s_dist")
            enter = enter_scaled(col("ffn1_norm", 0, 8))
            enter(0, [state["x"][0]] * 2)()
            state["second"] = enter(1, [state["x"][1]] * 2)
            for l in (0, 1):
                ffn("f1", l, enter_rms(col("mix_norm", l, 8)))
                mixer1(l, blk, enter_scaled(col("ffn2_norm", l, 8)))
                if l == 0:
                    ffn("f2", l, enter_scaled(col("ffn1_norm", 1, 8)))
        fence_b2 = state["fence"]

        b2 = ctx
        s_out = sem("s_out")
        for line in VR:
            line.buf, line.free = sbuf([128, D], F32, b2), [fence_b2]

        def once2(out, in_, name):
            sp.need(*fence_b2)
            return once(out, in_, name)

        U64 = sbuf([128, 128], F32, b2)
        t_u64 = once2(U64[:, :], msk_d[:, 384:512], "s_u64")
        tri = sbuf([128, 384], F32, b2)
        t_tri = once2(tri[:, :], msk_d[:, 0:384], "s_tri")
        strict = sbuf([128, 384], F32, b2)
        t_strict = once2(strict[:, :], bias_d[5], "s_strict")
        chunk = sbuf([128, 384], F32, b2)
        t_chunk = once2(chunk[:, :], bias_d[6], "s_chunk")
        rope2 = sbuf([128, 2, 32], F32, b2)
        t_rope2 = once2(rope2[:, :, :], rope_d[:, :, 64:96], "s_rope2")
        zero = sbuf([128, 256], F32, b2)
        dve.need(fence_b2)
        t_zero = dve.go(lambda e: e.memset(zero[:, :], 0.0))
        s_lam = sbuf([128, 128], F32, b2)
        rw_line, ar_line, scr_line = Line(sem("s_rw"), None), Line(sem("s_ar"), None), Line(sem("s_scr"), None)


        def mixer2(l, then):
            lam_init = 0.8 - 0.6 * math.exp(-0.3 * l)
            fence = state["fence"]
            with ExitStack() as ph:
                OA = sbuf([128, 2, 1024], F32, ph)
                OB = sbuf([128, 2, 1024], F32, ph)
                OC = XNB
                tmp = Pool([sbuf([128, 384], F32, ph) for _ in range(2)])
                pr = Pool([sbuf([128, 384], F32, ph) for _ in range(3)])
                pt = Pool([sbuf([128, 384], F32, ph) for _ in range(2)])
                rw = sbuf([128, 304], F32, ph)
                rw_line.buf = rw
                t_rw = load(rw_line, rw[:, :], rows[l:l + 1, :].broadcast_to([128, 304]), fence)
                rc = ph
                R1 = sbuf([128, 6144], F32, ph)
                QKA = R1[:, 0:4096].rearrange("p (a b) -> p a b", a=16)
                VAt = R1[:, 4096:6144].rearrange("p (a b) -> p a b", a=2)
                reg2 = ExitStack()
                Z = XN
                BC = sbuf([128, 4, 256], F32, reg2)
                XD = sbuf([128, 2, 1024], F32, reg2)
                AR = sbuf([128, 4, 256], F32, reg2)
                M = sbuf([128, 4, 384], F32, reg2)
                CB = sbuf([128, 2, 384], F32, reg2)
                cacc = Pool([sbuf([128, 256], F32, reg2) for _ in range(3)])
                ROT = Pool([sbuf([128, 512], F32, reg2) for _ in range(2)])
                rt = [sbuf([128, 128], F32, reg2) for _ in range(2)]
                dtt, dA = sbuf([128, 2, 16], F32, reg2), sbuf([128, 2, 16], F32, reg2)
                s16 = [sbuf([128, 32], F32, reg2) for _ in range(2)]
                arow = sbuf([16, 256], F32, reg2)
                acol = sbuf([128, 2, 16], F32, reg2)
                cadd = sbuf([128, 6, 16], F32, reg2)
                tk = {}

                def scalars():
                    d3 = s_lam[:, :].rearrange("p (a b) -> p a b", a=2)
                    l4 = rw[:, 0:256].rearrange("p (a c b) -> p a c b", a=2, c=2)
                    a = TT(d3, l4[:, :, 0, :], l4[:, :, 1, :], ALU.mult, [t_rw, fence])
                    sd = stat(2)
                    b = RED(sd, d3, ALU.add, [a])
                    es = stat(2)
                    c = A(es, sd, ACT.Exp, [b])
                    nl = stat(1)
                    TS(nl, es[:, 1:2], es[:, 0:1], -lam_init, ALU.subtract, ALU.add, [c])
                    tk["nlam"] = (dve.sem, dve.n)
                    gs = stat(1)
                    tk["gs"] = TS(gs, col("diff_subln_g_2", l, 1), 1.0 - lam_init, None, ALU.mult)
                    an = stat(16)
                    a = A(an, rw[:, 272:288], ACT.Exp, [t_rw])
                    tk["an"] = TS(an, an, -1.0, None, ALU.mult, need=[a])
                    return nl, gs, an

                nlam, gsub, aneg = scalars()

                def z_post(banks, tok, n):
                    for t in (0, 1):
                        a = A(Z[t][:, 512 * n:512 * n + 512], banks[t][:, :], ACT.Silu, [tok, state["xn"]])
                        mmb.put(banks[t], [a])
                        tk["z", n, t] = a
                    yield

                for n in (0, 1):
                    banks, need = two()
                    tok = gemm(("z", l, n), xT, 8, [[(b[:, :], 0, 512)] for b in banks], need,
                               None if n else between)
                    for _ in z_post(banks, tok, n):
                        pass
                run_later()

                b_, f = one()
                dtb = b_[0]
                tok = dt_gemm(l, dtb, f)

                def dts():
                    z, w = s16
                    for t in (0, 1):
                        a = TT(z[:, 16 * t:16 * t + 16], dtb[:, 16 * t:16 * t + 16], rw[:, 256:272], ALU.add,
                               [tok, t_rw])
                    mmb.put(dtb, [a])
                    yield
                    act.put(lambda e: e.preload_act_table_set("natural_log_exp_and_others"))
                    b = A(w[:, :], z[:, :], ACT.Abs, [a])
                    b = A(w[:, :], w[:, :], ACT.Exp, [b], scale=-1.0)
                    b = A(w[:, :], w[:, :], ACT.Ln, [b], bias=1.0)
                    d2 = dtt[:, :, :].rearrange("p t h -> p (t h)")
                    tk["dt"] = STT(d2, z[:, :], 0.0, w[:, :], ALU.max, ALU.add, [b])
                    c = TT(dA[:, :, :], dtt[:, :, :], bc1(aneg, 2), ALU.mult, [tk["dt"], tk["an"]])
                    yield
                    ps, free = aux.get()
                    pe.need(*free, c, t_u64)
                    for t in (0, 1):
                        a = mm(ps[0:16, 128 * t:128 * t + 128], dA[:, t, :], U64[:, :], True, True, t == 1)
                    a = A(arow[:, :], ps[0:16, 0:256], ACT.Copy, [a])
                    aux.put(ps, [a])
                    tk["arow"] = a
                    sp.need(a, scr_line.free)
                    scr_line.n += 1
                    sp.put(lambda e: e.dma_start(scratch[l], arow[:, :]).then_inc(scr_line.sem, 16))
                    tk["scr"] = (scr_line.sem, 16 * scr_line.n)
                    yield
                    ps, free = aux.get()
                    pe.need(*free, a)
                    for t in (0, 1):
                        b = tr(ps[:, 16 * t:16 * t + 16], arow[:, 128 * t:128 * t + 128], last=(t == 1))
                    c = CP(acol[:, :, :].rearrange("p t h -> p (t h)"), ps[:, 0:32], [b])
                    aux.put(ps, [c])
                    tk["acol"] = c

                f = dts()
                next(f)
                fibers.append(f)

                t_bc, t_xd, t_ob = [None] * 4, [None] * 4, [None] * 4

                def conv_tile(ct, src, prev):
                    acc, free = cacc.get()
                    w = colt[:, COLS[("ssm_conv_w_2", l)] + 4 * ct:COLS[("ssm_conv_w_2", l)] + 4 * ct + 4]
                    b = colt[:, COLS[("ssm_conv_b_2", l)] + ct:COLS[("ssm_conv_b_2", l)] + ct + 1]
                    a = A(acc[:, :], src, ACT.Identity, [tk["xbc"], *free, fence, prev], scale=w[:, 3:4], bias=b)
                    for s in (1, 2, 3):
                        a = STT(acc[:, s:256], src[:, 0:256 - s], w[:, 3 - s:4 - s], acc[:, s:256], ALU.mult, ALU.add,
                                [a])
                    return acc, a

                def xbc_chunk(c):
                    banks, need = two()
                    outs = [banks[m // 2][:, 256 * (m % 2):256 * (m % 2) + 256] for m in range(4)]
                    tk["xbc"] = gemm_w(("xbc", l, c), xT, 8, outs, need)

                    def post():
                        a = None
                        for m in range(4):
                            if c == 2:
                                acc, a = conv_tile(8 + m, outs[m], a)
                                t_bc[m] = A(BC[:, m, :], acc[:, :], ACT.Silu, [a])
                                cacc.put(acc, [t_bc[m]])
                                if m % 2:
                                    mmb.put(banks[m // 2], [a])
                                if m % 2:
                                    yield
                                continue
                            acc, a = conv_tile(4 * c + m, outs[m], a)
                            if m % 2:
                                mmb.put(banks[m // 2], [a])
                            b = A(acc[:, :], acc[:, :], ACT.Silu, [a])
                            ct = 4 * c + m
                            ps, free = aux.get()
                            pe.need(*free, b)
                            for t in (0, 1):
                                e = tr(ps[:, 128 * t:128 * t + 128], acc[:, 128 * t:128 * t + 128], last=(t == 1))
                            cacc.put(acc, [e])
                            for t in (0, 1):
                                p3 = ps[:, 128 * t:128 * t + 128].rearrange("p (h d) -> p h d", h=2)
                                o3 = OB[:, t, 128 * ct:128 * ct + 128].rearrange("p (h d) -> p h d", h=2)
                                x3 = XD[:, t, 128 * ct:128 * ct + 128].rearrange("p (h d) -> p h d", h=2)
                                TT(o3, p3, bc(rw[:, 288 + 2 * ct:290 + 2 * ct], 64), ALU.mult, [e, t_rw])
                                tk["xd"] = TT(x3, p3, bc(dtt[:, t, 2 * ct:2 * ct + 2], 64), ALU.mult, [tk["dt"]])
                            aux.put(ps, [tk["xd"]])
                            yield
                    f = post()
                    next(f)
                    fibers.append(f)

                for c in (2, 0, 1):
                    xbc_chunk(c)

                def ssd():
                    for g in (0, 1):
                        ps, free = aux.get()
                        pe.need(*free, *t_bc)
                        mm(ps[:, 0:256], BC[:, g, 0:128], BC[:, 2 + g, 0:256], True, True)
                        a = mm(ps[:, 256:384], BC[:, g, 128:256], BC[:, 2 + g, 128:256], True, True, True)
                        tk["cb", g] = TT(CB[:, g, :], ps[:, 0:384], tri[:, :], ALU.mult, [a, t_tri])
                        aux.put(ps, [tk["cb", g]])
                        yield
                    halves = [range(4 * q, 4 * q + 4) for q in range(4)]
                    t_m = None
                    ypsum = {}
                    for q in range(4):
                        hs = slice(4 * q, 4 * q + 4)
                        g = q // 2
                        src = scratch[l, 4 * q:4 * q + 4, :].unsqueeze(0).broadcast_to([128, 4, 256])
                        ta = load(ar_line, AR[:, :, :], src, [tk["scr"]])
                        base = TS(cadd[:, 0, hs], acol[:, 0, hs], -1.0, None, ALU.mult, need=[tk["acol"]])
                        b4 = TS(cadd[:, 4, hs], acol[:, 1, hs], -1.0, None, ALU.mult)
                        CP(cadd[:, 1, hs], cadd[:, 0, hs], [base])
                        c5 = CP(cadd[:, 5, hs], cadd[:, 4, hs], [b4])
                        tot = lambda c: AR[:, :, 64 * c + 63]
                        lowp = slice(0, 64)
                        a = TT(cadd[lowp, 1, hs], cadd[lowp, 1, hs], AR[lowp, :, 63], ALU.add, [ta, c5])
                        a = TT(cadd[:, 2, hs], cadd[:, 1, hs], tot(1), ALU.add, [a])
                        a = TT(cadd[:, 3, hs], cadd[:, 2, hs], tot(2), ALU.add, [a])
                        a = TT(cadd[lowp, 5, hs], cadd[lowp, 5, hs], AR[lowp, :, 64 * 2 + 63], ALU.add, [a])
                        for k, tc in enumerate((0, 1, 2, 3, 2, 3)):
                            b = TT(M[:, :, 64 * k:64 * k + 64], AR[:, :, 64 * tc:64 * tc + 64],
                                   bc(cadd[:, k, hs], 64), ALU.add, [a, tk.get("mfree")])
                        ar_line.free = [b]
                        yield
                        mf = M[:, :, :].rearrange("p h c -> p (h c)")
                        a = TS(mf, mf, 0.0, None, ALU.min, need=[b])
                        a = A(mf, mf, ACT.Exp, [a])
                        yield
                        b = TT(M[:, :, :], M[:, :, :], bc1(CB[:, g, :], 4), ALU.mult, [a, tk["cb", g]])
                        yield
                        ps, free = aux.get()
                        pe.need(*free, b, tk["xd"])
                        for j in range(4):
                            h = 4 * q + j
                            c = slice(64 * h, 64 * h + 64)
                            mm(ps[:, 64 * j:64 * j + 64], M[:, j, 0:128], XD[:, 0, c], True, True)
                            mm(ps[:, 256 + 64 * j:320 + 64 * j], M[:, j, 128:256], XD[:, 0, c], True, False)
                            e = mm(ps[:, 256 + 64 * j:320 + 64 * j], M[:, j, 256:384], XD[:, 1, c], False, True, j == 3)
                        tk["mfree"] = e
                        for t in (0, 1):
                            o = OB[:, t, 256 * q:256 * q + 256]
                            a = TT(o, o, ps[:, 256 * t:256 * t + 256], ALU.add, [e, tk["xd"]])
                            tk["y", q, t] = TT(o, o, Z[t][:, 256 * q:256 * q + 256], ALU.mult, [a, tk["z", q // 2, t]])
                        aux.put(ps, [a])
                        yield
                    scr_line.free = [ta]
                    tk["ob"] = []
                    for t in (0, 1):
                        ss, ms = stat(2), stat(2)
                        for g in (0, 1):
                            o = OB[:, t, 512 * g:512 * g + 512]
                            a = A(Z[t][:, 512 * g:512 * g + 512], o, ACT.Square, [tk["y", 2 * g, t], tk["y", 2 * g + 1, t]],
                                  accum=ss[:, g:g + 1])
                        b = TS(ms, ss, 1.0 / 512, 1e-5, ALU.mult, ALU.add, [a])
                        r, c = rsqrt(ms, [b])
                        for g in (0, 1):
                            o = OB[:, t, 512 * g:512 * g + 512]
                            tk["ob"].append(TS(o, o, r[:, g:g + 1], None, ALU.mult, need=[c]))
                    tk["zfree"] = tk["ob"]
                    yield

                bg_drain()
                fibers.append(ssd())

                def rope_chunk(name, n, base):
                    banks, need = two()
                    tok = gemm((name, l, n), xT, 8, [[(b[:, :], 0, 512)] for b in banks], need)

                    def post():
                        done, bufs = [], []
                        for t in (0, 1):
                            buf, free = ROT.get()
                            a = A(buf[:, :], banks[t][:, :], ACT.Copy, [tok, *free])
                            p3 = banks[t][:, :].rearrange("p (h d) -> p h d", h=8)[:, :, 0:16]
                            d3 = buf[:, :].rearrange("p (h d) -> p h d", h=8)
                            a3 = rt[0][:, :].rearrange("p (h d) -> p h d", h=8)
                            b3 = rt[1][:, :].rearrange("p (h d) -> p h d", h=8)
                            TT(a3, p3, bc1(rope2[:, t, 0:16], 8), ALU.mult, [tok, t_rope2, a, tk.get("rt")])
                            b = TT(b3, p3, bc1(rope2[:, t, 16:32], 8), ALU.mult)
                            mmb.put(banks[t], [b])
                            TT(d3[:, :, 0:8], a3[:, :, 0:8], b3[:, :, 8:16], ALU.subtract, [b])
                            tk["rt"] = TT(d3[:, :, 8:16], a3[:, :, 8:16], b3[:, :, 0:8], ALU.add)
                            done.append(tk["rt"])
                            bufs.append(buf)
                        yield
                        for k in (0, 2):
                            ps, free = aux.get()
                            pe.need(*free, *done)
                            for j in (0, 1):
                                for t in (0, 1):
                                    a = tr(ps[:, 256 * j + 128 * t:256 * j + 128 * t + 128],
                                           bufs[t][:, 128 * (k + j):128 * (k + j) + 128], last=(j == 1 and t == 1))
                            hh = base + 4 * n + k
                            b = A(QKA[:, hh:hh + 2, :].rearrange("p a b -> p (a b)"), ps[:, :], ACT.Copy, [a])
                            aux.put(ps, [b])
                            tk["qka", hh] = tk["qka", hh + 1] = b
                        for t in (0, 1):
                            ROT.put(bufs[t], [a])
                    f = post()
                    next(f)
                    fibers.append(f)

                for n in (0, 1):
                    rope_chunk("qa", n, 0)
                for n in (0, 1):
                    rope_chunk("ka", n, 8)

                def v_chunk(name, n, dst):
                    banks, need = two()
                    tok = gemm((name, l, n), xT, 8, [[(b[:, :], 0, 512)] for b in banks], need)
                    for t in (0, 1):
                        o = dst[:, t, 512 * n:512 * n + 512]
                        a = A(o, banks[t][:, :], ACT.Copy, [tok]) if t else CP(o, banks[t][:, :], [tok])
                        mmb.put(banks[t], [a])
                        tk[name, n, t] = a

                for n in (0, 1):
                    v_chunk("va", n, VAt)
                bg_drain()
                fence2 = [*tk["ob"], tk["mfree"]]
                reg2.close()
                reg3 = ExitStack()
                QKC = sbuf([128, 16, 256], F32, reg3)
                VCt = sbuf([128, 2, 1024], F32, reg3)

                def heads_a():
                    st, w_, pts = {}, {}, {}
                    for s in range(16 + 5):
                        if 0 <= s - 1 < 16:
                            st[s - 1] = st[s - 1](pr)
                        if s >= 5 and s % 2 == 1 and (s - 5) // 2 < 8:
                            h = (s - 5) // 2
                            q, tq = pts[h]
                            v = [VAt[:, t, 128 * h:128 * h + 128] for t in (0, 1)]
                            ps, t0 = values(q, tq, v, 128, pt, [tk["va", h // 4, 0], tk["va", h // 4, 1]])
                            ss, ms = stat(2), stat(2)
                            jb, jf = tmp.get()
                            for t in (0, 1):
                                a = A(jb[:, 128 * t:128 * t + 128], ps[:, 128 * t:128 * t + 128], ACT.Square,
                                      [t0, *jf], accum=ss[:, t:t + 1])
                            tmp.put(jb, [a])
                            b = TS(ms, ss, 1.0 / 128, 1e-5, ALU.mult, ALU.add, [a])
                            r, c = rsqrt(ms, [b])
                            o3 = OA[:, :, 128 * h:128 * h + 128]
                            tk["oa"] = TT(o3, ps[:, 0:256].rearrange("p (t d) -> p t d", t=2), bc(r, 128), ALU.mult,
                                          [c])
                            aux.put(ps, [tk["oa"]])
                        if s >= 4 and s % 2 == 0 and s // 2 - 2 < 8:
                            h = s // 2 - 2
                            pts[h] = turn_probs(w_[h][0], [w_[h][1]], pr, pt)
                        if s >= 2 and s % 2 == 0 and s // 2 - 1 < 8:
                            h = s // 2 - 1
                            p0, ta, d0 = st[2 * h]
                            p1, tb, d1 = st[2 * h + 1]
                            r = stat(4)
                            RCP(r[:, 0:2], d0, [ta])
                            a = RCP(r[:, 2:4], d1, [tb])
                            b = TS(r[:, 2:4], r[:, 2:4], nlam, None, ALU.mult, need=[a, tk["nlam"]])
                            sl = [slice(0, 128), slice(128, 384)]
                            for t in (0, 1):
                                a = TS(p0[:, sl[t]], p0[:, sl[t]], r[:, t:t + 1], None, ALU.mult, need=[b])
                            for t in (0, 1):
                                a = STT(p0[:, sl[t]], p1[:, sl[t]], r[:, 2 + t:3 + t], p0[:, sl[t]], ALU.mult, ALU.add,
                                        [(dve.sem, dve.n - 1)])
                            pr.put(p1, [a])
                            w_[h] = (p0, a)
                        if s < 16:
                            h, m = s // 2, s % 2
                            rr = slice(64 * m, 64 * m + 64)
                            nm, den = stat(2), stat(2)
                            st[s], _ = softmax_scores((QKA[rr, h, :], QKA[rr, 8 + h, :]), 0.125, chunk[:, :],
                                                      t_chunk, [tk["qka", h], tk["qka", 8 + h]], tmp, nm, den)
                        yield

                fibers.append(heads_a())

                def qkc_chunk(name, n, base):
                    banks, need = two()
                    outs = [banks[m // 2][:, 256 * (m % 2):256 * (m % 2) + 256] for m in range(4)]
                    tok = gemm_w((name, l, n), xT, 8, outs, need)
                    for j in (0, 1):
                        hh = base + 4 * n + 2 * j
                        o = QKC[:, hh:hh + 2, :].rearrange("p a b -> p (a b)")
                        a = (A(o, banks[j][:, :], ACT.Copy, [tok, *fence2]) if j
                             else CP(o, banks[j][:, :], [tok, *fence2]))
                        mmb.put(banks[j], [a])
                        tk["qkc", hh] = tk["qkc", hh + 1] = a

                for n in (0, 1):
                    qkc_chunk("qc", n, 0)
                for n in (0, 1):
                    qkc_chunk("kc", n, 8)
                for n in (0, 1):
                    v_chunk("vc", n, VCt)
                bg_drain()
                fence3 = [tk["oa"]]
                G = R1[:, :].rearrange("p (a b) -> p a b", a=2)

                def heads_c():
                    act.put(lambda e: e.preload_act_table_set("natural_log_exp_and_others"))
                    arg, pts = {}, {}
                    st1 = {}
                    for s in range(16 + 5):
                        if 0 <= s - 4 < 16:
                            h = s - 4
                            q, tq = pts[h]
                            v = [VCt[:, t, 64 * h:64 * h + 64] for t in (0, 1)]
                            ps, t0 = values(q, tq, v, 64, pt, [tk["vc", h // 8, 0], tk["vc", h // 8, 1]])
                            tk["oc"] = CP(OC[:, :, 64 * h:64 * h + 64],
                                          ps[:, 0:128].rearrange("p (t d) -> p t d", t=2), [t0, *fence2])
                            aux.put(ps, [tk["oc"]])
                        if 0 <= s - 3 < 16:
                            w, c = arg[s - 3]
                            pts[s - 3] = turn_probs(w, [c], pr, pt)
                        if 0 <= s - 1 < 16:
                            z, w, a = st1[s - 1]
                            a = STT(w[:, :], z[:, :], 0.0, w[:, :], ALU.max, ALU.add, [a])
                            dve.need(a)
                            for t, (lo_, n_) in enumerate(((0, 128), (128, 256))):
                                wv = w[:, lo_:lo_ + n_][:, ::-1]
                                cv = wv
                                dve.need(t_zero)
                                b = dve.go(lambda e, wv=wv, cv=cv, n_=n_: e.tensor_tensor_scan(
                                    cv, wv, zero[:, 0:n_], 0.0, ALU.add, ALU.add))
                            b = TT(z[:, :], z[:, :], w[:, :], ALU.subtract, [b])
                            c = A(w[:, :], z[:, :], ACT.Exp, [b])
                            tmp.put(z, [c])
                            arg[s - 1] = (w, c)
                        if s < 16:
                            rr = slice(64 * (s % 2), 64 * (s % 2) + 64)
                            b = s // 2
                            ps, free = aux.get()
                            pe.need(*free, tk["qkc", b], tk["qkc", 8 + b])
                            qT, kT = QKC[rr, b, :], QKC[rr, 8 + b, :]
                            mm(ps[:, 0:128], qT[:, 0:128], kT[:, 0:128], True, True)
                            t0 = mm(ps[:, 128:384], qT[:, 128:256], kT[:, 0:256], True, True, True)
                            z, f2 = tmp.get()
                            t1 = STT(z[:, :], ps[:, 0:384], 0.125, strict[:, :], ALU.mult, ALU.add, [t0, t_strict, *f2])
                            aux.put(ps, [t1])
                            w, f3 = pr.get()
                            a = A(w[:, :], z[:, :], ACT.Abs, [t1, *f3])
                            a = A(w[:, :], w[:, :], ACT.Exp, [a], scale=-1.0)
                            a = A(w[:, :], w[:, :], ACT.Ln, [a], bias=1.0)
                            st1[s] = (z, w, a)
                        yield

                oT = XT(8, reg3)
                oT.free = fence2
                fibers.append(heads_c())
                t_g = {}
                for c in range(6):
                    if c % 2 == 0:
                        line, tl = vrow((l, f"gb{c // 2}"))
                    banks, need = two()
                    tok = gemm(("g2", l, c), xT, 8, [[(b[:, :], 0, 512)] for b in banks], need)
                    for t in (0, 1):
                        g = G[:, t, 512 * c:512 * c + 512]
                        t_g[c, t] = TT(g, banks[t][:, :], line.buf[:, 512 * (c % 2):512 * (c % 2) + 512], ALU.add,
                                       [tok, tl, *fence3])
                        mmb.put(banks[t], [t_g[c, t]])
                    if c % 2:
                        line.free = [t_g[c, 0], t_g[c, 1]]
                    if c == 3:
                        t_ob2 = to_T([OB[:, t, :] for t in (0, 1)], tk["ob"], 8, oT, col("ssm_norm_g_2", l, 8))
                bg_drain()
                xT.free = [tok]
                for r in (1, 0, 2):
                    for t in (0, 1):
                        g = G[:, t, 1024 * r:1024 * r + 1024]
                        t_g[2 * r, t] = t_g[2 * r + 1, t] = A(g, g, ACT.Sigmoid, [t_g[2 * r + 1, t]])
                dm = [OB[:, t, :] for t in (0, 1)]
                to_T([OA[:, t, :] for t in (0, 1)], [tk["oa"], tk["gs"]], 8, xT, gsub.broadcast_to([128, 8]))
                third = lambda: to_T([OC[:, t, :] for t in (0, 1)], [tk["oc"]], 8, oT)
                branches("br2", l, [(1, 8), (0, 8), (2, 8)], [oT, xT, oT], G, t_g, dm, t_ob2, third)
                product_out("o2", l, then())
                reg3.close()
                rw_line.free = state["fence"]

        def dt_gemm(l, ps, need):
            pe.need(*need)
            key = ("dt", l)
            hi, lo, w, kts, ready = S.take(key)
            assert len(kts) == 8
            pe.need(*ready)
            for t in (0, 1):
                for kt in kts:
                    pe.need(xT.tok[kt][t])
                    o = kt * w
                    for n, (xs, ws) in enumerate(((xT.H, hi), (xT.H, lo), (xT.L, hi))):
                        tok = mm(ps[:, 16 * t:16 * t + 16], xs[:, kt, 128 * t:128 * t + 128], ws[:, o:o + w],
                                 kt == 0 and n == 0, kt == 7 and n == 2, kt == 7 and n == 2)
            S.done(tok)
            return tok

        def store(t, halves):
            ln3(t, halves)

            def f():
                sp.need(*state["x"][t])
                sp.put(lambda e: e.dma_start(out[0, 128 * t:128 * t + 128, :], X[t]).then_inc(s_out, 16))
            return f

        ffn("f2", 1, enter_final())
        for l in (0, 1):
            ffn("F1", l, enter_ln((l, "ln1_g"), (l, "ln1_b")))
            mixer2(l, lambda: enter_ln((l, "ln2_g"), (l, "ln2_b")))
            ln3 = enter_ln((l, "ln3_g"), (l, "ln3_b"))
            ffn("F2", l, ln3 if l == 0 else store)
        state["second"]()
        sp.need((s_out, 32), (scr_line.sem, 16 * scr_line.n))
        assert S.u == len(pieces)

        block = ctx.enter_context(nc.Block())
        block.sync(sp.run)
        block.scalar(act.run)
        block.vector(dve.run)
        block.gpsimd(pool.run)
        block.tensor(pe.run)


def constants():
    f = np.float32
    q = np.arange(128)[:, None]
    k = np.arange(128)[None, :]

    def three(fn):
        return np.concatenate([fn(q, k), fn(q + 128, k), fn(q + 128, k + 128)], axis=1)

    bias = np.zeros((7, 128, 384), f)
    allowed = [lambda a, b: (a >= b) & (a - b <= 128), lambda a, b: (a >= b) & ((a - b) % 4 == 0),
               lambda a, b: (a >= b) & ((a - b) % 16 == 0), lambda a, b: a >= b]
    for i, ok in enumerate(allowed):
        bias[i] = three(lambda a, b: np.where(ok(a, b), (b - a).astype(f), f(NEG)).astype(f))
    bias[4] = three(lambda a, b: np.where(a >= b, f(0), f(NEG)))
    bias[5] = three(lambda a, b: np.where(a > b, f(0), f(NEG)))
    bias[6] = three(lambda a, b: np.where(b // 64 <= a // 64, f(0), f(NEG)))
    msk = np.zeros((128, 512), f)
    msk[:, 0:128] = (k >= q)
    msk[:, 128:256] = 1.0
    msk[:, 256:384] = (k >= q)
    msk[:, 384:512] = (k >= q) & (k // 64 == q // 64)
    pos = np.arange(256, dtype=f)
    inv1 = f(10000.0) ** (-np.arange(0, 32, 2, dtype=f) / f(32))
    a1 = (pos[:, None] * inv1[None, :]).astype(f)
    inv2 = f(500000.0) ** (-np.arange(8, dtype=f) * f(2.0) / f(16))
    a2 = (pos[:, None] * inv2[None, :]).astype(f)
    c1, s1, c2, s2 = np.cos(a1), np.sin(a1), np.cos(a2), np.sin(a2)
    rope = np.concatenate([c1, c1, s1, s1, c2, c2, s2, s2], axis=1).astype(f)
    rope = np.ascontiguousarray(rope.reshape(2, 128, 96).transpose(1, 0, 2))
    return np.eye(128, dtype=f), bias, msk, rope


def kernel(**inputs):
    import numpy as _np
    import concourse.bacc as _bacc
    from concourse import mybir as _mybir
    from concourse.bass_utils import run_bass_kernel_spmd as _run

    a = {k: _np.ascontiguousarray(v) for k, v in inputs.items()}
    blocks = place_pieces()
    pieces = plan()
    total = sum(128 * used for _, used in blocks)
    wpack = _np.empty(total, _np.float32)
    at = 0
    for ps, used in blocks:
        dst = wpack[at:at + 128 * used].reshape(128, used)
        at += 128 * used
        for i, off, n in ps:
            _, width, kts = pieces[i]
            for idx, kt, ranges in kts:
                for name, c0, c1 in ranges:
                    dst[:, off:off + c1 - c0] = a[name][idx][128 * kt:128 * kt + 128, c0:c1]
                    off += c1 - c0
    cols = _np.empty((128, NCOLS), _np.float32)
    for name, l, c, n in _COLS:
        v = a[name][l]
        if name == "ssm_conv_w_2":
            cols[:, c:c + n] = v.reshape(4, 12, 128).transpose(2, 1, 0).reshape(128, 48)
        else:
            cols[:, c:c + n] = v.reshape(n, 128).T
    rows = _np.concatenate([a["diff_lambda_2"].reshape(2, 256), a["ssm_dt_bias_2"], a["ssm_A_log_2"], a["ssm_D_2"]],
                           axis=1)
    vr = [a["final_norm"]]
    for l in (0, 1):
        vr += [a["ln1_g_2"][l], a["ln1_b_2"][l], a["gate_bias_2"][l, 0], a["gate_bias_2"][l, 1],
               a["gate_bias_2"][l, 2], a["ln2_g_2"][l], a["ln2_b_2"][l], a["ln3_g_2"][l], a["ln3_b_2"][l]]
    ident, bias, msk, rope = constants()
    arrays = {"in_x": a["x"], "in_w": wpack, "in_cols": cols, "in_rows": _np.ascontiguousarray(rows),
              "in_vrows": _np.stack(vr), "in_ident": ident, "in_bias": bias, "in_msk": msk, "in_rope": rope}
    nc = _bacc.Bacc("TRN2", target_bir_lowering=False, num_devices=1)
    args = [nc.dram_tensor(k, v.shape, _mybir.dt.from_np(v.dtype), kind="ExternalInput").ap()
            for k, v in arrays.items()]
    scratch = nc.dram_tensor("scratch", (2, 16, 256), _mybir.dt.float32, kind="Internal").ap()
    out = nc.dram_tensor("out_0", (1, 256, 1024), _mybir.dt.float32, kind="ExternalOutput").ap()
    bass_two_blocks(nc, *args, scratch, out)
    r = _run(nc, [arrays], core_ids=[0])
    return r.results[0]["out_0"]
```

```python
import math
from collections import deque
from contextlib import ExitStack

import numpy as np

import concourse.bass as bass
from concourse import mybir

F32 = mybir.dt.float32
F32R = mybir.dt.float32r
ACT = mybir.ActivationFunctionType
ALU = mybir.AluOpType
AX_X = mybir.AxisListType.X

D = 1024
DFF = 2816
NCH = DFF // 256
NEG = -1e30
PIECE = 1024
BLOCK = 2048
NRAW = 3
NHL = 5
SKEW = 4
QA, KA, VA, ZB, XBC, DTB, QC, KC, VC, GP = (0, 1024, 2048, 3072, 4096, 5632, 5648, 6672, 7696, 8720)
ALPHA = 4.0 ** 0.25
SLOPES = [2.0 ** (-8.0 * i / 18) for i in range(1, 19)]


def plan():
    pieces = []

    def gemm(key, idx, nk, ranges):
        width = sum(c1 - c0 for _, c0, c1 in ranges)
        per = PIECE // width
        for k in range(0, nk, per):
            pieces.append((key, width, [(idx, kt, ranges) for kt in range(k, min(nk, k + per))]))

    def ffn(key, l, gate, up, shift, down):
        for c in range(NCH):
            gemm((key, "up", l, c), (l,), 8,
                 [(gate, 256 * c, 256 * c + 256), (up, shift + 256 * c, shift + 256 * c + 256)])
        gemm((key, "down", l), (l,), 22, [(down, 0, 1024)])

    for l in (0, 1):
        ffn("f1", l, "ffn1_w_gate", "ffn1_w_up", 0, "ffn1_w_down")
        gemm(("mla", l), (l,), 8, [("w_in", 0, 416)])
        mo, di = 416, 416 + 1152
        for c in range(4):
            gemm(("qk1", l, c), (l,), 8, QK1[c])
            if c == 0:
                for j in (0, 1):
                    gemm(("uq", l, j), (l,), 2, [("w_uq", 288 * j, 288 * j + 288)])
                for j in (0, 1):
                    gemm(("ukv", l, j), (l,), 1, [("w_ukv", 384 * j, 384 * j + 384)])
        gemm(("v1", l, 0), (l,), 8, [("w_in", mo + 768, mo + 1152)])
        gemm(("qk1", l, 4), (l,), 8, QK1[4])
        for j in (0, 1):
            gemm(("v1", l, 1 + j), (l,), 8, [("w_in", di + 1536 + 384 * j, di + 1920 + 384 * j)])
        for c in range(6):
            gemm(("g1", l, c), (l,), 8, [("w_in", 3872 + 512 * c, 4384 + 512 * c)])
        for r, name, nk in BR1:
            for n in (0, 1):
                gemm(("br1", l, r, n), (l,), nk, [(name, 512 * n, 512 * n + 512)])
        for n in (0, 1):
            gemm(("o1", l, n), (l,), 8, [("w_out", 512 * n, 512 * n + 512)])
        ffn("f2", l, "ffn2_w_gate", "ffn2_w_up", 0, "ffn2_w_down")
    for l in (0, 1):
        ffn("F1", l, "ffn1_w_in_2", "ffn1_w_in_2", DFF, "ffn1_w_out_2")
        w = "w_mix_in_2"
        for n in (0, 1):
            gemm(("z", l, n), (l,), 8, [(w, ZB + 512 * n, ZB + 512 * n + 512)])
        gemm(("dt", l), (l,), 8, [(w, DTB, DTB + 16)])
        for c in (2, 0, 1):
            gemm(("xbc", l, c), (l,), 8, [(w, XBC + 512 * c, XBC + 512 * c + 512)])
        for key, at in (("qa", QA), ("ka", KA), ("va", VA), ("qc", QC), ("kc", KC), ("vc", VC)):
            for n in (0, 1):
                gemm((key, l, n), (l,), 8, [(w, at + 512 * n, at + 512 * n + 512)])
        for c in range(6):
            gemm(("g2", l, c), (l,), 8, [(w, GP + 512 * c, GP + 512 * c + 512)])
        for r in (1, 0, 2):
            for n in (0, 1):
                gemm(("br2", l, r, n), (l, r), 8, [("w_branch_2", 512 * n, 512 * n + 512)])
        for n in (0, 1):
            gemm(("o2", l, n), (l,), 8, [("w_mix_out_2", 512 * n, 512 * n + 512)])
        ffn("F2", l, "ffn2_w_in_2", "ffn2_w_in_2", DFF, "ffn2_w_out_2")
    return pieces


BR1 = [(0, "w_br_mla", 3), (2, "w_br_dil", 2), (1, "w_br_moba", 3)]
_Q = [("w_in", 416 + 128 * i) for i in range(6)] + [("w_in", 1568 + 128 * i) for i in range(12)]
QK1 = [[(n, c, c + 128) for n, c in _Q[4 * i:4 * i + 4]] for i in range(5)]

COLS = {}


def cols_plan():
    out, at = [], 0
    for l in (0, 1):
        for name, n in (("ffn1_norm", 8), ("mix_norm", 8), ("q_norm", 2), ("kv_norm", 1), ("ffn2_norm", 8),
                        ("diff_subln_g_2", 1), ("ssm_norm_g_2", 8), ("ssm_conv_w_2", 48), ("ssm_conv_b_2", 12),
                        ("ssm_dt_bias_2", 1), ("ssm_A_log_2", 1)):
            out.append((name, l, at, n))
            COLS[(name, l)] = at
            at += n
    return out, at


_COLS, NCOLS = cols_plan()
VROWS = ["final"] + [(l, n) for l in (0, 1) for n in
                     ("ln1_g", "ln1_b", "gb0", "gb1", "gb2", "ln2_g", "ln2_b", "ln3_g", "ln3_b")]


def place_pieces():
    blocks, cur, used = [], [], 0
    for i, (key, width, kts) in enumerate(plan()):
        n = width * len(kts)
        if used + n > BLOCK or i == 1:
            blocks.append((cur, used))
            cur, used = [], 0
        cur.append((i, used, n))
        used += n
    blocks.append((cur, used))
    return blocks


class Engine:
    def __init__(self, sem):
        self.sem, self.queue, self.n, self.met = sem, [], 0, {}

    def need(self, *tokens):
        for t in tokens:
            if t is None:
                continue
            if isinstance(t, (list, deque)):
                self.need(*t)
                continue
            sem, v = t
            if self.met.get(id(sem), 0) < v:
                self.met[id(sem)] = v
                self.queue.append(lambda e, sem=sem, v=v: e.wait_ge(sem, v))

    def go(self, fn):
        self.n += 1
        self.queue.append(lambda e, fn=fn: fn(e).then_inc(self.sem, 1))
        return (self.sem, self.n)

    def put(self, fn):
        self.queue.append(fn)

    def run(self, e):
        for fn in self.queue:
            fn(e)


class Pool:

    def __init__(self, bufs):
        self.free = deque((b, []) for b in bufs)

    def get(self):
        return self.free.popleft()

    def put(self, buf, tokens):
        self.free.append((buf, list(tokens)))


class Line:

    def __init__(self, sem, buf):
        self.sem, self.buf, self.n, self.free = sem, buf, 0, []


def bass_two_blocks(nc: bass.Bass, x, wpack, cols, rows, vrows, ident_d, bias_d, msk_d, rope_d, scratch, out):
    ctx = ExitStack()
    with ctx:
        counter = [0]

        def sbuf(shape, dt=F32, scope=ctx):
            counter[0] += 1
            return scope.enter_context(nc.sbuf_tensor(f"t{counter[0]}", shape, dt))

        def sem(name):
            return ctx.enter_context(nc.semaphore(name))

        pe, act, dve, pool = (Engine(sem(n)) for n in ("s_pe", "s_act", "s_dve", "s_pool"))
        sp = Engine(sem("s_sp"))
        psum = [ctx.enter_context(nc.psum_tensor(f"ps{i}", [128, 512], F32)) for i in range(8)]
        mmb, aux = Pool(psum[0:4]), Pool(psum[4:8])

        RAW = [sbuf([128, BLOCK]) for _ in range(NRAW)]
        HI = [sbuf([128, PIECE], F32R) for _ in range(NHL)]
        LO = [sbuf([128, PIECE], F32R) for _ in range(NHL)]
        X = [sbuf([128, D])[:, :] for _ in range(2)]
        XNB = sbuf([128, 2, D])
        XN = [XNB[:, t, :] for t in (0, 1)]
        ident = sbuf([128, 128])
        colt = sbuf([128, NCOLS])
        STAT = sbuf([128, 512])
        stat_at = [0]

        def stat(n):
            if stat_at[0] + n > 512:
                stat_at[0] = 0
            a = STAT[:, stat_at[0]:stat_at[0] + n]
            stat_at[0] += n
            return a

        class XT:
            def __init__(self, nk, scope=ctx):
                self.H = sbuf([128, nk, 256], F32R, scope)
                self.L = sbuf([128, nk, 256], F32R, scope)
                self.tok = [[None, None] for _ in range(nk)]
                self.free = []

        xT = XT(8)
        phalf = sbuf([128, 2])
        t_half = pool.go(lambda e: e.memset(phalf[:, :], -0.5))

        def A(out, in_, func, need=(), scale=1.0, bias=None, accum=None):
            act.need(*need)
            kw = {}
            if bias is not None:
                kw["bias"] = bias
            if accum is not None:
                kw["accum_out"] = accum
            return act.go(lambda e: e.activation(out, in_, func, scale=scale, **kw))

        def TT(out, a, b, op, need=(), eng=None):
            g = eng or dve
            g.need(*need)
            return g.go(lambda e: e.tensor_tensor(out, a, b, op))

        def TS(out, a, s1, s2, op0, op1=None, need=()):
            dve.need(*need)
            if op1 is None:
                return dve.go(lambda e: e.tensor_scalar(out, a, s1, None, op0))
            return dve.go(lambda e: e.tensor_scalar(out, a, s1, s2, op0, op1))

        def STT(out, a, s, b, op0, op1, need=()):
            dve.need(*need)
            return dve.go(lambda e: e.scalar_tensor_tensor(out=out, in0=a, scalar=s, in1=b, op0=op0, op1=op1))

        def RED(out, a, op, need=(), negate=None):
            dve.need(*need)
            return dve.go(lambda e: e.tensor_reduce(out, a, AX_X, op, negate=negate))

        def RCP(out, a, need=()):
            dve.need(*need)
            return dve.go(lambda e: e.reciprocal(out, a))

        def CP(out, a, need=()):
            dve.need(*need)
            return dve.go(lambda e: e.tensor_copy(out, a))

        def mm(out, l, r, start, stop, last=False, skip=False):
            fn = lambda e: e.matmul(out, l, r, start=start, stop=stop, skip_group_check=skip)
            return pe.go(fn) if last else pe.put(fn)

        def tr(out, in_, last=False):
            k = in_.shape[0]
            fn = lambda e: e.transpose(out, in_, ident[0:k, 0:k])
            return pe.go(fn) if last else pe.put(fn)

        def rsqrt(var, need):
            n = var.shape[-1]
            r = stat(n)
            pool.need(t_half, *need)
            return r, pool.go(lambda e: e.tensor_tensor(r, var, phalf[:, 0:n], ALU.pow))

        def bc(ap, n):
            return ap.unsqueeze(2).broadcast_to([ap.shape[0], ap.shape[1], n])

        def bc1(ap, n):
            return ap.unsqueeze(1).broadcast_to([ap.shape[0], n, ap.shape[1]])

        def once(out, in_, name):
            s = sem(name)
            sp.put(lambda e: e.dma_start(out, in_).then_inc(s, 16))
            return (s, 16)

        def load(line, out, in_, need=()):
            sp.need(*line.free, *need)
            line.free = []
            line.n += 1
            sp.put(lambda e: e.dma_start(out, in_).then_inc(line.sem, 16))
            return (line.sem, 16 * line.n)

        pieces = plan()
        blocks = place_pieces()
        dsem = [sem(f"s_w{i}") for i in range(NRAW)]
        where = {}
        offs, at = [], 0
        for b, (ps, used) in enumerate(blocks):
            offs.append(at)
            at += 128 * used
            for i, off, n in ps:
                where[i] = (b, off, n)

        class Stream:
            u = 0
            loaded = 0
            split = [0, 0]
            on_pool = set()
            t_raw = {}
            t_hi = {}
            t_lo = {}
            t_pe = {}

            def load(self):
                b = self.loaded
                if b >= len(blocks):
                    return
                if b >= NRAW:
                    for i, _, _ in blocks[b - NRAW][0]:
                        sp.need(self.t_hi[i], self.t_lo[i])
                used = blocks[b][1]
                src = wpack[offs[b]:offs[b] + 128 * used].rearrange("(p c) -> p c", p=128)
                dst = RAW[b % NRAW][:, 0:used]
                sp.put(lambda e: e.dma_start(dst, src).then_inc(dsem[b % NRAW], 16))
                self.t_raw[b] = (dsem[b % NRAW], 16 * (b // NRAW + 1))
                self.loaded += 1

            def halve(self, i, part):
                b, off, n = where[i]
                raw = RAW[b % NRAW][:, off:off + n]
                hi, lo = HI[i % NHL][:, 0:n], LO[i % NHL][:, 0:n]
                if part == 0:
                    self.t_hi[i] = A(hi, raw, ACT.Copy, [self.t_raw[b], self.t_pe.get(i - NHL)])
                else:
                    self.t_lo[i] = TT(lo, raw, hi.bitcast(F32), ALU.subtract,
                                      [self.t_raw[b], self.t_hi[i], self.t_pe.get(i - NHL)],
                                      pool if i in self.on_pool else dve)

            def relieve(self):
                self.on_pool |= {self.u + NHL - 1, self.u + NHL + 1, self.u + NHL + 2}
                if self.split[0] > self.split[1] == self.u + NHL - 1:
                    self.halve(self.split[1], 1)
                    self.split[1] += 1
                    self.ahead()

            def ahead(self):
                while self.loaded < len(blocks) and (self.loaded < NRAW or
                                                     blocks[self.loaded - NRAW][0][-1][0] in self.t_lo):
                    self.load()

            def halves_to(self, hi, lo):
                for part, upto in ((0, hi), (1, lo)):
                    while self.split[part] < min(len(pieces), upto):
                        self.halve(self.split[part], part)
                        self.split[part] += 1
                        self.ahead()

            def take(self, key, j=0):
                i = self.u + j
                assert pieces[i][0] == key, (pieces[i][0], key)
                self.ahead()
                self.halves_to(self.u + NHL, self.u + NHL - 1)
                assert self.split[1] > i
                _, width, kts = pieces[i]
                return HI[i % NHL], LO[i % NHL], width, [kt for _, kt, _ in kts], [self.t_hi[i], self.t_lo[i]]

            def done(self, tok):
                self.t_pe[self.u] = tok
                self.u += 1
                bg_step()

        S = Stream()
        fibers = deque()

        chain = deque()

        def bg_step():
            while chain:
                try:
                    next(chain[0])
                    break
                except StopIteration:
                    chain.popleft()
            for f in list(fibers):
                try:
                    next(f)
                except StopIteration:
                    fibers.remove(f)

        def bg_drain():
            while fibers or chain:
                bg_step()

        def gemm(key, xt, nk, outs, need=(), mid=None, pre=None, post=None):

            def rows(piece, t):
                hi, lo, w, kts, ready = piece
                pe.need(*ready, need[t])
                sl = slice(128 * t, 128 * t + 128)
                for i, kt in enumerate(kts):
                    pe.need(xt.tok[kt][t])
                    o = i * w
                    for n, (xs, ws) in enumerate(((xt.H, hi), (xt.H, lo), (xt.L, hi))):
                        for ap, c0, c1 in outs[t]:
                            last = n == 2 and i == len(kts) - 1 and c1 == w
                            tok = mm(ap, xs[:, kt, sl], ws[:, o + c0:o + c1], kt == 0 and n == 0,
                                     kt == nk - 1 and n == 2, last)
                return tok

            total = sum(1 for p in pieces[S.u:S.u + 32] if p[0] == key)
            late = min(SKEW, total) if mid else 0
            toks = [None, None]
            for _ in range(total - late):
                piece = S.take(key)
                toks = [rows(piece, t) for t in (0, 1)]
                S.done(toks[1])
            if late:
                for j in range(late):
                    if pre and j == late - 1:
                        pre()
                    toks[0] = rows(S.take(key, j), 0)
                if post and key[0] not in ("f1", "f2", "o1"):
                    S.relieve()
                mid(toks[0])
                for j in range(late):
                    if post and j == late - 1:
                        post()
                    toks[1] = rows(S.take(key), 1)
                    S.done(toks[1])
            return toks

        def gemm_w(key, xt, nk, outs, need=()):
            pe.need(*need)
            seen = 0
            while seen < nk:
                hi, lo, w, kts, ready = S.take(key)
                pe.need(*ready)
                for i, kt in enumerate(kts):
                    pe.need(*xt.tok[kt])
                    for m, ap in enumerate(outs):
                        o = i * w + 128 * m
                        for n, (ws, xs) in enumerate(((hi, xt.H), (hi, xt.L), (lo, xt.H))):
                            last = n == 2 and m == len(outs) - 1 and i == len(kts) - 1
                            tok = mm(ap, ws[:, o:o + 128], xs[:, kt, :], kt == 0 and n == 0 and m % 2 == 0,
                                     kt == nk - 1 and n == 2, last, skip=True)
                seen += len(kts)
                S.done(tok)
            return [tok, tok]

        def to_T(src, toks, nk, xt, gain=None, at=0):
            last = None
            for k in range(0, nk, 2):
                m = min(2, nk - k)
                ps, free = aux.get()
                pe.need(*free, *toks)
                for j in range(m):
                    for t in (0, 1):
                        last = tr(ps[:, 256 * j + 128 * t:256 * j + 128 * t + 128],
                                  src[t][:, 128 * (k + j):128 * (k + j) + 128], last=(j == m - 1 and t == 1))
                if gain is None:
                    hi = xt.H[:, at + k:at + k + m, :].rearrange("p a b -> p (a b)")
                    lo = xt.L[:, at + k:at + k + m, :].rearrange("p a b -> p (a b)")
                    t1 = A(hi, ps[:, 0:256 * m], ACT.Copy, [last, xt.free])
                    t2 = TT(lo, ps[:, 0:256 * m], hi.bitcast(F32), ALU.subtract, [last, t1, xt.free])
                else:
                    for j in range(m):
                        t1 = A(xt.H[:, at + k + j, :], ps[:, 256 * j:256 * j + 256], ACT.Copy, [last, xt.free],
                               scale=gain[:, k + j:k + j + 1])
                    for j in range(m):
                        hi, lo = xt.H[:, at + k + j, :], xt.L[:, at + k + j, :]
                        g = gain[:, k + j:k + j + 1]
                        p = ps[:, 256 * j:256 * j + 256]
                        t2 = STT(lo, p, g, hi.bitcast(F32), ALU.mult, ALU.subtract, [last, t1, xt.free])
                for j in range(m):
                    xt.tok[at + k + j] = [[t1, t2], [t1, t2]]
                aux.put(ps, [t1, t2])
            return last

        def turn(src, toks, t, ks, xt, gain=None):
            sl = slice(128 * t, 128 * t + 128)
            m = 2
            for k0 in range(ks[0], ks[-1], m):
                ps, free = aux.get()
                pe.need(*free, *toks)
                for j in range(m):
                    last = tr(ps[:, 128 * j:128 * j + 128], src[:, 128 * (k0 + j):128 * (k0 + j) + 128],
                              last=(j == m - 1))
                if gain is None:
                    p3 = ps[:, 0:128 * m].rearrange("p (a b) -> p a b", a=m)
                    hi, lo = xt.H[:, k0:k0 + m, sl], xt.L[:, k0:k0 + m, sl]
                    t1 = A(hi, p3, ACT.Copy, [last, xt.free])
                    t2 = TT(lo, p3, hi.bitcast(F32), ALU.subtract, [last, t1, xt.free])
                else:
                    for j in range(m):
                        t1 = A(xt.H[:, k0 + j, sl], ps[:, 128 * j:128 * j + 128], ACT.Copy, [last, xt.free],
                               scale=gain[:, k0 + j:k0 + j + 1])
                    for j in range(m):
                        t2 = STT(xt.L[:, k0 + j, sl], ps[:, 128 * j:128 * j + 128], gain[:, k0 + j:k0 + j + 1],
                                 xt.H[:, k0 + j, sl].bitcast(F32), ALU.mult, ALU.subtract, [last, t1, xt.free])
                for j in range(m):
                    xt.tok[k0 + j][t] = [t1, t2]
                aux.put(ps, [t1, t2])
            return last

        def col(name, l, n):
            return colt[:, COLS[(name, l)]:COLS[(name, l)] + n]

        state = {"x": [[], []], "xn": [], "rstd": [None, None], "later": [], "second": None, "early": False}

        t_id = once(ident[:, :], ident_d, "s_id")
        load_x = lambda t: [once(X[t][:, :], x[0, 128 * t:128 * t + 128, :], f"s_x{t}")]
        state["x"][0] = load_x(0)
        t_col = once(colt[:, :], cols, "s_col")
        S.load()
        state["x"][1] = load_x(1)
        S.ahead()

        def mean_square(t, halves, eps=1e-6):
            ss, ms = stat(2), stat(1)
            for n in (0, 1):
                a = A(XN[t][:, 512 * n:512 * n + 512], X[t][:, 512 * n:512 * n + 512], ACT.Square,
                      [halves[n], state["xn"]], accum=ss[:, n:n + 1])
            b = TS(ms, ss[:, 0:1], ss[:, 1:2], 1.0 / D, ALU.add, ALU.mult, [a])
            b = TS(ms, ms, eps, None, ALU.add, need=[b])
            return rsqrt(ms, [b])

        VR = [Line(sem(f"s_vr{i}"), None) for i in range(2)]
        vr_at = [0]

        def vrow(name):
            line = VR[vr_at[0] % 2]
            vr_at[0] += 1
            i = VROWS.index(name)
            return line, load(line, line.buf[:, :], vrows[i:i + 1, :].broadcast_to([128, D]))

        def enter_scaled(gain):
            def f(t, halves):
                state["rstd"][t] = mean_square(t, halves)

                state["early"] = True

                def turned():
                    for n in (0, 1):
                        a = turn(X[t], [halves[n], t_id, t_col], t, range(4 * n, 4 * n + 4), xT, gain)
                    state["x"][t] = [*halves, a]
                return turned
            return f

        def enter_rms(gain):
            def f(t, halves):
                r, c = mean_square(t, halves)
                cols_ = [slice(512 * n, 512 * n + 512) for n in (0, 1)]
                a = [TS(XN[t][:, cs], X[t][:, cs], r, None, ALU.mult, need=[c]) for cs in cols_]
                state["rstd"][t] = None
                state["x"][t] = [*halves, *a]
                state["early"] = False

                def turned():
                    for n in (0, 1):
                        b = turn(XN[t], [a[n], t_id, t_col], t, range(4 * n, 4 * n + 4), xT, gain)
                    state["xn"] = [b]
                return turned
            return f

        def turn_x(t, a):
            state["early"] = False

            def turned():
                for n in (0, 1):
                    b = turn(X[t], [a[n], t_id], t, range(4 * n, 4 * n + 4), xT)

                def scale_x():
                    state["x"][t] = [TS(X[t], X[t], ALPHA, None, ALU.mult, need=[*a, b])]
                state["later"].append(scale_x)
            return turned

        def enter_final():
            line, tl = vrow("final")

            def f(t, halves):
                r, c = mean_square(t, halves)
                state["rstd"][t] = None
                a = []
                for n in (0, 1):
                    cs = slice(512 * n, 512 * n + 512)
                    a.append(STT(X[t][:, cs], X[t][:, cs], r, line.buf[:, cs], ALU.mult, ALU.mult, [c, tl]))
                line.free.append(a[1])
                return turn_x(t, a)
            return f

        def enter_ln(g, b):
            (lg, tg), (lb, tb) = vrow(g), vrow(b)

            def f(t, halves):
                st_, mv, ve = stat(12), stat(2), stat(1)
                for n in (0, 1):
                    dve.need(halves[n])
                    a = dve.go(lambda e, n=n: e.bn_stats(st_[:, 6 * n:6 * n + 6], X[t][:, 512 * n:512 * n + 512]))
                dve.need(a)
                a = dve.go(lambda e: e.bn_aggr(mv, st_))
                c = TS(ve, mv[:, 1:2], 1e-5, None, ALU.add, need=[a])
                r, c = rsqrt(ve, [c])
                done = []
                cols_ = [slice(512 * n, 512 * n + 512) for n in (0, 1)]
                for cs in cols_:
                    b = STT(X[t][:, cs], X[t][:, cs], mv[:, 0:1], lg.buf[:, cs], ALU.subtract, ALU.mult, [a, tg])
                for cs in cols_:
                    done.append(STT(X[t][:, cs], X[t][:, cs], r, lb.buf[:, cs], ALU.mult, ALU.add, [b, c, tb]))
                lg.free.append(done[1])
                lb.free.append(done[1])
                state["x"][t] = done
                state["rstd"][t] = None
                return turn_x(t, done)
            return f

        def between(tok=None):
            if state["second"]:
                state["second"]()
            state["second"] = None

        def between_early():
            if state["early"]:
                between()

        def run_later():
            for f in state["later"]:
                f()
            state["later"] = []

        def swiglu(key, l, hT, sring, update):
            def act_half(hb, free, t, bank, tok):
                rs = state["rstd"][t]
                if rs is None:
                    a = A(hb[:, t, :], bank[:, 0:256], ACT.Silu, [tok, *free])
                    th = TT(hb[:, t, :], hb[:, t, :], bank[:, 256:512], ALU.mult, [a, tok])
                else:
                    r, tr_ = rs
                    a = A(hb[:, t, :], bank[:, 0:256], ACT.Silu, [tok, tr_, *free], scale=r)
                    th = STT(hb[:, t, :], bank[:, 256:512], r, hb[:, t, :], ALU.mult, ALU.mult, [a, tok, tr_])
                mmb.put(bank, [th])
                return th

            def turn_later(c, hb, th):
                yield
                ps, free = aux.get()
                pe.need(*free, *th)
                for j in (0, 1):
                    for t in (0, 1):
                        last = tr(ps[:, 256 * j + 128 * t:256 * j + 128 * t + 128],
                                  hb[:, t, 128 * j:128 * j + 128], last=(j == 1 and t == 1))
                hi = hT.H[:, 2 * c:2 * c + 2, :].rearrange("p a b -> p (a b)")
                lo = hT.L[:, 2 * c:2 * c + 2, :].rearrange("p a b -> p (a b)")
                t1 = A(hi, ps[:, :], ACT.Copy, [last])
                t2 = TT(lo, ps[:, :], hi.bitcast(F32), ALU.subtract, [last, t1])
                hT.tok[2 * c] = hT.tok[2 * c + 1] = [[t1, t2], [t1, t2]]
                aux.put(ps, [t1, t2])
                sring.put(hb, [last])

            for c in range(NCH):
                banks, need = two()
                hb, free = sring.get()
                th = []

                def mid(tok):
                    th.append(act_half(hb, free, 0, banks[0], tok))
                    between()

                toks = gemm((key, "up", l, c), xT, 8, [[(b[:, :], 0, 512)] for b in banks], need,
                            mid if c == 0 else None, pre=between_early)
                for t in range(len(th), 2):
                    th.append(act_half(hb, free, t, banks[t], toks[t]))
                f = turn_later(c, hb, th)
                next(f)
                fibers.append(f)
                if c == 1:
                    run_later()
            xT.free = [toks[1]]
            (b01, n01), (b23, n23) = two(), two()
            banks = [b01, b23]
            outs = [[(banks[t][n][:, :], 512 * n, 512 * n + 512) for n in (0, 1)] for t in (0, 1)]
            turned = []

            def post():
                if state["early"]:
                    turned.pop()()

            toks = gemm((key, "down", l), hT, 22, outs, [n01, n23],
                        lambda tok: turned.append(update(0, banks[0], tok)), post=post)
            state["fence"] = [toks[1]]
            if turned:
                turned[0]()
            state["second"] = update(1, banks[1], toks[1])

        def two():
            (a, f), (b, g) = mmb.get(), mmb.get()
            return [a, b], [f, g]

        def one():
            a, f = mmb.get()
            return [a], f

        def ffn(key, l, then):
            with ExitStack() as ph:
                hT = XT(22, ph)
                sring = Pool([sbuf([128, 2, 256], F32, ph) for _ in range(2)])

                def update(t, banks, tok):
                    halves = []
                    for n in (0, 1):
                        xs = X[t][:, 512 * n:512 * n + 512]
                        halves.append(STT(xs, banks[n][:, :], 0.5, xs, ALU.mult, ALU.add, [tok, *state["x"][t]]))
                        mmb.put(banks[n], [halves[n]])
                    return then(t, halves)

                swiglu(key, l, hT, sring, update)

        def product_out(key, l, then, half=1.0):
            halves = [[], []]
            for n in (0, 1):
                banks, need = two()

                def update(t, tok):
                    xs = X[t][:, 512 * n:512 * n + 512]
                    halves[t].append(STT(xs, banks[t][:, :], half, xs, ALU.mult, ALU.add, [tok, *state["x"][t]]))
                    mmb.put(banks[t], [halves[t][-1]])

                turned = []

                def mid(tok):
                    update(0, tok)
                    turned.append(then(0, halves[0]))

                def post():
                    if state["early"]:
                        turned.pop()()

                toks = gemm((key, l, n), xT, 8, [[(b[:, :], 0, 512)] for b in banks], need, mid if n else None,
                            post=post)
                state["fence"] = [toks[1]]
                if n == 0:
                    update(0, toks[0])
                elif turned:
                    turned[0]()
                update(1, toks[1])
            state["second"] = then(1, halves[1])

        def softmax_scores(S_mm, scale, bias, bias_tok, need, tmp, nm, den, slope=1.0):
            ps, free = aux.get()
            pe.need(*free, *need)
            qT, kT = S_mm
            mm(ps[:, 0:128], qT[:, 0:128], kT[:, 0:128], True, True)
            t0 = mm(ps[:, 128:384], qT[:, 128:256], kT[:, 0:256], True, True, True)
            sm, f2 = tmp.get()
            t1 = STT(sm[:, :], ps[:, 0:384], scale / slope, bias, ALU.mult, ALU.add, [t0, bias_tok, *f2])
            aux.put(ps, [t1])
            RED(nm[:, 0:1], sm[:, 0:128], ALU.max, [t1], negate=True)
            t2 = RED(nm[:, 1:2], sm[:, 128:384], ALU.max, negate=True)
            if slope != 1.0:
                t2 = TS(nm, nm, slope, None, ALU.mult, need=[t2])

            def exps(pr):
                p, f3 = pr.get()
                A(p[:, 0:128], sm[:, 0:128], ACT.Exp, [t2, *f3], scale=slope, bias=nm[:, 0:1], accum=den[:, 0:1])
                t3 = A(p[:, 128:384], sm[:, 128:384], ACT.Exp, scale=slope, bias=nm[:, 1:2], accum=den[:, 1:2])
                tmp.put(sm, [t3])
                return p, t3, den
            return exps, t1

        def turn_probs(p, need, pr, pt):
            ps, free = aux.get()
            pe.need(*free, *need)
            for j in range(3):
                t0 = tr(ps[:, 128 * j:128 * j + 128], p[:, 128 * j:128 * j + 128], last=(j == 2))
            pr.put(p, [t0])
            q, f = pt.get()
            t1 = A(q[:, :], ps[:, 0:384], ACT.Copy, [t0, *f])
            aux.put(ps, [t1])
            return q, t1

        def values(q, t_q, v, dv, pt, need=()):
            ps, free = aux.get()
            pe.need(*free, t_q, *need)
            mm(ps[:, 0:dv], q[:, 0:128], v[0], True, True)
            mm(ps[:, dv:2 * dv], q[:, 128:256], v[0], True, False)
            t0 = mm(ps[:, dv:2 * dv], q[:, 256:384], v[1], False, True, True)
            pt.put(q, [t0])
            return ps, t0

        def mixer1(l, blk, then):
            with ExitStack() as ph:
                QK = sbuf([128, 18, 256], F32, ph)
                V = sbuf([128, 2, 1152], F32, ph)
                Omla = sbuf([128, 2, 384], F32, ph)
                Omo = sbuf([128, 2, 384], F32, ph)
                Odn = sbuf([128, 2, 768], F32, ph)
                Odl = sbuf([128, 2, 256], F32, ph)
                oT = [XT(3, ph) for _ in range(2)]
                tmp = Pool([sbuf([128, 384], F32, ph) for _ in range(2)])
                pr = Pool([sbuf([128, 384], F32, ph) for _ in range(3)])
                pt = Pool([sbuf([128, 384], F32, ph) for _ in range(2)])
                t_qk = {}
                t_v = {}
                res = {}
                fence = state["fence"]

                def finish(o_view, den2, n):
                    def f(ps, t0, need):
                        r = stat(2)
                        a = RCP(r, den2, need)
                        b = TT(o_view, ps[:, 0:2 * n].rearrange("p (t d) -> p t d", t=2), bc(r, n), ALU.mult,
                               [a, t0])
                        aux.put(ps, [b])
                        return b
                    return f

                nmd, dnd = stat(24), stat(24)

                def heads():
                    items = [("mo", h) for h in range(6)] + [("di", h) for h in range(12)]
                    probs, pts = {}, {}
                    for s in range(len(items) + 4):
                        if 0 <= s - 1 < len(items):
                            probs[s - 1] = probs[s - 1](pr)
                        if 0 <= s < len(items):
                            kind, h = items[s]
                            qb, kb = (h // 2, 3 + h // 2) if kind == "mo" else (6 + h // 2, 12 + h // 2)
                            rows_ = slice(64 * (h % 2), 64 * (h % 2) + 64)
                            if kind == "mo":
                                nm, den = stat(2), stat(2)
                            else:
                                nm = nmd.rearrange("p (t h) -> p h t", t=2)[:, h, :]
                                den = dnd.rearrange("p (t h) -> p h t", t=2)[:, h, :]
                            table, slope = (3, SLOPES[12 + h]) if kind == "mo" else (h // 4, SLOPES[h])
                            probs[s], _ = softmax_scores((QK[rows_, qb, :], QK[rows_, kb, :]), 0.125,
                                                         blk["dist"][:, table, :], blk["t_dist"],
                                                         [t_qk[qb], t_qk[kb]], tmp, nm, den, slope)
                        if 0 <= s - 2 < len(items):
                            p, t3, den = probs[s - 2]
                            pts[s - 2] = turn_probs(p, [t3], pr, pt)
                        if 0 <= s - 3 < len(items):
                            kind, h = items[s - 3]
                            q, tq = pts[s - 3]
                            if kind == "mo":
                                v = [V[:, t, 64 * h:64 * h + 64] for t in (0, 1)]
                                nv = [t_v[0, 0], t_v[0, 1]]
                            else:
                                v = [V[:, t, 384 + 64 * h:448 + 64 * h] for t in (0, 1)]
                                nv = [t_v[1 + h // 6, 0], t_v[1 + h // 6, 1]]
                            ps, t0 = values(q, tq, v, 64, pt, nv)
                            if kind == "mo":
                                res["mo"] = finish(Omo[:, :, 64 * h:64 * h + 64], probs[s - 3][2], 64)(
                                    ps, t0, [probs[s - 3][1]])
                            else:
                                t1 = CP(Odn[:, :, 64 * h:64 * h + 64],
                                        ps[:, 0:128].rearrange("p (t d) -> p t d", t=2), [t0])
                                aux.put(ps, [t1])
                                res["dn"] = [t1, probs[s - 3][1]]
                        yield
                        if s % 3 == 2:
                            yield
                    lg, ls = stat(24), stat(24)
                    act.put(lambda e: e.preload_act_table_set("natural_log_exp_and_others"))
                    a = A(lg, dnd, ACT.Ln, res["dn"])
                    b = TT(ls, lg, nmd, ALU.subtract, [a])
                    v4 = lambda ap: ap.rearrange("p (t g h) -> p t g h", t=2, g=3)
                    v4h = lambda ap: ap.rearrange("p (t g h) -> p t h g", t=2, g=3)
                    mx, sm_, e = stat(8), stat(8), stat(24)
                    c = RED(mx.rearrange("p (t h) -> p t h", t=2), v4h(ls), ALU.max, [b])
                    m3 = mx.rearrange("p (t h) -> p t h", t=2)
                    for g in range(3):
                        d = TT(v4(ls)[:, :, g, :], v4(ls)[:, :, g, :], m3, ALU.subtract, [c])
                    a = A(e, ls, ACT.Exp, [d])
                    b = RED(sm_.rearrange("p (t h) -> p t h", t=2), v4h(e), ALU.add, [a])
                    s3 = sm_.rearrange("p (t h) -> p t h", t=2)
                    for g in range(3):
                        c = TT(v4(ls)[:, :, g, :], v4(dnd)[:, :, g, :], s3, ALU.mult, [b])
                    d = RCP(lg, ls, [c])
                    w_ = stat(24)
                    d = TT(w_, e, lg, ALU.mult, [d])
                    yield
                    o4 = Odl[:, :, :].rearrange("p t (h d) -> p t h d", h=4)
                    for g in range(3):
                        n4 = Odn[:, :, 256 * g:256 * g + 256].rearrange("p t (h d) -> p t h d", h=4)
                        for t in (0, 1):
                            c = TT(n4[:, t], n4[:, t], bc(v4(w_)[:, t, g, :], 64), ALU.mult, [d, *res["dn"]])
                    s1 = TT(o4, Odn[:, :, 0:256].rearrange("p t (h d) -> p t h d", h=4),
                            Odn[:, :, 256:512].rearrange("p t (h d) -> p t h d", h=4), ALU.add, [c])
                    res["di"] = TT(o4, o4, Odn[:, :, 512:768].rearrange("p t (h d) -> p t h d", h=4), ALU.add, [s1])
                    yield

                with ExitStack() as pm:
                    lat = sbuf([128, 2, 416], F32, pm)
                    qs = sbuf([128, 2, 576], F32, pm)
                    ks = sbuf([128, 2, 576], F32, pm)
                    vm = sbuf([128, 2, 384], F32, pm)
                    cq = XT(2, pm)
                    ckv = XT(1, pm)
                    ra = sbuf([128, 2, 96], F32, pm)
                    rb = sbuf([128, 2, 96], F32, pm)
                    qkh = Pool([sbuf([96, 512], F32, pm) for _ in range(2)])
                    tm = {}

                    def rope(dst, src, t, h, need):
                        cc, ss = blk["rope"][:, t, 0:32], blk["rope"][:, t, 32:64]
                        a3 = ra[:, t, 0:32 * h].rearrange("p (h d) -> p h d", h=h)
                        b3 = rb[:, t, 0:32 * h].rearrange("p (h d) -> p h d", h=h)
                        TT(a3, src, bc1(cc, h), ALU.mult, [*need, blk["t_rope"]])
                        t1 = TT(b3, src, bc1(ss, h), ALU.mult)
                        TT(dst[:, :, 0:16], a3[:, :, 0:16], b3[:, :, 16:32], ALU.subtract, [t1])
                        return TT(dst[:, :, 16:32], a3[:, :, 16:32], b3[:, :, 0:16], ALU.add), t1

                    def latents(banks, tok):
                        a, b = [], []
                        ss = stat(4)
                        for t in (0, 1):
                            A(lat[:, t, 0:256], banks[t][:, 0:256], ACT.Square, [tok, *fence],
                              accum=ss[:, 2 * t:2 * t + 1])
                            a.append(A(lat[:, t, 256:384], banks[t][:, 256:384], ACT.Square,
                                       accum=ss[:, 2 * t + 1:2 * t + 2]))
                        ms = stat(4)
                        toks = []
                        for t in (0, 1):
                            TS(ms[:, 2 * t:2 * t + 1], ss[:, 2 * t:2 * t + 1], 1.0 / 256, 1e-6, ALU.mult, ALU.add, [a[t]])
                            b.append(TS(ms[:, 2 * t + 1:2 * t + 2], ss[:, 2 * t + 1:2 * t + 2], 1.0 / 128, 1e-6,
                                        ALU.mult, ALU.add))
                            kr = lat[:, t, 384:416].unsqueeze(1)
                            tk, _ = rope(kr, banks[t][:, 384:416].unsqueeze(1), t, 1, [tok, a[t]])
                            tm["kr", t] = CP(ks[:, t, :].rearrange("p (h d) -> p h d", h=6)[:, :, 64:96],
                                             bc1(lat[:, t, 384:416], 6), [tk])
                        for t in (0, 1):
                            r, c = rsqrt(ms[:, 2 * t:2 * t + 2], [b[t]])
                            toks.append(TS(lat[:, t, 0:256], banks[t][:, 0:256], r[:, 0:1], None, ALU.mult, need=[c]))
                            toks.append(TS(lat[:, t, 256:384], banks[t][:, 256:384], r[:, 1:2], None, ALU.mult))
                            mmb.put(banks[t], [toks[-1], tm["kr", t]])

                        yield
                        yield
                        to_T([lat[:, t, 0:256] for t in (0, 1)], toks, 2, cq, col("q_norm", l, 2))
                        to_T([lat[:, t, 256:384] for t in (0, 1)], toks, 1, ckv, col("kv_norm", l, 1))

                    banks, need = two()
                    tok = gemm(("mla", l), xT, 8, [[(b[:, 0:416], 0, 416)] for b in banks], need, between)
                    f = latents(banks, tok)
                    next(f)
                    fibers.append(f)

                    def qk_chunk(c):
                        n = 4 if c < 4 else 2
                        banks, need = two() if n == 4 else one()
                        outs = [banks[m // 2][:, 256 * (m % 2):256 * (m % 2) + 256] for m in range(n)]
                        tok = gemm_w(("qk1", l, c), xT, 8, outs, need)
                        for j, b in enumerate(banks):
                            dst = QK[:, 4 * c + 2 * j:4 * c + 2 * j + 2, :].rearrange("p a b -> p (a b)")
                            if j == 0:
                                t1 = A(dst, b[:, :], ACT.Copy, [tok])
                            else:
                                t1 = CP(dst, b[:, :], [tok])
                            mmb.put(b, [t1])
                            t_qk[4 * c + 2 * j] = t_qk[4 * c + 2 * j + 1] = t1

                    qk_chunk(0)
                    for j in (0, 1):
                        banks, need = two()
                        tok = gemm(("uq", l, j), cq, 2, [[(b[:, 0:288], 0, 288)] for b in banks], need)
                        for t in (0, 1):
                            dst = qs[:, t, 288 * j:288 * j + 288]
                            a = A(dst, banks[t][:, 0:288], ACT.Copy, [tok])
                            v3 = dst.rearrange("p (h d) -> p h d", h=3)[:, :, 64:96]
                            p3 = banks[t][:, 0:288].rearrange("p (h d) -> p h d", h=3)[:, :, 64:96]
                            b, t1 = rope(v3, p3, t, 3, [a])
                            tm["q", j, t] = b
                            mmb.put(banks[t], [a, t1])
                    for j in (0, 1):
                        banks, need = two()
                        tok = gemm(("ukv", l, j), ckv, 1, [[(b[:, 0:384], 0, 384)] for b in banks], need)
                        for t in (0, 1):
                            p3 = banks[t][:, 0:384].rearrange("p (h d) -> p h d", h=3)
                            k3 = ks[:, t, 288 * j:288 * j + 288].rearrange("p (h d) -> p h d", h=3)
                            v3 = vm[:, t, 192 * j:192 * j + 192].rearrange("p (h d) -> p h d", h=3)
                            a = A(k3[:, :, 0:64], p3[:, :, 0:64], ACT.Copy, [tok])
                            b = CP(v3, p3[:, :, 64:128], [tok, a])
                            tm["k", j, t] = [a, tm["kr", t]]
                            tm["v", j, t] = b
                            mmb.put(banks[t], [a, b])

                    def mla_heads():
                        turned, probs, pts = {}, {}, {}
                        for s in range(6 + 5):
                            if 0 <= s - 2 < 6:
                                probs[s - 2] = probs[s - 2](pr)
                            if s < 6:
                                ps, free = aux.get()
                                pe.need(*free)
                                for n, src in enumerate((qs, ks)):
                                    for t in (0, 1):
                                        pe.need(tm["qk"[n], s // 3, t])
                                        t0 = tr(ps[0:96, 256 * n + 128 * t:256 * n + 128 * t + 128],
                                                src[:, t, 96 * s:96 * s + 96], last=(n == 1 and t == 1))
                                b, f = qkh.get()
                                t1 = A(b[:, :], ps[0:96, :], ACT.Copy, [t0, *f])
                                aux.put(ps, [t1])
                                turned[s] = (b, t1)
                            if 0 <= s - 1 < 6:
                                h = s - 1
                                b, t1 = turned[h]
                                nm, den = stat(2), stat(2)
                                probs[h], t2 = softmax_scores((b[:, 0:256], b[:, 256:512]), 96.0 ** -0.5,
                                                              blk["causal"][:, :], blk["t_causal"], [t1], tmp, nm, den)
                                qkh.put(b, [t2])
                            if 0 <= s - 3 < 6:
                                h = s - 3
                                p, t3, den = probs[h]
                                pts[h] = turn_probs(p, [t3], pr, pt)
                            if 0 <= s - 4 < 6:
                                h = s - 4
                                q, tq = pts[h]
                                v = [vm[:, t, 64 * h:64 * h + 64] for t in (0, 1)]
                                ps, t0 = values(q, tq, v, 64, pt, [tm["v", h // 3, 0], tm["v", h // 3, 1]])
                                res["mla"] = finish(Omla[:, :, 64 * h:64 * h + 64], probs[h][2], 64)(ps, t0, [probs[h][1]])
                            yield
                            if s % 2:
                                yield

                    def v_chunk(j):
                        c0 = 384 * j
                        banks, need = two()
                        tok = gemm(("v1", l, j), xT, 8, [[(b[:, 0:384], 0, 384)] for b in banks], need)
                        for t in (0, 1):
                            dst = V[:, t, c0:c0 + 384]
                            t1 = (A(dst, banks[t][:, 0:384], ACT.Copy, [tok]) if t == 0
                                  else CP(dst, banks[t][:, 0:384], [tok]))
                            t_v[j, t] = t1
                            mmb.put(banks[t], [t1])

                    def all_heads():
                        yield from mla_heads()
                        res["mla_done"] = True
                        to_T([Omla[:, t, :] for t in (0, 1)], [res["mla"]], 3, oT[0])
                        yield from heads()
                        to_T([Odl[:, t, :] for t in (0, 1)], [res["di"]], 2, oT[1])

                    fibers.append(all_heads())
                    for c in (1, 2, 3):
                        qk_chunk(c)
                    v_chunk(0)
                    qk_chunk(4)
                    v_chunk(1)
                    v_chunk(2)
                    assert res["mla_done"]

                G = sbuf([128, 2, 3072], F32, ph)
                t_g = {}
                for c in range(6):
                    banks, need = two()
                    tok = gemm(("g1", l, c), xT, 8, [[(b[:, :], 0, 512)] for b in banks], need)
                    for t in (0, 1):
                        t_g[c, t] = A(G[:, t, 512 * c:512 * c + 512], banks[t][:, :], ACT.Tanh, [tok], scale=0.5)
                        mmb.put(banks[t], [t_g[c, t]])
                bg_drain()
                order = [(r, nk) for r, _, nk in BR1]
                third = lambda: to_T([Omo[:, t, :] for t in (0, 1)], [res["mo"]], 3, oT[0])
                branches("br1", l, order, [oT[0], oT[1], oT[0]], G, t_g, XN, state["xn"], third, 1.0)
                product_out("o1", l, then, 0.5)

        def branches(key, l, order, ots, G, t_g, dst, dfree, third, plus=0.0):
            merged = {}
            for i, (r, nk, *_) in enumerate(order):
                for n in (0, 1):
                    banks, need = two()

                    def merge(t, tok):
                        m = dst[t][:, 512 * n:512 * n + 512]
                        g = G[:, t, 1024 * r + 512 * n:1024 * r + 512 * n + 512]
                        if i == 0:
                            a = STT(m, g, plus, banks[t][:, :], ALU.add, ALU.mult, [tok, t_g[2 * r + n, t], dfree])
                            mmb.put(banks[t], [a])
                        else:
                            b = STT(g, g, plus, banks[t][:, :], ALU.add, ALU.mult, [tok, t_g[2 * r + n, t]])
                            mmb.put(banks[t], [b])
                            a = TT(m, m, g, ALU.add, [b, merged[t, n]], pool if i == 1 else dve)
                        merged[t, n] = a

                    late = i == len(order) - 1 and n == 1

                    def mid(tok):
                        merge(0, tok)
                        for t in (0, 1):
                            state["xn"] = [turn(dst[t], [merged[t, 0]], t, range(0, 4), xT)]

                    toks = gemm((key, l, r, n), ots[i], nk, [[(b[:, :], 0, 512)] for b in banks], need,
                                mid if late else None)
                    if not late:
                        merge(0, toks[0])
                    merge(1, toks[1])
                ots[i].free = [toks[1]]
                if i == 0:
                    third()

            def other_half():
                for t in (0, 1):
                    state["xn"] = [turn(dst[t], [merged[t, 1]], t, range(4, 8), xT)]
                yield

            fibers.append(other_half())

        with ExitStack() as b1:
            blk = {}
            blk["rope"] = sbuf([128, 2, 64], F32, b1)
            blk["t_rope"] = once(blk["rope"][:, :, :], rope_d[:, :, 0:64], "s_rope1")
            blk["causal"] = sbuf([128, 384], F32, b1)
            blk["t_causal"] = once(blk["causal"][:, :], bias_d[4], "s_causal1")
            blk["dist"] = sbuf([128, 4, 384], F32, b1)
            blk["t_dist"] = once(blk["dist"][:, :, :], bias_d[0:4].rearrange("n p c -> p n c"), "s_dist")
            enter = enter_scaled(col("ffn1_norm", 0, 8))
            enter(0, [state["x"][0]] * 2)()
            S.halves_to(1, 1)
            state["second"] = enter(1, [state["x"][1]] * 2)
            for l in (0, 1):
                ffn("f1", l, enter_rms(col("mix_norm", l, 8)))
                mixer1(l, blk, enter_scaled(col("ffn2_norm", l, 8)))
                if l == 0:
                    ffn("f2", l, enter_scaled(col("ffn1_norm", 1, 8)))
        fence_b2 = state["fence"]

        s_out = sem("s_out")
        for line in VR:
            line.buf, line.free = sbuf([128, D], F32, ctx), [fence_b2]

        def once2(out, in_, name):
            sp.need(*fence_b2)
            return once(out, in_, name)

        tri_line = Line(sem("s_tri"), None)
        strict = sbuf([128, 384], F32, ctx)
        t_strict = once2(strict[:, :], bias_d[5], "s_strict")
        chunk = sbuf([128, 384], F32, ctx)
        t_chunk = once2(chunk[:, :], bias_d[6], "s_chunk")
        rope2 = sbuf([128, 2, 32], F32, ctx)
        t_rope2 = once2(rope2[:, :, :], rope_d[:, :, 64:96], "s_rope2")
        zero = sbuf([128, 256], F32, ctx)
        dve.need(fence_b2)
        t_zero = dve.go(lambda e: e.memset(zero[:, :], 0.0))
        s_lam = sbuf([128, 128], F32, ctx)
        rw_line, scr_line = Line(sem("s_rw"), None), Line(sem("s_scr"), None)
        ar_lines = [Line(sem(f"s_ar{i}"), None) for i in range(2)]
        def mixer2(l, then):
            lam_init = 0.8 - 0.6 * math.exp(-0.3 * l)
            fence = state["fence"]
            with ExitStack() as ph:
                OA = sbuf([128, 2, 1024], F32, ph)
                OB = sbuf([128, 2, 1024], F32, ph)
                OC = XNB
                tmp = Pool([sbuf([128, 384], F32, ph) for _ in range(2)])
                pr = Pool([sbuf([128, 384], F32, ph) for _ in range(3)])
                pt = Pool([sbuf([128, 384], F32, ph) for _ in range(2)])
                rw = sbuf([128, 272], F32, ph)
                rw_line.buf = rw
                t_rw = load(rw_line, rw[:, :], rows[l:l + 1, :].broadcast_to([128, 272]), fence)
                R1 = sbuf([128, 6144], F32, ph)
                QKA = R1[:, 0:4096].rearrange("p (a b) -> p a b", a=16)
                VAt = R1[:, 4096:6144].rearrange("p (a b) -> p a b", a=2)
                reg2 = ExitStack()
                Z = XN
                BC = sbuf([128, 4, 256], F32, reg2)
                XD = sbuf([128, 2, 1024], F32, reg2)
                ARS = [sbuf([128, 4, 256], F32, reg2) for _ in range(2)]
                MS = [sbuf([128, 4, 384], F32, reg2) for _ in range(2)]
                CB = sbuf([128, 2, 384], F32, reg2)
                cacc = Pool([sbuf([128, 256], F32, reg2) for _ in range(3)])
                ROT = Pool([sbuf([128, 512], F32, reg2) for _ in range(2)])
                rt = [sbuf([128, 128], F32, reg2) for _ in range(2)]
                tri = MS[0][:, 3, :]
                t_tri = load(tri_line, tri, msk_d, fence)
                dtr, dtw, arow = (MS[0][0:16, i, 0:256] for i in range(3))
                crow = MS[1][0:16, 0:2, :].rearrange("p a b -> p (a b)").rearrange("p (n x) -> p n x", n=6)
                turned8 = sbuf([128, 8, 16], F32, reg2)
                dtt, cadd = turned8[:, 0:2, :], turned8[:, 2:8, :]
                tk = {}

                def scalars():
                    d3 = s_lam[:, :].rearrange("p (a b) -> p a b", a=2)
                    l4 = rw[:, 0:256].rearrange("p (a c b) -> p a c b", a=2, c=2)
                    a = TT(d3, l4[:, :, 0, :], l4[:, :, 1, :], ALU.mult, [t_rw, fence])
                    sd = stat(2)
                    b = RED(sd, d3, ALU.add, [a])
                    es = stat(2)
                    c = A(es, sd, ACT.Exp, [b])
                    nl = stat(1)
                    TS(nl, es[:, 1:2], es[:, 0:1], -lam_init, ALU.subtract, ALU.add, [c])
                    tk["nlam"] = (dve.sem, dve.n)
                    gs = stat(1)
                    tk["gs"] = TS(gs, col("diff_subln_g_2", l, 1), 1.0 - lam_init, None, ALU.mult)
                    an = stat(1)
                    a = A(an[0:16, :], col("ssm_A_log_2", l, 1)[0:16, :], ACT.Exp, [t_col])
                    tk["an"] = TS(an[0:16, :], an[0:16, :], -1.0, None, ALU.mult, need=[a])
                    return nl, gs, an[0:16, :]


                def z_post(banks, tok, n):
                    for t in (0, 1):
                        a = A(Z[t][:, 512 * n:512 * n + 512], banks[t][:, :], ACT.Silu, [tok, state["xn"]])
                        mmb.put(banks[t], [a])
                        tk["z", n, t] = a
                    yield

                for n in (0, 1):
                    banks, need = two()
                    tok = gemm(("z", l, n), xT, 8, [[(b[:, :], 0, 512)] for b in banks], need,
                               None if n else between)
                    for _ in z_post(banks, tok, n):
                        pass
                run_later()

                nlam, gsub, aneg = scalars()

                b_, f = one()
                dtp = b_[0]
                tok = dt_gemm(l, dtp, f)

                def sums(q):
                    src = scratch[l, 4 * q:4 * q + 4, :].unsqueeze(0).broadcast_to([128, 4, 256])
                    return load(ar_lines[q % 2], ARS[q % 2][:, :, :], src, [tk["scr"]])

                def dts():
                    act.put(lambda e: e.preload_act_table_set("natural_log_exp_and_others"))
                    bias = col("ssm_dt_bias_2", l, 1)[0:16, :]
                    b = A(dtw, dtp[0:16, 0:256], ACT.Abs, [tok, t_col, fence], bias=bias)
                    c = TS(dtr, dtp[0:16, 0:256], bias, 0.0, ALU.add, ALU.max, need=[b])
                    mmb.put(dtp, [c])
                    b = A(dtw, dtw, ACT.Exp, [b], scale=-1.0)
                    b = A(dtw, dtw, ACT.Ln, [b], bias=1.0)
                    yield
                    d = TT(dtr, dtr, dtw, ALU.add, [b, c])
                    c = TS(dtw, dtr, aneg, None, ALU.mult, need=[d, tk["an"]])
                    dve.need(c, t_zero)
                    for k in range(4):
                        cs = slice(64 * k, 64 * k + 64)
                        c = dve.go(lambda e, cs=cs: e.tensor_tensor_scan(arow[:, cs], dtw[:, cs], zero[0:16, 0:64],
                                                                         0.0, ALU.add, ALU.add))
                    sp.need(c, scr_line.free)
                    scr_line.n += 1
                    sp.put(lambda e: e.dma_start(scratch[l], arow).then_inc(scr_line.sem, 16))
                    tk["scr"] = (scr_line.sem, 16 * scr_line.n)
                    tk["ar"] = [sums(0), sums(1)]
                    tot = [arow[:, 64 * k + 63:64 * k + 64] for k in range(4)]
                    c = TS(crow[:, 0, :], arow[:, 0:128], -1.0, None, ALU.mult, need=[c])
                    d = TS(crow[:, 4, :], arow[:, 128:256], -1.0, None, ALU.mult)
                    CP(crow[:, 1, 64:128], crow[:, 0, 64:128], [c])
                    CP(crow[:, 5, 64:128], crow[:, 4, 64:128], [d])
                    TS(crow[:, 5, 0:64], crow[:, 4, 0:64], tot[2], None, ALU.add)
                    c = TS(crow[:, 1, 0:64], crow[:, 0, 0:64], tot[0], None, ALU.add)
                    c = TS(crow[:, 2, :], crow[:, 1, :], tot[1], None, ALU.add, need=[c])
                    c = TS(crow[:, 3, :], crow[:, 2, :], tot[2], None, ALU.add, need=[c])
                    yield
                    yield
                    ps, free = aux.get()
                    pe.need(*free, c)
                    srcs = [dtr[:, 0:128], dtr[:, 128:256]] + [crow[:, k, :] for k in range(6)]
                    for k, src in enumerate(srcs):
                        b = tr(ps[:, 16 * k:16 * k + 16], src, last=(k == 7))
                    c = CP(turned8[:, :, :].rearrange("p n h -> p (n h)"), ps[:, 0:128], [b])
                    aux.put(ps, [c])
                    tk["dt"] = c

                f = dts()
                next(f)
                fibers.append(f)

                t_bc, turning = [None] * 4, []

                def conv_first(ct, src):
                    acc, free = cacc.get()
                    w = colt[:, COLS[("ssm_conv_w_2", l)] + 4 * ct:COLS[("ssm_conv_w_2", l)] + 4 * ct + 4]
                    b = colt[:, COLS[("ssm_conv_b_2", l)] + ct:COLS[("ssm_conv_b_2", l)] + ct + 1]
                    a = A(acc[:, :], src, ACT.Identity, [tk["xbc", ct // 4], *free, fence], scale=w[:, 3:4], bias=b)
                    return acc, w, a

                def conv_rest(acc, w, src, a):
                    for s in (1, 2, 3):
                        a = STT(acc[:, s:256], src[:, 0:256 - s], w[:, 3 - s:4 - s], acc[:, s:256], ALU.mult, ALU.add,
                                [a])
                    return a

                def products_cb():
                    for g in (0, 1):
                        ps, free = aux.get()
                        pe.need(*free, *t_bc)
                        mm(ps[:, 0:256], BC[:, g, 0:128], BC[:, 2 + g, 0:256], True, True)
                        a = mm(ps[:, 256:384], BC[:, g, 128:256], BC[:, 2 + g, 128:256], True, True, True)
                        tk["cb", g] = TT(CB[:, g, :], ps[:, 0:384], tri, ALU.mult, [a, t_tri])
                        aux.put(ps, [tk["cb", g]])
                        yield

                def conv_out(ct, acc, b):
                    ps, free = aux.get()
                    pe.need(*free, b)
                    for t in (0, 1):
                        e = tr(ps[:, 128 * t:128 * t + 128], acc[:, 128 * t:128 * t + 128], last=(t == 1))
                    cacc.put(acc, [e])
                    o3 = OB[:, :, 128 * ct:128 * ct + 128]
                    a = A(o3, ps[:, 0:256].rearrange("p (t c) -> p t c", t=2), ACT.Copy, [e])
                    aux.put(ps, [a])
                    for t in (0, 1):
                        o3 = OB[:, t, 128 * ct:128 * ct + 128].rearrange("p (h d) -> p h d", h=2)
                        x3 = XD[:, t, 128 * ct:128 * ct + 128].rearrange("p (h d) -> p h d", h=2)
                        a = TT(x3, o3, bc(dtt[:, t, 2 * ct:2 * ct + 2], 64), ALU.mult, [a, tk["dt"]], pool)
                        tk["xd"] = TT(o3, o3, bc(rw[:, 256 + 2 * ct:258 + 2 * ct], 64), ALU.mult, [a, t_rw], pool)

                def conv_tiles(c, banks, outs):
                    for m in range(4):
                        if m % 2 == 0:
                            pair = [conv_first(4 * c + m + i, outs[m + i]) for i in (0, 1)]
                        acc, w, _ = pair[m % 2]
                        a = conv_rest(acc, w, outs[m], pair[1][2])
                        if m % 2:
                            mmb.put(banks[m // 2], [a])
                        if c == 2:
                            t_bc[m] = A(BC[:, m, :], acc[:, :], ACT.Silu, [a])
                            cacc.put(acc, [t_bc[m]])
                        else:
                            if turning:
                                conv_out(*turning.pop())
                            turning.append((4 * c + m, acc, A(acc[:, :], acc[:, :], ACT.Silu, [a])))
                        yield
                    if c == 2:
                        fibers.append(products_cb())
                    if c == 1:
                        conv_out(*turning.pop())

                def xbc_chunk(c):
                    banks, need = two()
                    outs = [banks[m // 2][:, 256 * (m % 2):256 * (m % 2) + 256] for m in range(4)]
                    tk["xbc", c] = gemm_w(("xbc", l, c), xT, 8, outs, need)

                    chain.append(conv_tiles(c, banks, outs))

                for c in (2, 0, 1):
                    xbc_chunk(c)

                def ssd():
                    tas = tk["ar"]
                    t_add, t_min, t_exp, t_mul, t_y = {}, {}, {}, {}, {}
                    mfree = [None, None]
                    for s in range(4 * 3 + 7):
                        q, r = divmod(s - 6, 4)
                        if r == 0 and 0 <= q < 4:
                            ps, e = t_y[q]
                            for t in (0, 1):
                                o = OB[:, t, 256 * q:256 * q + 256]
                                a = TT(o, o, ps[:, 256 * t:256 * t + 256], ALU.add, [e, tk["xd"]])
                                tk["y", q, t] = TT(o, o, Z[t][:, 256 * q:256 * q + 256], ALU.mult,
                                                   [a, tk["z", q // 2, t]])
                            aux.put(ps, [a])
                        q, r = divmod(s, 4)
                        M = MS[q % 2]
                        hs = slice(4 * q, 4 * q + 4)
                        if q < 4 and r == 0:
                            AR = ARS[q % 2]
                            for k0, c0, n in ((0, 0, 4), (4, 2, 2)):
                                src = AR[:, :, 64 * c0:64 * (c0 + n)].rearrange("p h (c x) -> p h c x", c=n)
                                dst = M[:, :, 64 * k0:64 * (k0 + n)].rearrange("p h (c x) -> p h c x", c=n)
                                add = cadd[:, k0:k0 + n, hs].rearrange("p c h -> p h c").unsqueeze(3)
                                b = TT(dst, src, add.broadcast_to([128, 4, n, 64]), ALU.add,
                                       [tas[q], tk["dt"], tk["cb", 1], mfree[q % 2]])
                            t_add[q] = b
                            ar_lines[q % 2].free = [b]
                            if q < 2:
                                tas.append(sums(q + 2))
                        if q < 4 and r == 1:
                            for k0 in (0, 256):
                                m = M[:, :, k0:k0 + 128]
                                t_min[q] = TS(m, m, 0.0, None, ALU.min, need=[t_add[q]])
                        if q < 4 and r == 2:
                            mf = M[:, :, :].rearrange("p h c -> p (h c)")
                            t_exp[q] = A(mf, mf, ACT.Exp, [t_min[q]])
                        if q < 4 and r == 3:
                            t_mul[q] = TT(M[:, :, :], M[:, :, :], bc1(CB[:, q // 2, :], 4), ALU.mult,
                                          [t_exp[q], tk["cb", q // 2]], pool)
                        q, r = divmod(s - 5, 4)
                        if r == 0 and 0 <= q < 4:
                            M = MS[q % 2]
                            ps, free = aux.get()
                            pe.need(*free, t_mul[q], tk["xd"])
                            for j in range(4):
                                c = slice(64 * (4 * q + j), 64 * (4 * q + j) + 64)
                                mm(ps[:, 64 * j:64 * j + 64], M[:, j, 0:128], XD[:, 0, c], True, True)
                                mm(ps[:, 256 + 64 * j:320 + 64 * j], M[:, j, 128:256], XD[:, 0, c], True, False)
                                e = mm(ps[:, 256 + 64 * j:320 + 64 * j], M[:, j, 256:384], XD[:, 1, c], False, True,
                                       j == 3)
                            mfree[q % 2] = tk["mfree"] = e
                            t_y[q] = (ps, e)
                        yield
                    scr_line.free = [tas[2], tas[3]]
                    tk["ob"] = []
                    for t in (0, 1):
                        ss, ms = stat(2), stat(2)
                        for g in (0, 1):
                            o = OB[:, t, 512 * g:512 * g + 512]
                            a = A(Z[t][:, 512 * g:512 * g + 512], o, ACT.Square, [tk["y", 2 * g, t], tk["y", 2 * g + 1, t]],
                                  accum=ss[:, g:g + 1])
                        b = TS(ms, ss, 1.0 / 512, 1e-5, ALU.mult, ALU.add, [a])
                        r, c = rsqrt(ms, [b])
                        for g in (0, 1):
                            o = OB[:, t, 512 * g:512 * g + 512]
                            tk["ob"].append(TS(o, o, r[:, g:g + 1], None, ALU.mult, need=[c]))
                    tk["zfree"] = tk["ob"]
                    yield

                chain.append(ssd())

                def rope_chunk(name, n, base):
                    banks, need = two()
                    tok = gemm((name, l, n), xT, 8, [[(b[:, :], 0, 512)] for b in banks], need)

                    def post():
                        done, bufs = [], []
                        for t in (0, 1):
                            buf, free = ROT.get()
                            a = A(buf[:, :], banks[t][:, :], ACT.Copy, [tok, *free])
                            p3 = banks[t][:, :].rearrange("p (h d) -> p h d", h=8)[:, :, 0:16]
                            d3 = buf[:, :].rearrange("p (h d) -> p h d", h=8)
                            a3 = rt[0][:, :].rearrange("p (h d) -> p h d", h=8)
                            b3 = rt[1][:, :].rearrange("p (h d) -> p h d", h=8)
                            TT(a3, p3, bc1(rope2[:, t, 0:16], 8), ALU.mult, [tok, t_rope2, a, tk.get("rt")])
                            b = TT(b3, p3, bc1(rope2[:, t, 16:32], 8), ALU.mult)
                            mmb.put(banks[t], [b])
                            TT(d3[:, :, 0:8], a3[:, :, 0:8], b3[:, :, 8:16], ALU.subtract, [b])
                            tk["rt"] = TT(d3[:, :, 8:16], a3[:, :, 8:16], b3[:, :, 0:8], ALU.add)
                            done.append(tk["rt"])
                            bufs.append(buf)
                        yield
                        yield
                        for k in (0, 2):
                            ps, free = aux.get()
                            pe.need(*free, *done)
                            for j in (0, 1):
                                for t in (0, 1):
                                    a = tr(ps[:, 256 * j + 128 * t:256 * j + 128 * t + 128],
                                           bufs[t][:, 128 * (k + j):128 * (k + j) + 128], last=(j == 1 and t == 1))
                            hh = base + 4 * n + k
                            b = A(QKA[:, hh:hh + 2, :].rearrange("p a b -> p (a b)"), ps[:, :], ACT.Copy, [a])
                            aux.put(ps, [b])
                            tk["qka", hh] = tk["qka", hh + 1] = b
                        for t in (0, 1):
                            ROT.put(bufs[t], [a])
                    f = post()
                    next(f)
                    fibers.append(f)

                for n in (0, 1):
                    rope_chunk("qa", n, 0)
                for n in (0, 1):
                    rope_chunk("ka", n, 8)

                def v_chunk(name, n, dst):
                    banks, need = two()
                    tok = gemm((name, l, n), xT, 8, [[(b[:, :], 0, 512)] for b in banks], need)
                    for t in (0, 1):
                        o = dst[:, t, 512 * n:512 * n + 512]
                        a = A(o, banks[t][:, :], ACT.Copy, [tok]) if t else CP(o, banks[t][:, :], [tok])
                        mmb.put(banks[t], [a])
                        tk[name, n, t] = a

                for n in (0, 1):
                    v_chunk("va", n, VAt)
                bg_drain()
                fence2 = [*tk["ob"], tk["mfree"]]
                reg2.close()
                reg3 = ExitStack()
                QKC = sbuf([128, 16, 256], F32, reg3)
                VCt = sbuf([128, 2, 1024], F32, reg3)

                def heads_a():
                    st, w_, pts = {}, {}, {}
                    for s in range(16 + 5):
                        if 0 <= s - 1 < 16:
                            st[s - 1] = st[s - 1](pr)
                        if s >= 5 and s % 2 == 1 and (s - 5) // 2 < 8:
                            h = (s - 5) // 2
                            q, tq = pts[h]
                            v = [VAt[:, t, 128 * h:128 * h + 128] for t in (0, 1)]
                            ps, t0 = values(q, tq, v, 128, pt, [tk["va", h // 4, 0], tk["va", h // 4, 1]])
                            ss, ms = stat(2), stat(2)
                            jb, jf = tmp.get()
                            for t in (0, 1):
                                a = A(jb[:, 128 * t:128 * t + 128], ps[:, 128 * t:128 * t + 128], ACT.Square,
                                      [t0, *jf], accum=ss[:, t:t + 1])
                            tmp.put(jb, [a])
                            b = TS(ms, ss, 1.0 / 128, 1e-5, ALU.mult, ALU.add, [a])
                            r, c = rsqrt(ms, [b])
                            o3 = OA[:, :, 128 * h:128 * h + 128]
                            tk["oa"] = TT(o3, ps[:, 0:256].rearrange("p (t d) -> p t d", t=2), bc(r, 128), ALU.mult,
                                          [c])
                            aux.put(ps, [tk["oa"]])
                        if s >= 4 and s % 2 == 0 and s // 2 - 2 < 8:
                            h = s // 2 - 2
                            pts[h] = turn_probs(w_[h][0], [w_[h][1]], pr, pt)
                        if s >= 2 and s % 2 == 0 and s // 2 - 1 < 8:
                            h = s // 2 - 1
                            p0, ta, d0 = st[2 * h]
                            p1, tb, d1 = st[2 * h + 1]
                            r = stat(4)
                            RCP(r[:, 0:2], d0, [ta])
                            a = RCP(r[:, 2:4], d1, [tb])
                            b = TS(r[:, 2:4], r[:, 2:4], nlam, None, ALU.mult, need=[a, tk["nlam"]])
                            sl = [slice(0, 128), slice(128, 384)]
                            for t in (0, 1):
                                a = TS(p0[:, sl[t]], p0[:, sl[t]], r[:, t:t + 1], None, ALU.mult, need=[b])
                            for t in (0, 1):
                                a = STT(p0[:, sl[t]], p1[:, sl[t]], r[:, 2 + t:3 + t], p0[:, sl[t]], ALU.mult, ALU.add,
                                        [(dve.sem, dve.n - 1)])
                            pr.put(p1, [a])
                            w_[h] = (p0, a)
                        if s < 16:
                            h, m = s // 2, s % 2
                            rr = slice(64 * m, 64 * m + 64)
                            nm, den = stat(2), stat(2)
                            st[s], _ = softmax_scores((QKA[rr, h, :], QKA[rr, 8 + h, :]), 0.125, chunk[:, :],
                                                      t_chunk, [tk["qka", h], tk["qka", 8 + h]], tmp, nm, den)
                        yield

                fibers.append(heads_a())

                def qkc_chunk(name, n, base):
                    banks, need = two()
                    outs = [banks[m // 2][:, 256 * (m % 2):256 * (m % 2) + 256] for m in range(4)]
                    tok = gemm_w((name, l, n), xT, 8, outs, need)
                    for j in (0, 1):
                        hh = base + 4 * n + 2 * j
                        o = QKC[:, hh:hh + 2, :].rearrange("p a b -> p (a b)")
                        a = (A(o, banks[j][:, :], ACT.Copy, [tok, *fence2]) if j
                             else CP(o, banks[j][:, :], [tok, *fence2]))
                        mmb.put(banks[j], [a])
                        tk["qkc", hh] = tk["qkc", hh + 1] = a

                for n in (0, 1):
                    qkc_chunk("qc", n, 0)
                for n in (0, 1):
                    qkc_chunk("kc", n, 8)
                for n in (0, 1):
                    v_chunk("vc", n, VCt)
                bg_drain()
                fence3 = [tk["oa"]]
                G = R1[:, :].rearrange("p (a b) -> p a b", a=2)

                def heads_c():
                    act.put(lambda e: e.preload_act_table_set("natural_log_exp_and_others"))
                    arg, pts = {}, {}
                    st1 = {}
                    for s in range(16 + 5):
                        if 0 <= s - 4 < 16:
                            h = s - 4
                            q, tq = pts[h]
                            v = [VCt[:, t, 64 * h:64 * h + 64] for t in (0, 1)]
                            ps, t0 = values(q, tq, v, 64, pt, [tk["vc", h // 8, 0], tk["vc", h // 8, 1]])
                            tk["oc"] = CP(OC[:, :, 64 * h:64 * h + 64],
                                          ps[:, 0:128].rearrange("p (t d) -> p t d", t=2), [t0, *fence2])
                            aux.put(ps, [tk["oc"]])
                        if 0 <= s - 3 < 16:
                            w, c = arg[s - 3]
                            pts[s - 3] = turn_probs(w, [c], pr, pt)
                        if 0 <= s - 1 < 16:
                            z, w, a = st1[s - 1]
                            a = STT(w[:, :], z[:, :], 0.0, w[:, :], ALU.max, ALU.add, [a])
                            dve.need(a)
                            for t, (lo_, n_) in enumerate(((0, 128), (128, 256))):
                                wv = w[:, lo_:lo_ + n_][:, ::-1]
                                dve.need(t_zero)
                                b = dve.go(lambda e, wv=wv, n_=n_: e.tensor_tensor_scan(
                                    wv, wv, zero[:, 0:n_], 0.0, ALU.add, ALU.add))
                            b = TT(z[:, :], z[:, :], w[:, :], ALU.subtract, [b])
                            c = A(w[:, :], z[:, :], ACT.Exp, [b])
                            tmp.put(z, [c])
                            arg[s - 1] = (w, c)
                        if s < 16:
                            rr = slice(64 * (s % 2), 64 * (s % 2) + 64)
                            b = s // 2
                            ps, free = aux.get()
                            pe.need(*free, tk["qkc", b], tk["qkc", 8 + b])
                            qT, kT = QKC[rr, b, :], QKC[rr, 8 + b, :]
                            mm(ps[:, 0:128], qT[:, 0:128], kT[:, 0:128], True, True)
                            t0 = mm(ps[:, 128:384], qT[:, 128:256], kT[:, 0:256], True, True, True)
                            z, f2 = tmp.get()
                            t1 = STT(z[:, :], ps[:, 0:384], 0.125, strict[:, :], ALU.mult, ALU.add, [t0, t_strict, *f2])
                            aux.put(ps, [t1])
                            w, f3 = pr.get()
                            a = A(w[:, :], z[:, :], ACT.Abs, [t1, *f3])
                            a = A(w[:, :], w[:, :], ACT.Exp, [a], scale=-1.0)
                            a = A(w[:, :], w[:, :], ACT.Ln, [a], bias=1.0)
                            st1[s] = (z, w, a)
                        yield

                oT = XT(8, reg3)
                oT.free = fence2
                fibers.append(heads_c())
                t_g = {}
                for c in range(6):
                    if c % 2 == 0:
                        line, tl = vrow((l, f"gb{c // 2}"))
                    banks, need = two()
                    tok = gemm(("g2", l, c), xT, 8, [[(b[:, :], 0, 512)] for b in banks], need)
                    for t in (0, 1):
                        g = G[:, t, 512 * c:512 * c + 512]
                        t_g[c, t] = TT(g, banks[t][:, :], line.buf[:, 512 * (c % 2):512 * (c % 2) + 512], ALU.add,
                                       [tok, tl, *fence3])
                        mmb.put(banks[t], [t_g[c, t]])
                    if c % 2:
                        line.free = [t_g[c, 0], t_g[c, 1]]
                    if c == 3:
                        t_ob2 = to_T([OB[:, t, :] for t in (0, 1)], tk["ob"], 8, oT, col("ssm_norm_g_2", l, 8))
                bg_drain()
                xT.free = [tok]

                def gates():
                    for r in (1, 0, 2):
                        for t in (0, 1):
                            g = G[:, t, 1024 * r:1024 * r + 1024]
                            t_g[2 * r, t] = t_g[2 * r + 1, t] = A(g, g, ACT.Sigmoid, [t_g[2 * r + 1, t]])
                            yield

                f = gates()
                next(f)
                next(f)
                fibers.append(f)
                dm = [OB[:, t, :] for t in (0, 1)]
                to_T([OA[:, t, :] for t in (0, 1)], [tk["oa"], tk["gs"]], 8, xT, gsub.broadcast_to([128, 8]))
                third = lambda: to_T([OC[:, t, :] for t in (0, 1)], [tk["oc"]], 8, oT)
                branches("br2", l, [(1, 8), (0, 8), (2, 8)], [oT, xT, oT], G, t_g, dm, t_ob2, third)
                product_out("o2", l, then())
                reg3.close()
                rw_line.free = state["fence"]

        def dt_gemm(l, ps, need):
            pe.need(*need)
            key = ("dt", l)
            hi, lo, w, kts, ready = S.take(key)
            assert len(kts) == 8
            pe.need(*ready)
            for kt in kts:
                pe.need(*xT.tok[kt])
                o = kt * w
                for n, (ws, xs) in enumerate(((hi, xT.H), (hi, xT.L), (lo, xT.H))):
                    tok = mm(ps[0:16, 0:256], ws[:, o:o + w], xs[:, kt, :], kt == 0 and n == 0,
                             kt == 7 and n == 2, kt == 7 and n == 2)
            S.done(tok)
            return tok

        def store(t, halves):
            ln3(t, halves)

            def f():
                sp.need(*state["x"][t])
                sp.put(lambda e: e.dma_start(out[0, 128 * t:128 * t + 128, :], X[t]).then_inc(s_out, 16))
            return f

        ffn("f2", 1, enter_final())
        for l in (0, 1):
            ffn("F1", l, enter_ln((l, "ln1_g"), (l, "ln1_b")))
            mixer2(l, lambda: enter_ln((l, "ln2_g"), (l, "ln2_b")))
            ln3 = enter_ln((l, "ln3_g"), (l, "ln3_b"))
            ffn("F2", l, ln3 if l == 0 else store)
        state["second"]()
        sp.need((s_out, 32), (scr_line.sem, 16 * scr_line.n))
        assert S.u == len(pieces)

        block = ctx.enter_context(nc.Block())
        block.sync(sp.run)
        block.scalar(act.run)
        block.vector(dve.run)
        block.gpsimd(pool.run)
        block.tensor(pe.run)


def constants():
    f = np.float32
    q = np.arange(128)[:, None]
    k = np.arange(128)[None, :]

    def three(fn):
        return np.concatenate([fn(q, k), fn(q + 128, k), fn(q + 128, k + 128)], axis=1)

    bias = np.zeros((7, 128, 384), f)
    allowed = [lambda a, b: (a >= b) & (a - b <= 128), lambda a, b: (a >= b) & ((a - b) % 4 == 0),
               lambda a, b: (a >= b) & ((a - b) % 16 == 0), lambda a, b: a >= b]
    for i, ok in enumerate(allowed):
        bias[i] = three(lambda a, b: np.where(ok(a, b), (b - a).astype(f), f(NEG)).astype(f))
    bias[4] = three(lambda a, b: np.where(a >= b, f(0), f(NEG)))
    bias[5] = three(lambda a, b: np.where(a > b, f(0), f(NEG)))
    bias[6] = three(lambda a, b: np.where(b // 64 <= a // 64, f(0), f(NEG)))
    msk = np.zeros((128, 384), f)
    msk[:, 0:128] = (k >= q)
    msk[:, 128:256] = 1.0
    msk[:, 256:384] = (k >= q)
    pos = np.arange(256, dtype=f)
    inv1 = f(10000.0) ** (-np.arange(0, 32, 2, dtype=f) / f(32))
    a1 = (pos[:, None] * inv1[None, :]).astype(f)
    inv2 = f(500000.0) ** (-np.arange(8, dtype=f) * f(2.0) / f(16))
    a2 = (pos[:, None] * inv2[None, :]).astype(f)
    c1, s1, c2, s2 = np.cos(a1), np.sin(a1), np.cos(a2), np.sin(a2)
    rope = np.concatenate([c1, c1, s1, s1, c2, c2, s2, s2], axis=1).astype(f)
    rope = np.ascontiguousarray(rope.reshape(2, 128, 96).transpose(1, 0, 2))
    return np.eye(128, dtype=f), bias, msk, rope


def kernel(**inputs):
    import numpy as _np
    import concourse.bacc as _bacc
    from concourse import mybir as _mybir
    from concourse.bass_utils import run_bass_kernel_spmd as _run

    a = {k: _np.ascontiguousarray(v) for k, v in inputs.items()}
    blocks = place_pieces()
    pieces = plan()
    total = sum(128 * used for _, used in blocks)
    wpack = _np.empty(total, _np.float32)
    at = 0
    for ps, used in blocks:
        dst = wpack[at:at + 128 * used].reshape(128, used)
        at += 128 * used
        for i, off, n in ps:
            _, width, kts = pieces[i]
            for idx, kt, ranges in kts:
                for name, c0, c1 in ranges:
                    dst[:, off:off + c1 - c0] = a[name][idx][128 * kt:128 * kt + 128, c0:c1]
                    off += c1 - c0
    cols = _np.zeros((128, NCOLS), _np.float32)
    for name, l, c, n in _COLS:
        v = a[name][l]
        if name == "ssm_conv_w_2":
            cols[:, c:c + n] = v.reshape(4, 12, 128).transpose(2, 1, 0).reshape(128, 48)
        elif v.size == 16:
            cols[:16, c] = v
        else:
            cols[:, c:c + n] = v.reshape(n, 128).T
    rows = _np.concatenate([a["diff_lambda_2"].reshape(2, 256), a["ssm_D_2"]], axis=1)
    vr = [a["final_norm"]]
    for l in (0, 1):
        vr += [a["ln1_g_2"][l], a["ln1_b_2"][l], a["gate_bias_2"][l, 0], a["gate_bias_2"][l, 1],
               a["gate_bias_2"][l, 2], a["ln2_g_2"][l], a["ln2_b_2"][l], a["ln3_g_2"][l], a["ln3_b_2"][l]]
    ident, bias, msk, rope = constants()
    arrays = {"in_x": a["x"], "in_w": wpack, "in_cols": cols, "in_rows": _np.ascontiguousarray(rows),
              "in_vrows": _np.stack(vr), "in_ident": ident, "in_bias": bias, "in_msk": msk, "in_rope": rope}
    nc = _bacc.Bacc("TRN2", target_bir_lowering=False, num_devices=1)
    args = [nc.dram_tensor(k, v.shape, _mybir.dt.from_np(v.dtype), kind="ExternalInput").ap()
            for k, v in arrays.items()]
    scratch = nc.dram_tensor("scratch", (2, 16, 256), _mybir.dt.float32, kind="Internal").ap()
    out = nc.dram_tensor("out_0", (1, 256, 1024), _mybir.dt.float32, kind="ExternalOutput").ap()
    bass_two_blocks(nc, *args, scratch, out)
    r = _run(nc, [arrays], core_ids=[0])
    return r.results[0]["out_0"]
```
